# Optimizing a Trainium2 kernel written in Bass

```python
import jax, jax.numpy as jnp
from jax import lax
import numpy as np

D_MODEL = 1024
BATCH = 1
SEQ = 1024
DEPTH = 1

D_MIX = D_MODEL
RWKV_HEAD = 64
RWKV_HEADS = 8
RWKV_WIDTH = RWKV_HEADS * RWKV_HEAD
DECAY_LORA = 64
ICLR_LORA = 64
GATE_LORA = 128
MLA_HEADS = 8
MLA_NOPE = 64
MLA_ROPE = 32
MLA_V = 64
MLA_WIDTH = MLA_HEADS * MLA_V
Q_LORA = 384
KV_LORA = 256
ROPE_BASE = 10000.0
ATTN_BLOCK = 128
D_FF = 4 * D_MODEL
ALPHA = (2 * DEPTH) ** 0.25
BETA = (8 * DEPTH) ** -0.25
LN_EPS = 1e-5
RMS_EPS = 1e-6
GN_EPS = 64e-5
RWKV_SPLITS = [RWKV_WIDTH, RWKV_WIDTH, RWKV_WIDTH, DECAY_LORA, ICLR_LORA, GATE_LORA]
MLA_SPLITS = [Q_LORA, KV_LORA, MLA_ROPE]
RWKV_COLS = sum(RWKV_SPLITS)
MLA_COLS = sum(MLA_SPLITS)
IN_COLS = RWKV_COLS + MLA_COLS

kernel_name = "hymba_rwkv7_mla_deepnorm_layer"

def _split(z, sizes):
    return jnp.split(z, list(np.cumsum(sizes)[:-1]), axis=-1)

def layer_norm(x, g, b):
    xf = x.astype(jnp.float32)
    mu = jnp.mean(xf, axis=-1, keepdims=True)
    var = jnp.mean(jnp.square(xf - mu), axis=-1, keepdims=True)
    return ((xf - mu) * lax.rsqrt(var + LN_EPS)).astype(x.dtype) * g + b

def rms_norm(x, g):
    xf = x.astype(jnp.float32)
    return (xf * lax.rsqrt(jnp.mean(xf * xf, axis=-1, keepdims=True) + RMS_EPS)).astype(x.dtype) * g

def rope(z, ang):
    cos, sin = jnp.cos(ang), jnp.sin(ang)
    zf = z.astype(jnp.float32)
    z1, z2 = jnp.split(zf, 2, axis=-1)
    return jnp.concatenate([z1 * cos - z2 * sin, z2 * cos + z1 * sin], axis=-1).astype(z.dtype)

def token_shift(z):
    return jnp.pad(z, ((0, 0), (1, 0), (0, 0)))[:, :-1]

def wkv7_scan(r, w, k, v, kk, a):
    B, _, H, N = r.shape
    tm = lambda t: jnp.moveaxis(t.astype(jnp.float32), 1, 0)

    def step(S, inp):
        r_t, w_t, k_t, v_t, kk_t, a_t = inp
        sa = jnp.einsum('bhvk,bhk->bhv', S, -kk_t)
        S = (S * w_t[:, :, None, :]
             + sa[..., :, None] * (kk_t * a_t)[:, :, None, :]
             + v_t[..., :, None] * k_t[:, :, None, :])
        y = jnp.einsum('bhvk,bhk->bhv', S, r_t)
        return S, y

    S0 = jnp.zeros((B, H, N, N), jnp.float32)
    _, y = lax.scan(step, S0, (tm(r), tm(w), tm(k), tm(v), tm(kk), tm(a)))
    return jnp.moveaxis(y, 0, 1).astype(r.dtype)

def rwkv7_group(hr, shift_mu, decay_w0, decay_w2, iclr_a0, iclr_a2, gate_g2, k_k, k_a, r_k, lnx_g, lnx_b):
    B, S, _ = hr.shape
    H, N = RWKV_HEADS, RWKV_HEAD
    hr = hr + (token_shift(hr) - hr) * shift_mu
    r, k, v, xw, xa, xg = _split(hr, RWKV_SPLITS)
    w_log = -jax.nn.softplus(-(decay_w0 + jnp.tanh(xw) @ decay_w2)) - 0.5
    decay = jnp.exp(-jnp.exp(w_log.astype(jnp.float32)))
    a = jax.nn.sigmoid(iclr_a0 + xa @ iclr_a2)
    g = jax.nn.sigmoid(xg) @ gate_g2
    heads = lambda t: t.reshape(B, S, H, N)
    kk = heads(k * k_k).astype(jnp.float32)
    kk = kk / jnp.maximum(jnp.sqrt(jnp.sum(kk * kk, axis=-1, keepdims=True)), 1e-12)
    k = k * (1.0 + (a - 1.0) * k_a)
    rh, kh, vh, ah = heads(r), heads(k), heads(v), heads(a)
    y = wkv7_scan(rh, heads(decay), kh, vh, kk, ah)
    yf = y.astype(jnp.float32)
    mu = jnp.mean(yf, axis=-1, keepdims=True)
    var = jnp.mean(jnp.square(yf - mu), axis=-1, keepdims=True)
    yn = ((yf - mu) * lax.rsqrt(var + GN_EPS)).astype(y.dtype).reshape(B, S, RWKV_WIDTH) * lnx_g + lnx_b
    bonus = (jnp.sum(rh * kh * r_k, axis=-1, keepdims=True) * vh).reshape(B, S, RWKV_WIDTH)
    return (yn + bonus) * g

def causal_block_attention(q, k, v):
    B, S, H, Dq = q.shape
    Dv = v.shape[-1]
    nb = S // ATTN_BLOCK
    scale = Dq ** -0.5
    qb = jnp.moveaxis(q.reshape(B, nb, ATTN_BLOCK, H, Dq), 1, 0)
    kpos = jnp.arange(S)

    def one_block(args):
        q_blk, i = args
        s = jnp.einsum('bqhd,bkhd->bhqk', q_blk, k).astype(jnp.float32) * scale
        qpos = i * ATTN_BLOCK + jnp.arange(ATTN_BLOCK)
        s = jnp.where(kpos[None, :] <= qpos[:, None], s, -jnp.inf)
        p = jax.nn.softmax(s, axis=-1).astype(v.dtype)
        return jnp.einsum('bhqk,bkhd->bqhd', p, v)

    o = lax.map(one_block, (qb, jnp.arange(nb)))
    return jnp.moveaxis(o, 0, 1).reshape(B, S, H * Dv)

def mla_group(hm, positions, q_norm_g, w_uq, kv_norm_g, w_ukv):
    B, S, _ = hm.shape
    H = MLA_HEADS
    c_q, c_kv, k_pe = _split(hm, MLA_SPLITS)
    inv_freq = ROPE_BASE ** (-jnp.arange(0, MLA_ROPE, 2, dtype=jnp.float32) / MLA_ROPE)
    ang = positions.astype(jnp.float32)[..., None] * inv_freq
    q = (rms_norm(c_q, q_norm_g) @ w_uq).reshape(B, S, H, MLA_NOPE + MLA_ROPE)
    q_nope, q_pe = _split(q, [MLA_NOPE, MLA_ROPE])
    q_pe = rope(q_pe, ang[:, :, None, :])
    kv = (rms_norm(c_kv, kv_norm_g) @ w_ukv).reshape(B, S, H, MLA_NOPE + MLA_V)
    k_nope, v = _split(kv, [MLA_NOPE, MLA_V])
    k_pe = rope(k_pe, ang)
    q = jnp.concatenate([q_nope, q_pe], axis=-1)
    k = jnp.concatenate([k_nope, jnp.broadcast_to(k_pe[:, :, None, :], (B, S, H, MLA_ROPE))], axis=-1)
    return causal_block_attention(q, k, v)

def setup_inputs(seed: int = 0) -> dict:
    key = jax.random.key(seed)
    ks = jax.random.split(key, 26)
    f32 = jnp.float32
    nrm = lambda k, shape, s: jax.random.normal(k, shape, f32) * s
    L = DEPTH
    x = jax.random.normal(ks[0], (BATCH, SEQ, D_MODEL), f32)
    offset = jax.random.randint(ks[1], (BATCH, 1), 0, 4096, dtype=jnp.int32)
    positions = (offset + jnp.arange(SEQ, dtype=jnp.int32)[None, :]).astype(jnp.int32)
    return {
        "x": x,
        "positions": positions,
        "w_in": nrm(ks[2], (L, D_MODEL, IN_COLS), D_MODEL ** -0.5),
        "shift_mu": jax.random.uniform(ks[3], (L, RWKV_COLS), f32),
        "decay_w0": jax.random.uniform(ks[4], (L, RWKV_WIDTH), f32, -5.0, 1.0),
        "decay_w2": nrm(ks[5], (L, DECAY_LORA, RWKV_WIDTH), 0.1),
        "iclr_a0": nrm(ks[6], (L, RWKV_WIDTH), 0.5),
        "iclr_a2": nrm(ks[7], (L, ICLR_LORA, RWKV_WIDTH), 0.1),
        "gate_g2": nrm(ks[8], (L, GATE_LORA, RWKV_WIDTH), GATE_LORA ** -0.5),
        "k_k": 0.85 + nrm(ks[9], (L, RWKV_WIDTH), 0.05),
        "k_a": 1.0 + nrm(ks[10], (L, RWKV_WIDTH), 0.05),
        "r_k": nrm(ks[11], (L, RWKV_HEADS, RWKV_HEAD), 0.1),
        "lnx_g": 1.0 + nrm(ks[12], (L, RWKV_WIDTH), 0.1),
        "lnx_b": nrm(ks[13], (L, RWKV_WIDTH), 0.01),
        "q_norm_g": 1.0 + nrm(ks[14], (L, Q_LORA), 0.1),
        "w_uq": nrm(ks[15], (L, Q_LORA, MLA_HEADS * (MLA_NOPE + MLA_ROPE)), Q_LORA ** -0.5),
        "kv_norm_g": 1.0 + nrm(ks[16], (L, KV_LORA), 0.1),
        "w_ukv": nrm(ks[17], (L, KV_LORA, MLA_HEADS * (MLA_NOPE + MLA_V)), KV_LORA ** -0.5),
        "w_out": nrm(ks[18], (L, D_MIX, D_MODEL), BETA * D_MIX ** -0.5),
        "ln1_g": 1.0 + nrm(ks[19], (L, D_MODEL), 0.1),
        "ln1_b": nrm(ks[20], (L, D_MODEL), 0.01),
        "w_ffn1": nrm(ks[21], (L, D_MODEL, D_FF), D_MODEL ** -0.5),
        "w_ffn2": nrm(ks[22], (L, D_FF, D_MODEL), BETA * D_FF ** -0.5),
        "ln2_g": 1.0 + nrm(ks[23], (L, D_MODEL), 0.1),
        "ln2_b": nrm(ks[24], (L, D_MODEL), 0.01),
    }

def reference(x, positions, w_in, shift_mu, decay_w0, decay_w2, iclr_a0, iclr_a2, gate_g2, k_k, k_a, r_k,
              lnx_g, lnx_b, q_norm_g, w_uq, kv_norm_g, w_ukv, w_out, ln1_g, ln1_b, w_ffn1, w_ffn2,
              ln2_g, ln2_b):
    for l in range(DEPTH):
        h = x @ w_in[l]
        y_rwkv = rwkv7_group(h[..., :RWKV_COLS], shift_mu[l], decay_w0[l], decay_w2[l], iclr_a0[l],
                             iclr_a2[l], gate_g2[l], k_k[l], k_a[l], r_k[l], lnx_g[l], lnx_b[l])
        y_mla = mla_group(h[..., RWKV_COLS:], positions, q_norm_g[l], w_uq[l], kv_norm_g[l], w_ukv[l])
        mix = jnp.concatenate([y_rwkv, y_mla], axis=-1) @ w_out[l]
        x = layer_norm(ALPHA * x + mix, ln1_g[l], ln1_b[l])
        f = jnp.square(jax.nn.relu(x @ w_ffn1[l])) @ w_ffn2[l]
        x = layer_norm(ALPHA * x + f, ln2_g[l], ln2_b[l])
    return x


_drawn_inputs = setup_inputs


def setup_inputs(seed=0):
    import zlib

    import numpy as np

    out = dict(_drawn_inputs(seed))
    spreads = {}
    factors = {'decay_w2': 5.632,
     'k_k': 61.592,
     'k_a': 17.667,
     'lnx_g': 8.275,
     'lnx_b': 64.0,
     'q_norm_g': 8.0,
     'kv_norm_g': 7.917,
     'ln1_b': 5.671,
     'ln2_b': 5.711}
    for name, (base, spread) in spreads.items():
        noise = np.random.default_rng([zlib.crc32(name.encode()), seed]).standard_normal(out[name].shape)
        drawn = base * np.exp(spread * noise) if base else spread * noise
        out[name] = __import__('jax').numpy.asarray(drawn.astype(out[name].dtype))
    for name, factor in factors.items():
        out[name] = (out[name] * factor).astype(out[name].dtype)
    return out
```

```python
from contextlib import ExitStack

import numpy as np

import concourse.bass as bass
from concourse import mybir

ALU = mybir.AluOpType
ACT = mybir.ActivationFunctionType
F32 = mybir.dt.float32
F32R = mybir.dt.float32r
I32 = mybir.dt.int32
AX_X = mybir.AxisListType.X

P = 128
D = 1024
S = 1024
KT = D // P
TT = S // P
HALF = 512
NH = 8
HD = 64
ROPE = 32
RW = NH * HD
RT = RW // P
QL, KVL = 384, 256
QLT, KVLT = QL // P, KVL // P
SLABS = 20
T_R, T_K, T_V, T_WA, T_G, T_CQ, T_CKV, T_PE = 0, 4, 8, 12, 13, 14, 17, 19
DFF = 4096
ALPHA = 2.0 ** 0.25
LN_EPS, RMS_EPS, GN_EPS = 1e-5, 1e-6, 64e-5
CH = 64
NC_ = S // CH
EXP_M05 = float(np.exp(-0.5))
SCALE = float((HD + ROPE) ** -0.5)
NEG = -1.0e30

C_MU = 0
C_W0 = C_MU + SLABS
C_A0 = C_W0 + RT
C_KK = C_A0 + RT
C_KA = C_KK + RT
C_RK = C_KA + RT
C_LG = C_RK + RT
C_LB = C_LG + RT
C_QG = C_LB + RT
C_KVG = C_QG + QLT
C_FREQ = C_KVG + KVLT
C_SIGN = C_FREQ + 1
C_ROT = C_SIGN + 1
NCOLS = C_ROT

KB = 1024
BASE = 16512


OUT_SHAPE = (1, S, D)


class Steps:

    def __init__(self, eng, sem):
        self.eng, self.sem, self.base, self.n = eng, sem, 0, 0

    def mark(self, ins):
        ins.then_inc(self.sem, 1)
        self.n += 1
        return self.n

    def wait(self, n=None):
        self.eng.wait_ge(self.sem, self.base + (self.n if n is None else n))

    def enter(self, trip, per):
        self.start, self.per = self.base + self.n, per
        self.base, self.n = self.start + trip * per, 0

    def leave(self, trips):
        assert self.n == self.per, f"the body marks {self.n} steps"
        self.base, self.n = self.start + trips * self.per, 0


class Memory:

    def __init__(self, nc):
        self.nc = nc

    def at(self, name, kb, shape, dtype=F32):
        return self.nc.alloc_sbuf_tensor_at(name, shape, dtype, offset=BASE + int(kb * KB))


def sems(nc, ctx, *names):
    return [ctx.enter_context(nc.semaphore(n)) for n in names]


def project3(nc, outs, w_hi, w_lo, r_hi, r_lo, tiles):
    for kt in range(tiles):
        for n, (w, r) in enumerate(((w_hi, r_hi), (w_hi, r_lo), (w_lo, r_hi))):
            for b, out in enumerate(outs):
                last = nc.tensor.matmul(out, w[:, kt, :], r(kt, b), start=kt == 0 and n == 0,
                                        stop=kt == tiles - 1 and n == 2)
    return last


def split2(nc, dve, raw, hi, lo, hi_sem, count, lo_sem):
    nc.vector.tensor_copy(hi, raw).then_inc(hi_sem, 1)
    dve.wait_ge(hi_sem, count)
    nc.vector.tensor_tensor(lo, raw, hi.bitcast(F32), ALU.subtract).then_inc(lo_sem, 1)


def project_in(nc, mem, k, x, w_in):
    x_tok = mem.at("x_tok", 38 + 48, [P, TT, D])
    x_hi = mem.at("xT_hi", 118, [P, KT, S], F32R)
    x_lo = mem.at("xT_lo", 150, [P, KT, S], F32R)
    w_raw = [mem.at(f"win_raw{j}", 182 + 4 * j, [P, KT, P]) for j in range(2)]
    w_hi = [mem.at(f"win_hi{j}", 190 + 4 * j, [P, KT, P], F32R) for j in range(2)]
    w_lo = [mem.at(f"win_lo{j}", 198 + 4 * j, [P, KT, P], F32R) for j in range(2)]
    hT, cols, ident, ps = k.hT, k.cols, k.ident, k.ps
    keep = k.keep
    trips = SLABS // 2
    with ExitStack() as ctx:
        consts_in, x_in0, x_in1, xT_ready, xhi_done, xlo_done, keep_done = sems(
            nc, ctx, "a_consts_in", "a_x_in0", "a_x_in1", "a_xT_ready", "a_xhi_done", "a_xlo_done", "a_keep_done")
        w_in_sem = sems(nc, ctx, "a_w_loaded0", "a_w_loaded1")
        w_split = sems(nc, ctx, "a_w_split0", "a_w_split1")
        w_whi = sems(nc, ctx, "a_w_hi0", "a_w_hi1")
        slab_mm = sems(nc, ctx, "a_slab_mm0", "a_slab_mm1")
        h_scaled = sems(nc, ctx, "a_h_scaled0", "a_h_scaled1")
        h_mixed = sems(nc, ctx, "a_h_mixed0", "a_h_mixed1")
        block = ctx.enter_context(nc.Block())

        @block.sync
        def _(sp):
            sp.dma_start(ident[:], k.d_ident).then_inc(consts_in, 16)
            sp.dma_start(cols[:], k.d_cols).then_inc(consts_in, 16)
            xt = x.rearrange("o (t p) d -> p (o t) d", p=P)
            for g, sem in enumerate((x_in0, x_in1)):
                sp.dma_start(x_tok[:, 4 * g:4 * g + 4, :], xt[:, 4 * g:4 * g + 4, :]).then_inc(sem, 16)
            for j in range(2):
                sp.dma_start(w_raw[j][:], w_in[j]).then_inc(w_in_sem[j], 16)
            with sp.Fori(1, trips) as i:
                for j in range(2):
                    sp.wait_ge(w_split[j], i)
                    sp.dma_start(w_raw[j][:], w_in[2 * i + j]).then_inc(w_in_sem[j], 16)

        @block.tensor
        def _(pe):
            pe.wait_ge(consts_in, 32)
            for g in range(2):
                pe.wait_ge((x_in0, x_in1)[g], 16)
                for kt in range(KT):
                    n = g * KT + kt
                    if n >= 4:
                        pe.wait_ge(xlo_done, n - 3)
                    for t in range(4):
                        last = nc.tensor.transpose(ps[:, n % 4, t * P:(t + 1) * P],
                                                   x_tok[:, 4 * g + t, kt * P:(kt + 1) * P], ident[:])
                    last.then_inc(xT_ready, 1)
            pe.wait_ge(xlo_done, 2 * KT)
            pe.wait_ge(xhi_done, 2 * KT)
            with pe.Fori(0, trips) as i:
                for j in range(2):
                    pe.wait_ge(w_split[j], i + 1)
                    last = project3(nc, [ps[:, 2 * j + b, :] for b in range(2)], w_hi[j], w_lo[j],
                                    lambda kt, b: x_hi[:, kt, b * HALF:(b + 1) * HALF],
                                    lambda kt, b: x_lo[:, kt, b * HALF:(b + 1) * HALF], KT)
                    last.then_inc(slab_mm[j], 1)

        @block.scalar
        def _(act):
            for n in range(2 * KT):
                g, kt = divmod(n, KT)
                act.wait_ge(xT_ready, n + 1)
                nc.scalar.activation(x_hi[:, kt, g * HALF:(g + 1) * HALF], ps[:, n % 4, :], ACT.Copy)\
                    .then_inc(xhi_done, 1)
            act.wait_ge(keep_done, 1)
            with act.Fori(0, trips) as i:
                for j in range(2):
                    act.wait_ge(slab_mm[j], i + 1)
                    nc.scalar.activation(hT[:, 2 * i + j, :], ps[:, 2 * j:2 * j + 2, :].rearrange("p b n -> p (b n)"),
                                         ACT.Identity, scale=keep[:, bass.ds(2 * i + j, 1)]).then_inc(h_scaled[j], 1)

        @block.vector
        def _(dve):
            dve.wait_ge(consts_in, 32)
            nc.vector.tensor_scalar(keep[:], cols[:, C_MU:C_MU + SLABS], -1.0, 1.0, ALU.mult, ALU.add)\
                .then_inc(keep_done, 1)
            for n in range(2 * KT):
                g, kt = divmod(n, KT)
                cut = slice(g * HALF, (g + 1) * HALF)
                dve.wait_ge(xhi_done, n + 1)
                nc.vector.tensor_tensor(x_lo[:, kt, cut], ps[:, n % 4, :], x_hi[:, kt, cut].bitcast(F32), ALU.subtract)\
                    .then_inc(xlo_done, 1)

            def split(j, trip):
                dve.wait_ge(w_in_sem[j], 16 * (trip + 1))
                split2(nc, dve, w_raw[j][:], w_hi[j][:], w_lo[j][:], w_whi[j], trip + 1, w_split[j])

            def mix(j, i):
                dve.wait_ge(h_scaled[j], i + 1)
                flat = ps[:, 2 * j:2 * j + 2, :].rearrange("p b n -> p (b n)")
                nc.vector.scalar_tensor_tensor(hT[:, 2 * i + j, 1:S], flat[:, 0:S - 1],
                                               cols[:, bass.ds(C_MU + 2 * i + j, 1)], hT[:, 2 * i + j, 1:S],
                                               ALU.mult, ALU.add).then_inc(h_mixed[j], 1)

            for j in range(2):
                split(j, 0)
            with dve.Fori(0, trips - 1) as i:
                for j in range(2):
                    mix(j, i)
                    split(j, i + 1)
            for j in range(2):
                mix(j, trips - 1)


def mla(nc, mem, k, t):
    hT, cols, ident, ps = k.hT, k.cols, k.ident, k.ps
    ym_hi, ym_lo = k.ym_hi, k.ym_lo
    cos = mem.at("cos", 118, [P, S])
    sin = mem.at("sin", 122, [P, S])
    q_hi = [mem.at(f"q_hi{p}", 126 + 4 * p, [P, S], F32R) for p in range(2)]
    q_lo = [mem.at(f"q_lo{p}", 134 + 4 * p, [P, S], F32R) for p in range(2)]
    k_hi = [mem.at(f"k_hi{p}", 142 + 4 * p, [P, S], F32R) for p in range(2)]
    k_lo = [mem.at(f"k_lo{p}", 150 + 4 * p, [P, S], F32R) for p in range(2)]
    v_one = [mem.at(f"v_one{p}", 158 + 4 * p, [P, TT, P]) for p in range(2)]
    probs = [mem.at(f"probs{n}", 166 + 4 * n, [P, S]) for n in range(3)]
    w_uq = [mem.at(f"w_uq{p}", 178 + 1.5 * p, [P, QLT, P]) for p in range(2)]
    w_ukv = [mem.at(f"w_ukv{p}", 181 + p, [P, KVLT, P]) for p in range(2)]
    rot_a = mem.at("rot_a", 183, [P, S])
    rot_b = mem.at("rot_b", 187, [P, S])
    tmp = mem.at("mla_tmp", 191, [P, 3, S])
    pos = mem.at("mla_pos", 203, [P, S], I32)
    recip = mem.at("att_recip", 191, [P, S])
    y_full = mem.at("att_y", 195, [P, S])
    ones = mem.at("ones_full", 1, [P, P])
    causal = mem.at("causal", 1.5, [P, P])
    causal_r = mem.at("causal_r", 2, [P, P], F32R)
    ident_r = mem.at("ident_r", 2.5, [P, P], F32R)
    top = mem.at("row_max", 3, [P, TT])
    top_r = mem.at("neg_row_max_r", 3.125, [P, TT], F32R)
    rms_eps = mem.at("rms_eps", 3.25, [P, 1])
    PI2 = 2 * np.pi
    C1 = 6.28125
    C2 = float(np.float32(round((PI2 - C1) * 2 ** 20) / 2 ** 20))
    C3 = float(np.float32(PI2 - C1 - C2))
    MAGIC = 1.5 * 2.0 ** 23
    PI_BELOW = 3.1415925
    A, O = (0, 1), (6, 7)
    T = ((2, 3), (4, 5))
    flat = lambda pair, rows=slice(0, P): ps[rows, pair[0]:pair[0] + 2, :].rearrange("p b n -> p (b n)")
    lo64, hi64, pe32, sw32 = slice(0, 64), slice(64, 128), slice(64, 96), slice(96, 128)
    ONE = slice(96, 97)
    ITEMS = 12
    FREES = ITEMS - 1
    S_AT = {3: (7, 6), 4: (5, 4), 5: (3,), 6: (2, 1), 7: (0,)}
    S_ORDER = [i for j in sorted(S_AT) for i in S_AT[j]]

    with ExitStack() as ctx:
        in_sem, squares, sums, roots, ready, setup, causal_rr, sin_in, sin_out, pooled = sems(
            nc, ctx, "b_in", "b_squares", "b_sums", "b_roots", "b_latents_ready", "b_setup", "b_causal_r",
            "b_sin_in", "b_sin_out", "b_pooled")
        w_in = sems(nc, ctx, "b_w_in0", "b_w_in1")
        item, a_free, q_hi_done, k_hi_done, rot_ready, q_ready, m_ready, row_ready = sems(
            nc, ctx, "b_item", "b_a_free", "b_q_hi_done", "b_k_hi_done", "b_rot_ready", "b_q_ready",
            "b_m_ready", "b_row_ready")
        st_ready, exp_done, pv_done, o_read, y_done, dve_step, pool_step = sems(
            nc, ctx, "b_st_ready", "b_exp_done", "b_pv_done", "b_o_read", "b_y_done", "b_dve_step", "b_pool_step")
        T_FREE, PROBS_FREE, O_FREE, Y_FREE = 2, 3, 1, 2
        block = ctx.enter_context(nc.Block())

        @block.sync
        def _(sp):
            sp.dma_start(causal[:], t["causal"]).then_inc(in_sem, 16)
            sp.dma_start(pos[:], t["positions"].to_broadcast([P, S])).then_inc(in_sem, 16)

            def load(h, p):
                sp.dma_start(w_uq[p][:], t["w_uq"][h]).then_inc(w_in[p], 16)
                sp.dma_start(w_ukv[p][:], t["w_ukv"][h]).then_inc(w_in[p], 16)

            load(0, 0)
            load(1, 1)
            with sp.Fori(1, NH // 2) as i:
                for p in range(2):
                    sp.wait_ge(item, ITEMS * (2 * i + p - 2) + 3)
                    load(2 * i + p, p)

        @block.tensor
        def _(pe):
            pe.wait_ge(setup, 1)
            pe.wait_ge(squares, 1)
            for b in range(2):
                for c in range(QLT):
                    last = nc.tensor.matmul(ps[:, b, :], ones[:], tmp[:, c, b * HALF:(b + 1) * HALF],
                                            start=c == 0, stop=c == QLT - 1)
            last.then_inc(sums, 1)
            pe.wait_ge(squares, 2)
            for b in range(2):
                for c in range(KVLT):
                    last = nc.tensor.matmul(ps[:, 2 + b, :], ones[:], tmp[:, c, b * HALF:(b + 1) * HALF],
                                            start=c == 0, stop=c == KVLT - 1)
            last.then_inc(sums, 1)
            pe.sem_inc(pv_done, PROBS_FREE)
            pe.wait_ge(ready, 2)
            pe.wait_ge(causal_rr, 2)

            def take(h, n):
                pe.wait_ge(a_free, FREES * h + n)

            def q_item(h, p, i, first):
                pe.wait_ge(w_in[p], 32 * (i + 1))
                if not first:
                    take(h, 0)
                for b in range(2):
                    for c in range(QLT):
                        last = nc.tensor.matmul(ps[:, b, :], w_uq[p][:, c, :],
                                                hT[:, T_CQ + c, b * HALF:(b + 1) * HALF],
                                                start=c == 0, stop=c == QLT - 1)
                last.then_inc(item, 1)

            def k_item(h, p):
                take(h, 1)
                for b in range(2):
                    for c in range(KVLT):
                        last = nc.tensor.matmul(ps[lo64, b, :], w_ukv[p][:, c, 0:HD],
                                                hT[:, T_CKV + c, b * HALF:(b + 1) * HALF],
                                                start=c == 0, stop=c == KVLT - 1)
                last.then_inc(item, 1)

            def v_item(h, p):
                take(h, 2)
                for tt in range(TT):
                    for c in range(KVLT):
                        last = nc.tensor.matmul(ps[:, 0, tt * HD:(tt + 1) * HD],
                                                hT[:, T_CKV + c, tt * P:(tt + 1) * P], w_ukv[p][:, c, HD:2 * HD],
                                                start=c == 0, stop=c == KVLT - 1)
                last.then_inc(item, 1)

            def s_item(h, p, qt):
                n = S_ORDER.index(qt)
                take(h, 3 + n)
                if n == 0:
                    pe.wait_ge(q_ready, h + 1)
                q = q_hi[p][0:96, qt * P:(qt + 1) * P]
                for c in range(0, (qt + 1) * P, HALF):
                    end = min(c + HALF, (qt + 1) * P)
                    nc.tensor.matmul(ps[:, c // HALF, 0:end - c], q, k_hi[p][0:96, c:end], start=True,
                                     stop=end < (qt + 1) * P)
                at = qt * P % HALF
                nc.tensor.matmul(ps[:, qt * P // HALF, at:at + P], causal_r[:], ident_r[:],
                                 start=False, stop=True).then_inc(item, 1)

            def m_item(h):
                take(h, 11)
                pe.wait_ge(m_ready, h + 1)
                for qt in range(TT):
                    last = nc.tensor.matmul(ps[0:1, qt // 4, qt % 4 * P:(qt % 4 + 1) * P], top_r[:, qt:qt + 1],
                                            ident_r[:], start=True, stop=True)
                last.then_inc(item, 1)

            def st(h, p, kt):
                g = kt % 2
                pe.wait_ge(exp_done, TT * h + kt - 1 + T_FREE)
                if kt == 0:
                    pe.wait_ge(row_ready, h + 1)
                for b in range(2):
                    lo = max(kt * P, b * HALF)
                    if lo >= (b + 1) * HALF:
                        continue
                    out = ps[:, T[g][b], lo - b * HALF:HALF]
                    q = slice(lo, (b + 1) * HALF)
                    keys = slice(kt * P, (kt + 1) * P)
                    diag = lo == kt * P
                    for n, (kk, qq) in enumerate(((k_hi, q_hi), (k_hi, q_lo), (k_lo, q_hi))):
                        last = nc.tensor.matmul(out, kk[p][0:97, keys], qq[p][0:97, q], start=n == 0,
                                                stop=n == 2 and not diag)
                    if diag:
                        last = nc.tensor.matmul(out[:, 0:P], ident_r[:], causal_r[:], start=False, stop=True)
                last.then_inc(st_ready, 1)

            def pv(h, p, kt):
                pe.wait_ge(exp_done, TT * h + kt + 1 + T_FREE)
                if kt == 0:
                    pe.wait_ge(o_read, h + O_FREE)
                for b in range(2):
                    lo = max(kt * P, b * HALF)
                    if lo >= (b + 1) * HALF:
                        continue
                    last = nc.tensor.matmul(ps[:, O[b], lo - b * HALF:HALF], v_one[p][:, kt, :],
                                            probs[kt % 3][:, lo:(b + 1) * HALF], start=kt == 0,
                                            stop=kt == (3, 7)[b])
                last.then_inc(pv_done, 1)

            def sweep(h, p, i, more):
                nh, np_, ni = h + 1, 1 - p, i + p
                for kt in range(TT):
                    st(h, p, kt)
                    if more:
                        if kt == 0:
                            q_item(nh, np_, ni, False)
                        if kt == 1:
                            k_item(nh, np_)
                            v_item(nh, np_)
                        for qt in S_AT.get(kt, ()):
                            s_item(nh, np_, qt)
                    if kt >= 1:
                        pv(h, p, kt - 1)
                pv(h, p, TT - 1)
                if more:
                    m_item(nh)

            q_item(0, 0, 0, True)
            k_item(0, 0)
            v_item(0, 0)
            for qt in S_ORDER:
                s_item(0, 0, qt)
            m_item(0)
            with pe.Fori(0, NH // 2 - 1) as i:
                for p in range(2):
                    sweep(2 * i + p, p, i, True)
            sweep(NH - 2, 0, NH // 2 - 1, True)
            sweep(NH - 1, 1, NH // 2 - 1, False)

        @block.scalar
        def _(act):
            nc.scalar.activation(tmp[:, 0:QLT, :], hT[:, T_CQ:T_CQ + QLT, :], ACT.Square).then_inc(squares, 1)
            act.wait_ge(setup, 2)
            act.wait_ge(sums, 1)
            nc.scalar.activation(tmp[:, 0:KVLT, :], hT[:, T_CKV:T_CKV + KVLT, :], ACT.Square).then_inc(squares, 1)
            nc.scalar.activation(rot_a[:], flat((0, 1)), ACT.Sqrt, scale=1.0 / QL, bias=rms_eps[:]).then_inc(roots, 1)
            act.wait_ge(sums, 2)
            nc.scalar.activation(rot_b[:], flat((2, 3)), ACT.Sqrt, scale=1.0 / KVL, bias=rms_eps[:]).then_inc(roots, 1)
            act.wait_ge(sin_in, 1)
            nc.scalar.activation(sin[:], sin[:], ACT.Sin).then_inc(sin_out, 1)
            nc.scalar.activation(cos[:], cos[:], ACT.Sin).then_inc(sin_out, 1)

            def front(h, p, n):
                if n == 0:
                    act.wait_ge(item, ITEMS * h + 1)
                    nc.scalar.activation(q_hi[p][lo64, :], flat(A, lo64), ACT.Copy).then_inc(q_hi_done, 1)
                if n == 1:
                    act.wait_ge(item, ITEMS * h + 2)
                    nc.scalar.activation(k_hi[p][lo64, :], flat(A, lo64), ACT.Copy).then_inc(k_hi_done, 1)
                if n == 2:
                    act.wait_ge(item, ITEMS * h + 3)
                    nc.scalar.activation(v_one[p][:, :, 0:HD], ps[:, 0, :].rearrange("p (t d) -> p t d", d=HD),
                                         ACT.Copy).then_inc(a_free, 1)
                if n == 3:
                    act.wait_ge(item, ITEMS * h + 12)
                    nc.scalar.activation(q_hi[p][ONE, :], flat(A, slice(0, 1)), ACT.Copy).then_inc(row_ready, 1)

            def sweep(h, p, more):
                for kt in range(TT):
                    act.wait_ge(st_ready, TT * h + kt + 1)
                    act.wait_ge(pv_done, TT * h + kt - 2 + PROBS_FREE)
                    nc.scalar.activation(probs[kt % 3][:, kt * P:S], flat(T[kt % 2])[:, kt * P:S], ACT.Exp,
                                         scale=SCALE).then_inc(exp_done, 1)
                    if more and kt == 0:
                        front(h + 1, 1 - p, 0)
                    if more and kt == 1:
                        front(h + 1, 1 - p, 1)
                        front(h + 1, 1 - p, 2)
                if more:
                    front(h + 1, 1 - p, 3)

            act.sem_inc(exp_done, T_FREE)
            for n in range(4):
                front(0, 0, n)
            with act.Fori(0, NH // 2 - 1) as i:
                for p in range(2):
                    sweep(2 * i + p, p, True)
            sweep(NH - 2, 0, True)
            sweep(NH - 1, 1, False)

        @block.vector
        def _(dve):
            step = Steps(dve, dve_step)
            V = nc.vector
            V.memset(ones[:], 1.0).then_inc(setup, 1)
            V.memset(rms_eps[:], RMS_EPS).then_inc(setup, 1)
            for p in range(2):
                V.memset(v_one[p][:, :, HD:P], 1.0)
                V.memset(k_hi[p][ONE, :].bitcast(F32), 1.0)
                V.memset(k_lo[p][ONE, :].bitcast(F32), 0.0)
                V.memset(q_lo[p][ONE, :].bitcast(F32), 0.0)
            dve.wait_ge(in_sem, 32)
            V.tensor_copy(causal_r[:], causal[:]).then_inc(causal_rr, 1)
            V.tensor_copy(ident_r[:], ident[:]).then_inc(causal_rr, 1)
            where, turns = probs[0], cos
            step.mark(V.tensor_copy(where[:], pos[:]))
            step.wait()
            step.mark(V.tensor_scalar(sin[:], where[:], cols[:, C_FREQ:C_FREQ + 1], None, ALU.mult))
            step.wait()
            step.mark(V.tensor_scalar(turns[:], sin[:], 1.0 / PI2, MAGIC, ALU.mult, ALU.add))
            step.wait()
            step.mark(V.tensor_scalar(turns[:], turns[:], MAGIC, None, ALU.subtract))
            for c in (C1, C2, C3):
                step.wait()
                step.mark(V.scalar_tensor_tensor(sin[:], turns[:], -c, sin[:], ALU.mult, ALU.add))
            step.wait()
            step.mark(V.tensor_scalar(sin[:], sin[:], PI_BELOW, -PI_BELOW, ALU.min, ALU.max))
            step.wait()
            step.mark(V.scalar_tensor_tensor(where[:], sin[:], -1.0, sin[:], ALU.mult, ALU.max))
            step.wait()
            V.tensor_scalar(cos[:], where[:], -1.0, float(np.pi / 2), ALU.mult, ALU.add).then_inc(sin_in, 1)
            for n, (root, tile0, tiles, gain) in enumerate(((rot_a, T_CQ, QLT, C_QG), (rot_b, T_CKV, KVLT, C_KVG))):
                dve.wait_ge(roots, n + 1)
                step.mark(V.reciprocal(root[:], root[:]))
                step.wait()
                for c in range(tiles):
                    last = V.scalar_tensor_tensor(hT[:, tile0 + c, :], hT[:, tile0 + c, :], cols[:, gain + c:gain + c + 1],
                                                  root[:], ALU.mult, ALU.mult)
            last.then_inc(ready, 1)
            dve.wait_ge(ready, 1)
            dve.wait_ge(sin_out, 2)
            step.mark(V.tensor_scalar(sin[:], sin[:], cols[:, C_SIGN:C_SIGN + 1], None, ALU.mult))
            step.wait()
            step.mark(V.tensor_tensor(rot_a[pe32, :], hT[pe32, T_PE, :], cos[pe32, :], ALU.mult))
            step.mark(V.tensor_tensor(rot_b[pe32, :], hT[sw32, T_PE, :], sin[sw32, :], ALU.mult))
            step.wait()
            step.mark(V.tensor_tensor(rot_a[pe32, :], rot_a[pe32, :], rot_b[pe32, :], ALU.add))
            step.wait()
            for p in range(2):
                step.mark(V.tensor_copy(k_hi[p][pe32, :], rot_a[pe32, :]))
            step.wait()
            for p in range(2):
                last = V.tensor_tensor(k_lo[p][pe32, :], rot_a[pe32, :], k_hi[p][pe32, :].bitcast(F32), ALU.subtract)
            last.then_inc(ready, 1)

            def front(h, p, first=False):
                dve.wait_ge(q_hi_done, h + 1)
                V.tensor_tensor(q_lo[p][lo64, :], flat(A, lo64), q_hi[p][lo64, :].bitcast(F32), ALU.subtract)
                if first:
                    dve.wait_ge(ready, 2)
                else:
                    dve.wait_ge(q_ready, h)
                V.tensor_tensor(rot_a[pe32, :], flat(A, pe32), cos[pe32, :], ALU.mult).then_inc(rot_ready, 1)
                V.tensor_tensor(rot_b[pe32, :], flat(A, sw32), sin[sw32, :], ALU.mult).then_inc(a_free, 1)
                dve.wait_ge(k_hi_done, h + 1)
                V.tensor_tensor(k_lo[p][lo64, :], flat(A, lo64), k_hi[p][lo64, :].bitcast(F32), ALU.subtract)\
                    .then_inc(a_free, 1)
                for n, qt in enumerate(S_ORDER):
                    dve.wait_ge(item, ITEMS * h + 4 + n)
                    last = V.reduce_max(top[:, qt:qt + 1], flat(A)[:, 0:(qt + 1) * P], AX_X).then_inc(a_free, 1)
                dve.wait_ge(a_free, FREES * (h + 1))
                V.tensor_scalar(top_r[:], top[:], -1.0, None, ALU.mult).then_inc(m_ready, 1)

            def leave(h, p):
                dve.wait_ge(pv_done, TT * (h + 1) + PROBS_FREE)
                step.mark(V.reciprocal(recip[lo64, :], flat(O, hi64)))
                step.wait()
                dve.wait_ge(y_done, h - 1 + Y_FREE)
                V.tensor_tensor(y_full[64 * p:64 * p + 64, :], flat(O, lo64), recip[lo64, :], ALU.mult)\
                    .then_inc(o_read, 1)

            dve.sem_inc(o_read, O_FREE)
            front(0, 0, True)
            with dve.Fori(0, NH // 2 - 1) as i:
                step.enter(i, 2)
                for p in range(2):
                    front(2 * i + p + 1, 1 - p)
                    leave(2 * i + p, p)
                step.leave(NH // 2 - 1)
            front(NH - 1, 1)
            leave(NH - 2, 0)
            leave(NH - 1, 1)

        @block.gpsimd
        def _(pool):
            step = Steps(pool, pool_step)
            G = nc.gpsimd

            def rotate(h, p):
                pool.wait_ge(rot_ready, h + 1)
                pool.wait_ge(a_free, FREES * h + 1)
                step.mark(G.tensor_tensor(q_hi[p][pe32, :], rot_a[pe32, :], rot_b[pe32, :], ALU.add))
                step.mark(G.tensor_tensor(rot_a[pe32, :], rot_a[pe32, :], rot_b[pe32, :], ALU.add))
                step.wait()
                G.tensor_tensor(q_lo[p][pe32, :], rot_a[pe32, :], q_hi[p][pe32, :].bitcast(F32), ALU.subtract)\
                    .then_inc(q_ready, 1)

            def store(h, p, i):
                rows = slice(64 * p, 64 * p + 64)
                pool.wait_ge(o_read, h + 1 + O_FREE)
                step.mark(G.tensor_tensor(ym_hi[rows, i, :], y_full[rows, :], ones[rows, 0:1].to_broadcast([64, S]),
                                          ALU.mult))
                step.wait()
                G.tensor_tensor(ym_lo[rows, i, :], y_full[rows, :], ym_hi[rows, i, :].bitcast(F32), ALU.subtract)\
                    .then_inc(y_done, 1)

            pool.sem_inc(y_done, Y_FREE)
            rotate(0, 0)
            with pool.Fori(0, NH // 2 - 1) as i:
                step.enter(i, 6)
                for p in range(2):
                    rotate(2 * i + p + 1, 1 - p)
                    store(2 * i + p, p, i)
                step.leave(NH // 2 - 1)
            rotate(NH - 1, 1)
            store(NH - 2, 0, NH // 2 - 1)
            store(NH - 1, 1, NH // 2 - 1)


def rwkv_inputs(nc, mem, k, t):
    hT, cols, ps = k.hT, k.cols, k.ps
    w_lora = mem.at("w_lora", 94, [P, RW])
    reset = mem.at("reset", 96, [P, S])
    logw = [mem.at(f"logw{j}", 100 + 4 * j, [P, S]) for j in range(2)]
    norm = [mem.at(f"norm{j}", 108 + 4 * j, [P, S]) for j in range(2)]
    square = [mem.at(f"kk_square{j}", 116 + 4 * j, [P, S]) for j in range(2)]
    rate = [mem.at(f"rate{j}", 124 + 4 * j, [P, S]) for j in range(2)]
    keep_a = mem.at("keep_a", 4.25, [P, RT])
    beta, cum, kk, ones_block = k.beta, k.cum, k.kk, k.ones_block
    flat = lambda b: ps[:, b:b + 2, :].rearrange("p b n -> p (b n)")
    with ExitStack() as ctx:
        loaded, tanh_done, z_mm, a_mm, logw_done, rate_done, sq_done, ss_mm, root_done, k_free, cum_done, step_s = sems(
            nc, ctx, "c_loaded", "c_tanh", "c_z_mm", "c_a_mm", "c_logw", "c_rate", "c_sq", "c_ss_mm", "c_root",
            "c_k_free", "c_cum", "c_dve_step")
        kk_done, = sems(nc, ctx, "c_kk_done")
        block = ctx.enter_context(nc.Block())

        @block.sync
        def _(sp):
            sp.dma_start(w_lora[:], t["w_lora"]).then_inc(loaded, 16)
            sp.dma_start(ones_block[:], t["ones_block"]).then_inc(loaded, 16)
            sp.dma_start(k.gate[:], t["gate_g2"]).then_inc(loaded, 16)
            sp.dma_start(k.chunk_mask[:], t["chunk_mask"]).then_inc(loaded, 16)
            sp.dma_start(k.merge[:], t["merge"]).then_inc(loaded, 16)
            sp.wait_ge(loaded, 80)

        @block.tensor
        def _(pe):
            pe.wait_ge(loaded, 80)
            pe.wait_ge(tanh_done, 1)
            for c in range(RT):
                for n, (done, free, rows) in enumerate(((z_mm, logw_done, slice(0, 64)), (a_mm, rate_done, slice(64, P)))):
                    if c:
                        pe.wait_ge(free, c)
                    for b in range(2):
                        last = nc.tensor.matmul(ps[:, 2 * n + b, :], w_lora[rows, c * P:(c + 1) * P],
                                                hT[rows, T_WA, b * HALF:(b + 1) * HALF], start=True, stop=True)
                    last.then_inc(done, 1)
            for c in range(RT):
                pe.wait_ge(sq_done, c + 1)
                if c >= 2:
                    pe.wait_ge(root_done, c - 1)
                for b in range(2):
                    last = nc.tensor.matmul(ps[:, 4 + 2 * (c % 2) + b, :], ones_block[:],
                                            square[c % 2][:, b * HALF:(b + 1) * HALF], start=True, stop=True)
                last.then_inc(ss_mm, 1)

        def root(act, c):
            act.wait_ge(ss_mm, c + 1)
            if c >= 2:
                act.wait_ge(kk_done, c - 1)
            nc.scalar.activation(norm[c % 2][:], flat(4 + 2 * (c % 2)), ACT.Sqrt).then_inc(root_done, 1)

        @block.scalar
        def _(act):
            nc.scalar.activation(hT[0:64, T_WA, :], hT[0:64, T_WA, :], ACT.Tanh).then_inc(tanh_done, 1)
            nc.scalar.activation(hT[:, T_G, :], hT[:, T_G, :], ACT.Sigmoid)
            for c in range(RT):
                act.wait_ge(z_mm, c + 1)
                if c >= 2:
                    act.wait_ge(cum_done, c - 1)
                nc.scalar.activation(logw[c % 2][:], flat(0), ACT.Sigmoid, bias=cols[:, C_W0 + c:C_W0 + c + 1])\
                    .then_inc(logw_done, 1)
                act.wait_ge(a_mm, c + 1)
                nc.scalar.activation(beta[:, c, :], flat(2), ACT.Sigmoid, bias=cols[:, C_A0 + c:C_A0 + c + 1])\
                    .then_inc(rate_done, 1)
            for c in range(RT):
                if c >= 2:
                    act.wait_ge(ss_mm, c - 1)
                nc.scalar.activation(square[c % 2][:], hT[:, T_K + c, :], ACT.Square,
                                     scale=cols[:, C_KK + c:C_KK + c + 1]).then_inc(sq_done, 1)
                if c:
                    root(act, c - 1)
            root(act, RT - 1)

        @block.vector
        def _(dve):
            V = nc.vector
            step = Steps(dve, step_s)
            V.memset(k.one[:], 1.0)
            step.mark(V.memset(reset[:], 1.0))
            step.wait()
            V.memset(reset[:].rearrange("p (n c) -> p n c", c=CH)[:, :, 0:1], 0.0)
            step.mark(V.tensor_scalar(keep_a[:], cols[:, C_KA:C_KA + RT], -1.0, 1.0, ALU.mult, ALU.add))
            for c in range(RT):
                dve.wait_ge(logw_done, c + 1)
                step.mark(V.tensor_scalar(logw[c % 2][:], logw[c % 2][:], -EXP_M05, None, ALU.mult))
                step.wait()
                V.tensor_tensor_scan(cum[:, c, :], reset[:], logw[c % 2][:], 0.0, ALU.mult, ALU.add).then_inc(cum_done, 1)
            for c in range(RT):
                dve.wait_ge(sq_done, c + 1)
                dve.wait_ge(rate_done, c + 1)
                dve.wait_ge(root_done, c + 1)
                step.mark(V.tensor_scalar(norm[c % 2][:], norm[c % 2][:], 1e-12, None, ALU.max))
                step.mark(V.tensor_scalar(rate[c % 2][:], beta[:, c, :], cols[:, C_KA + c:C_KA + c + 1],
                                          keep_a[:, c:c + 1], ALU.mult, ALU.add))
                step.wait(step.n - 1)
                step.mark(V.reciprocal(norm[c % 2][:], norm[c % 2][:]))
                step.wait()
                step.mark(V.scalar_tensor_tensor(kk[:, c, :], hT[:, T_K + c, :], cols[:, C_KK + c:C_KK + c + 1],
                                                 norm[c % 2][:], ALU.mult, ALU.mult))
                V.tensor_tensor(hT[:, T_K + c, :], hT[:, T_K + c, :], rate[c % 2][:], ALU.mult)
                step.wait()
                V.scalar_tensor_tensor(beta[:, c, :], beta[:, c, :], -1.0, kk[:, c, :], ALU.mult, ALU.mult)\
                    .then_inc(kk_done, 1)


def rwkv_chunks(nc, mem, k):
    ident, ps = k.ident, k.ps
    hT, cum, kk_all, beta, mask, merge = k.hT, k.cum, k.kk, k.beta, k.chunk_mask, k.merge
    at = [94.0]

    def new(name, shape, dtype=F32, copies=1):
        out = []
        size = -(-int(np.prod(shape[1:])) * 4 // 32) * 32 / KB
        for n in range(copies):
            out.append(mem.at(f"{name}{n}", at[0], shape, dtype))
            at[0] += size
        return out if copies > 1 else out[0]

    pair = [P, RT, P]
    decay = new("decay", [P, RT, CH + 1], copies=2)
    undecay = new("undecay", [P, RT, CH], copies=2)
    bk = new("bk_chunk", [P, RT, 2, CH], copies=2)
    ar = new("ar_chunk", [P, RT, 2, CH], copies=2)
    v_st = new("v_static", [P, RT, CH], copies=2)
    scores = new("scores", [P, 2, RT, P], copies=2)
    inv_t = new("inverse_t", pair, copies=2)
    bk_tok = new("bk_tok", pair, copies=2)
    uv = new("u_v", [P, 2, RT, CH], copies=2)
    sv = new("s_v", [P, 2, RT, CH], copies=2)
    am = new("a_m", [P, 2, RT, CH], copies=2)
    rho = new("rho", [P, 2, RT, CH], copies=2)
    end = new("end_decay", [64, 2, RT], copies=2)
    low_t = new("lower_t", pair)
    inv = new("inverse", pair)
    prod = new("product", pair)
    rhs = new("rhs", [P, RT, CH])
    state_sum = new("state_sum", [64, 2, RT, CH])
    assert at[0] <= 153, at
    LEVELS = 6
    lo, hi = slice(0, 64), slice(64, P)
    half = lambda p: slice(64 * p, 64 * p + 64)
    grp = lambda g: slice(2 * g, 2 * g + 2)
    B_SA, B_RHS = 0, 1
    B_T1, B_X, B_XT = (2, 3), (4, 5), (6, 7)
    B_BKT, B_V = 6, 7
    view = lambda bank, n=P, rows=slice(0, P), cols=2: ps[rows, bank, 0:cols * n].rearrange("p (c n) -> p c n", n=n)

    with ExitStack() as ctx:
        exps, bk_ready, x_reset, ar_ready, scores_mm, tr_done, sc_ready, low_ready, am_ready, tok_ready, init = sems(
            nc, ctx, "d_exps", "d_bk_ready", "d_x_reset", "d_ar_ready", "d_scores_mm", "d_tr_done", "d_sc_ready",
            "d_low_ready", "d_am_ready", "d_tok_ready", "d_init")
        t1_mm = sems(nc, ctx, "d_t1_mm0", "d_t1_mm1")
        t1_out = sems(nc, ctx, "d_t1_out0", "d_t1_out1")
        x_mm = sems(nc, ctx, "d_x_mm0", "d_x_mm1")
        xt_mm = sems(nc, ctx, "d_xt_mm0", "d_xt_mm1")
        x_up = sems(nc, ctx, "d_x_up0", "d_x_up1")
        xt_up = sems(nc, ctx, "d_xt_up0", "d_xt_up1")
        rhs_mm, rhs_ready, sa_mm, sa_ready, s_mm, state_ready, y_mm, y_out, dve_step, passed = sems(
            nc, ctx, "d_rhs_mm", "d_rhs_ready", "d_sa_mm", "d_sa_ready", "d_s_mm", "d_state_ready", "d_y_mm",
            "d_y_out", "d_dve_step", "d_passed")
        SLOTS_FREE, Y_FREE = 2, 1
        block = ctx.enter_context(nc.Block())

        def stages(body, eng):
            body(0, 0, False, True)
            with eng.Fori(0, NC_ // 2 - 1) as i:
                body(2 * i + 1, 1, True, True)
                body(2 * i + 2, 0, True, True)
            body(NC_ - 1, 1, True, False)

        @block.tensor
        def _(pe):
            mm = nc.tensor.matmul

            def rhs_step(n, q):
                pe.wait_ge(am_ready, n + 1)
                pe.wait_ge(tok_ready, n + 1)
                pe.wait_ge(state_ready, n + 1)
                for c in range(RT):
                    for p in range(2):
                        last = mm(ps[half(p), B_RHS, c * CH:(c + 1) * CH], am[q][:, p, c, :], sv[q][:, p, c, :],
                                  start=True, stop=True)
                last.then_inc(rhs_mm, 1)

            def sa_step(n, q):
                pe.wait_ge(rhs_ready, n + 1)
                for g in range(2):
                    pe.wait_ge(xt_up[g], LEVELS * (n + 1))
                for c in range(RT):
                    last = mm(ps[:, B_SA, c * CH:(c + 1) * CH], inv_t[q][:, c, :], rhs[:, c, :], start=True, stop=True)
                last.then_inc(sa_mm, 1)

            def state_step(n, q):
                pe.wait_ge(sa_ready, n + 1)
                for p in range(2):
                    for c in range(RT):
                        last = mm(ps[lo, B_SA, (p * RT + c) * CH:(p * RT + c + 1) * CH], bk_tok[q][:, c, half(p)],
                                  uv[q][:, p, c, :], start=True, stop=True)
                last.then_inc(s_mm, 1)

            def y_step(n, q):
                for c in range(RT):
                    for p in range(2):
                        out = ps[half(p), B_RHS, c * CH:(c + 1) * CH]
                        mm(out, sv[q][:, p, c, :], rho[q][:, p, c, :], start=True, stop=False)
                        last = mm(out, uv[q][:, p, c, :], scores[q][:, p, c, CH:P], start=False, stop=True)
                last.then_inc(y_mm, 1)

            def stage(m, q, chain, ahead):
                n, qn = m - 1, 1 - q
                pe.wait_ge(bk_ready, m + 1)
                pe.wait_ge(ar_ready, m + 1)
                if chain:
                    pe.wait_ge(y_out, m - 1 + Y_FREE)
                    pe.wait_ge(state_ready, m)
                for c in range(RT):
                    for p in range(2):
                        last = mm(ps[:, p, c * P:(c + 1) * P], bk[q][half(p), c, :, :].rearrange("p a t -> p (a t)"),
                                  ar[q][half(p), c, :, :].rearrange("p a t -> p (a t)"), start=True, stop=True)
                last.then_inc(scores_mm, 1)
                if chain:
                    for g in range(2):
                        pe.wait_ge(xt_up[g], LEVELS * m)
                for c in range(RT):
                    nc.tensor.transpose(ps[:, B_BKT, c * P:(c + 1) * P],
                                        bk[q][:, c, :, :].rearrange("p a t -> p (a t)"), ident[:])
                for c in range(RT):
                    last = nc.tensor.transpose(ps[lo, B_V, c * P:(c + 1) * P], v_st[q][:, c, :], ident[:])
                last.then_inc(tr_done, 1)
                pe.wait_ge(low_ready, m + 1)
                for g in range(2):
                    for c in range(2):
                        last = mm(ps[:, B_T1[g], c * P:(c + 1) * P], low_t[:, 2 * g + c, :], ident[:], start=True, stop=True)
                    last.then_inc(t1_mm[g], 1)
                if chain:
                    pe.wait_ge(sc_ready, m + 1)
                    rhs_step(n, qn)
                for l in range(1, LEVELS):
                    for g in range(2):
                        pe.wait_ge(x_up[g], (LEVELS - 1) * m + l)
                        for c in range(2):
                            last = mm(ps[:, B_T1[g], c * P:(c + 1) * P], low_t[:, 2 * g + c, :], inv[:, 2 * g + c, :],
                                      start=True, stop=True)
                        last.then_inc(t1_mm[g], 1)
                    if chain and l == 1:
                        sa_step(n, qn)
                    if chain and l == 2:
                        state_step(n, qn)
                    if chain and l == 3:
                        y_step(n, qn)
                    if l == 1:
                        pe.wait_ge(tok_ready, m + 1)
                    for g in range(2):
                        pe.wait_ge(t1_out[g], (LEVELS - 1) * m + l)
                        pe.wait_ge(xt_up[g], LEVELS * m + l)
                        if l < LEVELS - 1:
                            for c in range(2):
                                last = mm(ps[:, B_X[g], c * P:(c + 1) * P], inv_t[q][:, 2 * g + c, :], prod[:, 2 * g + c, :],
                                          start=True, stop=True)
                            last.then_inc(x_mm[g], 1)
                        for c in range(2):
                            last = mm(ps[:, B_XT[g], c * P:(c + 1) * P], prod[:, 2 * g + c, :], inv_t[q][:, 2 * g + c, :],
                                      start=True, stop=True)
                        last.then_inc(xt_mm[g], 1)

            pe.wait_ge(init, 1)
            pe.sem_inc(y_mm, SLOTS_FREE)
            stages(stage, pe)
            n, q = NC_ - 1, 1
            pe.wait_ge(y_out, n + Y_FREE)
            rhs_step(n, q)
            sa_step(n, q)
            state_step(n, q)
            y_step(n, q)

        @block.scalar
        def _(act):
            A = nc.scalar.activation

            def exp_step(m, q):
                if type(m) is not int:
                    act.wait_ge(ar_ready, m - 1)
                    act.wait_ge(bk_ready, m - 1)
                A(decay[q][:, :, 1:CH + 1], cum[:, :, bass.ds(m * CH, CH)], ACT.Exp)
                A(undecay[q][:], cum[:, :, bass.ds(m * CH, CH)], ACT.Exp, scale=-1.0).then_inc(exps, 1)

            def u_step(n, q):
                act.wait_ge(sa_mm, n + 1)
                for p in range(2):
                    last = A(uv[q][lo, p, :, :], view(B_SA, CH, half(p), RT), ACT.Copy)
                last.then_inc(sa_ready, 1)

            def y_leave(n, q):
                act.wait_ge(y_mm, n + 1 + SLOTS_FREE)
                A(cum[:, :, bass.ds(n * CH, CH)], view(B_RHS, CH, cols=RT), ACT.Copy).then_inc(y_out, 1)

            def stage(m, q, chain, ahead):
                n, qn = m - 1, 1 - q
                act.wait_ge(y_mm, m - 1 + SLOTS_FREE)
                act.wait_ge(ar_ready, m + 1)
                for p in range(2):
                    A(am[q][lo, p, :, :], ar[q][half(p), :, 0, :], ACT.Copy)
                    A(rho[q][lo, p, :, :], ar[q][half(p), :, 1, :], ACT.Copy)
                    A(end[q][:, p, :], decay[q][half(p), :, CH], ACT.Copy)
                act.wait_ge(sc_ready, m + 1)
                for p in range(2):
                    last = A(low_t[half(p), :, half(p)], scores[q][lo, p, :, 0:CH], ACT.Copy)
                last.then_inc(low_ready, 1)
                A(am[q][hi, :, :, :].rearrange("p a c t -> p (a c) t"),
                  scores[q][hi, :, :, 0:CH].rearrange("p a c t -> p (a c) t"), ACT.Copy).then_inc(am_ready, 1)
                act.wait_ge(tr_done, m + 1)
                A(bk_tok[q][:], view(B_BKT, cols=RT), ACT.Copy)
                v_tok = ps[lo, B_V, :].rearrange("p (c a d) -> p a c d", a=2, d=HD)
                A(sv[q][hi, :, :, :], v_tok, ACT.Copy)
                A(uv[q][hi, :, :, :], v_tok, ACT.Copy).then_inc(tok_ready, 1)
                for l in range(1, LEVELS):
                    for g in range(2):
                        act.wait_ge(t1_mm[g], LEVELS * m + l + 1)
                        A(prod[:, grp(g), :], view(B_T1[g]), ACT.Copy).then_inc(t1_out[g], 1)
                    if chain and l == 1:
                        u_step(n, qn)
                    if chain and l == 3:
                        y_leave(n, qn)
                if ahead:
                    exp_step(m + 1, 1 - q)

            act.wait_ge(init, 1)
            exp_step(0, 0)
            stages(stage, act)
            u_step(NC_ - 1, 1)
            y_leave(NC_ - 1, 1)

        @block.vector
        def _(dve):
            V = nc.vector
            step = Steps(dve, dve_step)

            def ar_step(m, q):
                if not (type(m) is int and m < 2):
                    dve.wait_ge(scores_mm, m - 1)
                    dve.wait_ge(am_ready, m - 1)
                dve.wait_ge(exps, m + 1)
                now = bass.ds(m * CH, CH)
                V.tensor_tensor(ar[q][:, :, 0, :], kk_all[:, :, now], decay[q][:, :, 0:CH], ALU.mult)
                V.tensor_tensor(ar[q][:, :, 1, :], hT[:, T_R:T_R + RT, now], decay[q][:, :, 1:CH + 1], ALU.mult)\
                    .then_inc(ar_ready, 1)

            def rhs_out(n, q):
                dve.wait_ge(rhs_mm, n + 1)
                V.tensor_copy(rhs[:], view(B_RHS, CH, cols=RT)).then_inc(rhs_ready, 1)

            def state_out(n, q):
                dve.wait_ge(s_mm, n + 1)
                flat = lambda x: x.rearrange("p a c d -> p (a c) d")
                step.mark(V.tensor_tensor(flat(state_sum[:]), flat(sv[q][lo, :, :, :]), view(B_SA, CH, lo, 2 * RT), ALU.add))
                step.wait()
                V.tensor_tensor(flat(sv[1 - q][lo, :, :, :]), flat(state_sum[:]),
                                end[q][:].rearrange("p a (c o) -> p (a c) o", o=1).to_broadcast([64, 2 * RT, CH]),
                                ALU.mult).then_inc(state_ready, 1)

            def wait_alone(sem, value):
                dve.wait_ge(sem, value).then_inc(passed, 1)

            def merged(x, l, transposed, new, g):
                m01 = merge[:, 2 * l + transposed:2 * l + transposed + 1, :].to_broadcast([P, 2, P])
                return V.copy_predicated(x[:, grp(g), :], m01, new)

            def stage(m, q, chain, ahead):
                n, qn = m - 1, 1 - q
                dve.wait_ge(scores_mm, m + 1)
                dve.wait_ge(y_mm, m - 1 + SLOTS_FREE)
                for p in range(2):
                    last = V.tensor_tensor(scores[q][:, p, :, :], view(p, cols=RT),
                                           mask[:].rearrange("p (o n) -> p o n", o=1).to_broadcast([P, RT, P]), ALU.mult)
                last.then_inc(sc_ready, 1)
                wait_alone(x_reset, m + 1)
                wait_alone(low_ready, m + 1)
                for g in range(2):
                    merged(inv_t[q], 0, 1, low_t[:, grp(g), :], g).then_inc(xt_up[g], 1)
                for g in range(2):
                    wait_alone(t1_mm[g], LEVELS * m + 1)
                    merged(inv, 0, 0, view(B_T1[g]), g).then_inc(x_up[g], 1)
                if chain:
                    rhs_out(n, qn)
                for l in range(1, LEVELS):
                    for g in range(2):
                        if l < LEVELS - 1:
                            wait_alone(x_mm[g], (LEVELS - 2) * m + l)
                            merged(inv, l, 0, view(B_X[g]), g).then_inc(x_up[g], 1)
                        wait_alone(xt_mm[g], (LEVELS - 1) * m + l)
                        merged(inv_t[q], l, 1, view(B_XT[g]), g).then_inc(xt_up[g], 1)
                    if chain and l == 2:
                        state_out(n, qn)
                if ahead:
                    ar_step(m + 1, 1 - q)

            for q in range(2):
                V.memset(decay[q][:, :, 0:1], 1.0)
                V.memset(rho[q][hi, :, :, :], 0.0)
            V.memset(sv[0][lo, :, :, :], 0.0).then_inc(state_ready, 1)
            V.memset(low_t[:], 0.0).then_inc(init, 1)
            ar_step(0, 0)
            stage(0, 0, False, True)
            with dve.Fori(0, NC_ // 2 - 1) as i:
                step.enter(i, 2)
                stage(2 * i + 1, 1, True, True)
                stage(2 * i + 2, 0, True, True)
                step.leave(NC_ // 2 - 1)
            stage(NC_ - 1, 1, True, False)
            rhs_out(NC_ - 1, 1)
            state_out(NC_ - 1, 1)

        @block.gpsimd
        def _(pool):
            G = nc.gpsimd

            def bk_step(m, q):
                if not (type(m) is int and m < 2):
                    pool.wait_ge(tr_done, m - 1)
                pool.wait_ge(exps, m + 1)
                now = bass.ds(m * CH, CH)
                G.tensor_tensor(bk[q][:, :, 0, :], beta[:, :, now], undecay[q][:], ALU.mult)
                G.tensor_tensor(bk[q][:, :, 1, :], hT[:, T_K:T_K + RT, now], undecay[q][:], ALU.mult)
                G.tensor_copy(v_st[q][:], hT[:, T_V:T_V + RT, now]).then_inc(bk_ready, 1)

            def stage(m, q, chain, ahead):
                if chain:
                    pool.wait_ge(t1_mm[1], LEVELS * m)
                    pool.wait_ge(y_mm, m - 1 + SLOTS_FREE)
                eye = ident[:].rearrange("p (o n) -> p o n", o=1).to_broadcast([P, RT, P])
                one = k.one[:, 0:1].rearrange("p (a b) -> p a b", a=1).to_broadcast([P, RT, P])
                G.tensor_tensor(inv_t[q][:], eye, one, ALU.mult)
                G.tensor_tensor(inv[:], eye, one, ALU.mult).then_inc(x_reset, 1)
                if ahead:
                    bk_step(m + 1, 1 - q)

            pool.sem_inc(y_out, Y_FREE)
            bk_step(0, 0)
            stages(stage, pool)


def rwkv_outputs(nc, mem, k):
    hT, cols, ps, y, ones_block = k.hT, k.cols, k.ps, k.cum, k.ones_block
    square = [mem.at(f"dev_square{j}", 126 + 4 * j, [P, S]) for j in range(2)]
    scale = [mem.at(f"gn_scale{j}", 134 + 4 * j, [P, S]) for j in range(2)]
    dot = [mem.at(f"bonus{j}", 142 + 4 * j, [P, S]) for j in range(2)]
    full = [mem.at(f"yr_full{j}", 150 + 4 * j, [P, S]) for j in range(2)]
    gn_eps = mem.at("gn_eps", 4.5, [P, 1])
    flat = lambda b: ps[:, b:b + 2, :].rearrange("p b n -> p (b n)")
    with ExitStack() as ctx:
        init, mean_mm, dot_in, dot_mm, gate_mm, dev, sq_done, var_mm, root_done, done, hi_done, lo_done, step_s = sems(
            nc, ctx, "e_init", "e_mean_mm", "e_dot_in", "e_dot_mm", "e_gate_mm", "e_dev", "e_sq", "e_var_mm",
            "e_root", "e_done", "e_hi", "e_lo", "e_dve_step")
        block = ctx.enter_context(nc.Block())

        @block.tensor
        def _(pe):
            def product(bank, w, r):
                for b in range(2):
                    last = nc.tensor.matmul(ps[:, bank + b, :], w, r[:, b * HALF:(b + 1) * HALF], start=True, stop=True)
                return last

            for c in range(RT):
                if c:
                    pe.wait_ge(dev, c)
                product(0, ones_block[:], y[:, c, :]).then_inc(mean_mm, 1)
                pe.wait_ge(dot_in, c + 1)
                if c:
                    pe.wait_ge(done, c)
                product(2, ones_block[:], dot[c % 2]).then_inc(dot_mm, 1)
                product(4, k.gate[:, c * P:(c + 1) * P], hT[:, T_G, :]).then_inc(gate_mm, 1)
                pe.wait_ge(sq_done, c + 1)
                if c:
                    pe.wait_ge(root_done, c)
                product(6, ones_block[:], square[c % 2]).then_inc(var_mm, 1)

        @block.scalar
        def _(act):
            act.wait_ge(init, 1)
            for c in range(RT):
                act.wait_ge(dev, c + 1)
                nc.scalar.activation(square[c % 2][:], y[:, c, :], ACT.Square).then_inc(sq_done, 1)
                act.wait_ge(var_mm, c + 1)
                nc.scalar.activation(scale[c % 2][:], flat(6), ACT.Sqrt, scale=1.0 / HD, bias=gn_eps[:])\
                    .then_inc(root_done, 1)
                act.wait_ge(done, c + 1)
                nc.scalar.activation(k.yr_hi[:, c, :], full[c % 2][:], ACT.Copy).then_inc(hi_done, 1)

        @block.vector
        def _(dve):
            V = nc.vector
            step = Steps(dve, step_s)
            V.memset(gn_eps[:], GN_EPS).then_inc(init, 1)

            for c in range(RT):
                V.scalar_tensor_tensor(dot[c % 2][:], hT[:, T_R + c, :], cols[:, C_RK + c:C_RK + c + 1],
                                       hT[:, T_K + c, :], ALU.mult, ALU.mult).then_inc(dot_in, 1)
                dve.wait_ge(mean_mm, c + 1)
                V.scalar_tensor_tensor(y[:, c, :], flat(0), -1.0 / HD, y[:, c, :], ALU.mult, ALU.add).then_inc(dev, 1)
                dve.wait_ge(dot_mm, c + 1)
                step.mark(V.tensor_tensor(dot[c % 2][:], flat(2), hT[:, T_V + c, :], ALU.mult))
                dve.wait_ge(root_done, c + 1)
                step.mark(V.reciprocal(scale[c % 2][:], scale[c % 2][:]))
                step.wait()
                step.mark(V.scalar_tensor_tensor(y[:, c, :], y[:, c, :], cols[:, C_LG + c:C_LG + c + 1], scale[c % 2][:],
                                                 ALU.mult, ALU.mult))
                step.wait()
                step.mark(V.scalar_tensor_tensor(y[:, c, :], y[:, c, :], cols[:, C_LB + c:C_LB + c + 1], dot[c % 2][:],
                                                 ALU.add, ALU.add))
                step.wait()
                dve.wait_ge(gate_mm, c + 1)
                V.tensor_tensor(full[c % 2][:], flat(4), y[:, c, :], ALU.mult).then_inc(done, 1)
                dve.wait_ge(hi_done, c + 1)
                V.tensor_tensor(k.yr_lo[:, c, :], full[c % 2][:], k.yr_hi[:, c, :].bitcast(F32), ALU.subtract)\
                    .then_inc(lo_done, 1)


def layer_norm_stats(nc, dve, step, rows, stats, mean_var):
    a = step.mark(nc.vector.bn_stats(stats[:, 0, :], rows[:, 0:HALF]))
    step.mark(nc.vector.bn_stats(stats[:, 1, :], rows[:, HALF:D]))
    step.wait()
    return nc.vector.bn_aggr(mean_var, stats[:].rearrange("p a n -> p (a n)"))


def mix_out(nc, mem, k, t):
    ps, x1 = k.ps, k.x1
    w_hi = mem.at("wout_hi", 126, [P, KT, D], F32R)
    w_lo = mem.at("wout_lo", 158, [P, KT, D], F32R)
    w_raw = [mem.at(f"wout_raw{j}", 190 + 4 * j, [P, D]) for j in range(2)]
    gain = mem.at("ln1_gain", 70, [P, D])
    bias = mem.at("ln1_bias", 74, [P, D])
    stats = mem.at("ln1_stats", 78, [P, TT, 2, 6])
    mean_var = mem.at("ln1_mean_var", 78.5, [P, TT, 2])
    sd = mem.at("ln1_sd", 79, [P, TT])
    eps = mem.at("ln1_eps", 79.25, [P, 1])
    y = lambda kt: (k.yr_hi, k.yr_lo) if kt < RT else (k.ym_hi, k.ym_lo)
    with ExitStack() as ctx:
        x_in, rows_in, init, w_whi, w_split, mix_mm, mixed, var_done, sd_done, scaled, normed, step_s = sems(
            nc, ctx, "f_x_in", "f_rows_in", "f_init", "f_w_hi", "f_w_split", "f_mix_mm", "f_mixed", "f_var",
            "f_sd", "f_scaled", "f_normed", "f_dve_step")
        pool_step, = sems(nc, ctx, "f_pool_step")
        w_in = sems(nc, ctx, "f_w_in0", "f_w_in1")
        block = ctx.enter_context(nc.Block())

        @block.sync
        def _(sp):
            for kt in range(KT):
                if kt >= 2:
                    sp.wait_ge(w_split, kt - 1)
                sp.dma_start(w_raw[kt % 2][:], t["w_out"][kt]).then_inc(w_in[kt % 2], 16)
                if kt == 1:
                    sp.dma_start(x1[:], t["x"].rearrange("o (t p) d -> p (o t) d", p=P)).then_inc(x_in, 16)
                    sp.dma_start(gain[:], t["ln"][0:1, :].to_broadcast([P, D])).then_inc(rows_in, 16)
                    sp.dma_start(bias[:], t["ln"][1:2, :].to_broadcast([P, D])).then_inc(rows_in, 16)

        @block.tensor
        def _(pe):
            def products(tt, bank, kt):
                y_hi, y_lo = y(kt)
                tok = slice(tt * P, (tt + 1) * P)
                for n, (a, w) in enumerate(((y_hi, w_hi), (y_hi, w_lo), (y_lo, w_hi))):
                    for b in range(2):
                        last = nc.tensor.matmul(ps[:, bank + b, :], a[:, kt % RT, tok], w[:, kt, b * HALF:(b + 1) * HALF],
                                                start=kt == 0 and n == 0, stop=kt == KT - 1 and n == 2)
                return last

            for kt in range(KT):
                pe.wait_ge(w_split, kt + 1)
                for tt in range(4):
                    last = products(tt, 2 * tt, kt)
                    if kt == KT - 1:
                        last.then_inc(mix_mm, 1)
            for tt in range(4, TT):
                pe.wait_ge(mixed, tt - 3)
                for kt in range(KT):
                    last = products(tt, 2 * (tt - 4), kt)
                last.then_inc(mix_mm, 1)

        @block.scalar
        def _(act):
            act.wait_ge(init, 1)
            for tt in range(TT):
                act.wait_ge(var_done, tt + 1)
                nc.scalar.activation(sd[:, tt:tt + 1], mean_var[:, tt, 1:2], ACT.Sqrt, bias=eps[:]).then_inc(sd_done, 1)

        @block.vector
        def _(dve):
            V = nc.vector
            step = Steps(dve, step_s)
            V.memset(eps[:], LN_EPS).then_inc(init, 1)
            for kt in range(KT):
                dve.wait_ge(w_in[kt % 2], 16 * (kt // 2 + 1))
                split2(nc, dve, w_raw[kt % 2][:], w_hi[:, kt, :], w_lo[:, kt, :], w_whi, kt + 1, w_split)
            dve.wait_ge(x_in, 16)

            def normalise(tt):
                dve.wait_ge(sd_done, tt + 1)
                step.mark(V.reciprocal(sd[:, tt:tt + 1], sd[:, tt:tt + 1]))
                step.wait()
                V.tensor_scalar(x1[:, tt, :], x1[:, tt, :], mean_var[:, tt, 0:1], sd[:, tt:tt + 1],
                                ALU.subtract, ALU.mult).then_inc(scaled, 1)

            for tt in range(TT):
                dve.wait_ge(mix_mm, tt + 1)
                bank = 2 * (tt % 4)
                V.scalar_tensor_tensor(x1[:, tt, :], x1[:, tt, :], ALPHA,
                                       ps[:, bank:bank + 2, :].rearrange("p b n -> p (b n)"), ALU.mult, ALU.add)\
                    .then_inc(mixed, 1)
                dve.wait_ge(mixed, tt + 1)
                layer_norm_stats(nc, dve, step, x1[:, tt, :], stats[:, tt, :, :], mean_var[:, tt, :]).then_inc(var_done, 1)
                if tt:
                    normalise(tt - 1)
            normalise(TT - 1)

        @block.gpsimd
        def _(pool):
            G = nc.gpsimd
            step = Steps(pool, pool_step)
            pool.wait_ge(rows_in, 32)
            for tt in range(TT):
                pool.wait_ge(scaled, tt + 1)
                step.mark(G.tensor_tensor(x1[:, tt, :], x1[:, tt, :], gain[:], ALU.mult))
                step.wait()
                G.tensor_tensor(x1[:, tt, :], x1[:, tt, :], bias[:], ALU.add).then_inc(normed, 1)


def ffn(nc, mem, k, t, out):
    ps, acc, ident = k.ps, k.x1, k.ident
    GRP = 2
    GROUPS = DFF // P // GRP
    OUTS = 2 * TT
    x_hi = mem.at("x1T_hi", 70, [P, KT, S], F32R)
    x_lo = mem.at("x1T_lo", 102, [P, KT, S], F32R)
    hid_hi = [mem.at(f"hid_hi{q}", 134 + 8 * q, [P, GRP, S], F32R) for q in range(2)]
    hid_lo = [mem.at(f"hid_lo{q}", 150 + 8 * q, [P, GRP, S], F32R) for q in range(2)]
    w2_hi = mem.at("w2_hi", 166, [P, GRP, D], F32R)
    w2_lo = mem.at("w2_lo", 174, [P, GRP, D], F32R)
    w2_raw = mem.at("w2_raw", 182, [P, GRP, D])
    w1_hi = [mem.at(f"w1_hi{j}", 190 + 4 * j, [P, KT, P], F32R) for j in range(GRP)]
    w1_lo = [mem.at(f"w1_lo{j}", 198 + 4 * j, [P, KT, P], F32R) for j in range(GRP)]
    w1_raw = [mem.at(f"w1_raw{j}", 6 + 4 * j, [P, KT, P]) for j in range(GRP)]
    gain = mem.at("ln2_gain", 14, [P, D])
    bias = mem.at("ln2_bias", 18, [P, D])
    relu = [mem.at(f"relu{j}", 22 + 4 * j, [P, S]) for j in range(GRP)]
    squared = [mem.at(f"squared{j}", 30 + 4 * j, [P, S]) for j in range(GRP)]
    stats = mem.at("ln2_stats", 1, [P, TT, 2, 6])
    mean_var = mem.at("ln2_mean_var", 1.5, [P, TT, 2])
    sd = mem.at("ln2_sd", 2, [P, TT])
    eps = mem.at("ln2_eps", 2.25, [P, 1])
    flat = lambda b: ps[:, b:b + 2, :].rearrange("p b n -> p (b n)")
    with ExitStack() as ctx:
        rows_in, init, xT_ready, xhi_done, xlo_done, alpha_done, relu_done, square_done, hid_ready, out_mm, added = sems(
            nc, ctx, "g_rows_in", "g_init", "g_xT_ready", "g_xhi", "g_xlo", "g_alpha", "g_relu", "g_square",
            "g_hid_ready", "g_out_mm", "g_added")
        var_done, sd_done, scaled, normed, stored, dve_step, pool_step, w2_in, w2_whi, w2_split = sems(
            nc, ctx, "g_var", "g_sd", "g_scaled", "g_normed", "g_stored", "g_dve_step", "g_pool_step", "g_w2_in",
            "g_w2_hi", "g_w2_split")
        relu_free, = sems(nc, ctx, "g_relu_free")
        w1_in = sems(nc, ctx, "g_w1_in0", "g_w1_in1")
        w1_whi = sems(nc, ctx, "g_w1_hi0", "g_w1_hi1")
        w1_split = sems(nc, ctx, "g_w1_split0", "g_w1_split1")
        slab_mm = sems(nc, ctx, "g_slab_mm0", "g_slab_mm1")
        SLAB_FREE, OUT_FREE = GRP, 4
        block = ctx.enter_context(nc.Block())
        loops = GROUPS // 2 - 1

        @block.sync
        def _(sp):
            for j in range(GRP):
                sp.dma_start(w1_raw[j][:], t["w_ffn1"][j]).then_inc(w1_in[j], 16)
            load2 = lambda g: sp.dma_start(w2_raw[:], t["w_ffn2"][g]).then_inc(w2_in, 16)
            load2(0)
            sp.dma_start(gain[:], t["ln"][2:3, :].to_broadcast([P, D])).then_inc(rows_in, 16)
            sp.dma_start(bias[:], t["ln"][3:4, :].to_broadcast([P, D])).then_inc(rows_in, 16)
            with sp.Fori(1, GROUPS) as g:
                for j in range(GRP):
                    sp.wait_ge(w1_split[j], g)
                    sp.dma_start(w1_raw[j][:], t["w_ffn1"][GRP * g + j]).then_inc(w1_in[j], 16)
                sp.wait_ge(w2_split, g)
                load2(g)
            for tt in range(TT):
                sp.wait_ge(normed, tt + 1)
                sp.dma_start(out[0, tt * P:(tt + 1) * P, :], acc[:, tt, :]).then_inc(stored, 16)
            sp.wait_ge(stored, 16 * TT)

        @block.tensor
        def _(pe):
            for n in range(2 * KT):
                h, kt = divmod(n, KT)
                if n >= 4:
                    pe.wait_ge(xlo_done, n - 3)
                for tt in range(4):
                    last = nc.tensor.transpose(ps[:, n % 4, tt * P:(tt + 1) * P],
                                               acc[:, 4 * h + tt, kt * P:(kt + 1) * P], ident[:])
                last.then_inc(xT_ready, 1)
            pe.wait_ge(xlo_done, 2 * KT)
            pe.wait_ge(alpha_done, 1)

            def first(g):
                for j in range(GRP):
                    pe.wait_ge(w1_split[j], g + 1)
                    pe.wait_ge(relu_done, GRP * (g - 1) + j + 1 + SLAB_FREE)
                    project3(nc, [ps[:, 2 * j + b, :] for b in range(2)], w1_hi[j], w1_lo[j],
                             lambda kt, b: x_hi[:, kt, b * HALF:(b + 1) * HALF],
                             lambda kt, b: x_lo[:, kt, b * HALF:(b + 1) * HALF], KT).then_inc(slab_mm[j], 1)

            def second(g, q):
                pe.wait_ge(w2_split, g + 1)
                pe.wait_ge(hid_ready, GRP * (g + 1))
                for n in range(OUTS):
                    tt, b = divmod(n, 2)
                    tok, col = slice(tt * P, (tt + 1) * P), slice(b * HALF, (b + 1) * HALF)
                    pe.wait_ge(added, OUTS * g + n - 3 + OUT_FREE)
                    for j in range(GRP):
                        for m, (a, w) in enumerate(((hid_hi, w2_hi), (hid_hi, w2_lo), (hid_lo, w2_hi))):
                            last = nc.tensor.matmul(ps[:, 4 + n % 4, :], a[q][:, j, tok], w[:, j, col],
                                                    start=j == 0 and m == 0, stop=j == GRP - 1 and m == 2)
                    last.then_inc(out_mm, 1)

            first(0)
            with pe.Fori(0, loops) as i:
                for q in range(2):
                    first(2 * i + q + 1)
                    second(2 * i + q, q)
            first(GROUPS - 1)
            second(GROUPS - 2, 0)
            second(GROUPS - 1, 1)

        @block.scalar
        def _(act):
            A = nc.scalar.activation
            act.sem_inc(relu_done, SLAB_FREE)
            for n in range(2 * KT):
                h, kt = divmod(n, KT)
                act.wait_ge(xT_ready, n + 1)
                A(x_hi[:, kt, h * HALF:(h + 1) * HALF], ps[:, n % 4, :], ACT.Copy).then_inc(xhi_done, 1)

            def first(g, q):
                for j in range(GRP):
                    act.wait_ge(slab_mm[j], g + 1)
                    act.wait_ge(relu_free, GRP * (g - 1) + j + 1 + GRP)
                    A(relu[j][:], flat(2 * j), ACT.Relu).then_inc(relu_done, 1)
                    act.wait_ge(relu_done, GRP * g + j + 1 + SLAB_FREE)
                    A(hid_hi[q][:, j, :], relu[j][:], ACT.Square).then_inc(square_done, 1)

            first(0, 0)
            with act.Fori(0, loops) as i:
                for q in range(2):
                    first(2 * i + q + 1, 1 - q)
            first(GROUPS - 1, 1)
            act.wait_ge(init, 1)
            for tt in range(TT):
                act.wait_ge(var_done, tt + 1)
                A(sd[:, tt:tt + 1], mean_var[:, tt, 1:2], ACT.Sqrt, bias=eps[:]).then_inc(sd_done, 1)

        @block.vector
        def _(dve):
            V = nc.vector
            step = Steps(dve, dve_step)
            V.memset(eps[:], LN_EPS).then_inc(init, 1)

            def split1(g, j):
                dve.wait_ge(w1_in[j], 16 * (g + 1))
                split2(nc, dve, w1_raw[j][:], w1_hi[j][:], w1_lo[j][:], w1_whi[j], g + 1, w1_split[j])

            def first(g, q):
                for j in range(GRP):
                    dve.wait_ge(relu_done, GRP * g + j + 1 + SLAB_FREE)
                    V.tensor_tensor(squared[j][:], relu[j][:], relu[j][:], ALU.mult).then_inc(relu_free, 1)
                    dve.wait_ge(relu_free, GRP * g + j + 1 + GRP)
                    dve.wait_ge(square_done, GRP * g + j + 1)
                    V.tensor_tensor(hid_lo[q][:, j, :], squared[j][:], hid_hi[q][:, j, :].bitcast(F32), ALU.subtract)\
                        .then_inc(hid_ready, 1)
                    yield j

            def split_second(g):
                dve.wait_ge(w2_in, 16 * (g + 1))
                split2(nc, dve, w2_raw[:], w2_hi[:], w2_lo[:], w2_whi, g + 1, w2_split)

            def add(g, n):
                tt, b = divmod(n, 2)
                piece = acc[:, tt, b * HALF:(b + 1) * HALF]
                dve.wait_ge(out_mm, OUTS * g + n + 1)
                return V.tensor_tensor(piece, ps[:, 4 + n % 4, :], piece, ALU.add).then_inc(added, 1)

            def stage(g, q, more, ahead):
                if more:
                    for j in first(g + 1, 1 - q):
                        if ahead:
                            split1(g + 2, j)
                for n in range(OUTS):
                    add(g, n)
                if more:
                    split_second(g + 1)

            dve.sem_inc(relu_free, GRP)
            for j in range(GRP):
                split1(0, j)
            for n in range(2 * KT):
                h, kt = divmod(n, KT)
                cut = slice(h * HALF, (h + 1) * HALF)
                dve.wait_ge(xhi_done, n + 1)
                V.tensor_tensor(x_lo[:, kt, cut], ps[:, n % 4, :], x_hi[:, kt, cut].bitcast(F32), ALU.subtract)\
                    .then_inc(xlo_done, 1)
            dve.wait_ge(xT_ready, 2 * KT)
            V.tensor_scalar(acc[:], acc[:], ALPHA, None, ALU.mult).then_inc(alpha_done, 1)
            dve.sem_inc(added, OUT_FREE)
            split_second(0)
            for j in first(0, 0):
                split1(1, j)
            with dve.Fori(0, loops) as i:
                for q in range(2):
                    stage(2 * i + q, q, True, True)
            stage(GROUPS - 2, 0, True, False)

            def normalise(tt):
                dve.wait_ge(sd_done, tt + 1)
                step.mark(V.reciprocal(sd[:, tt:tt + 1], sd[:, tt:tt + 1]))
                step.wait()
                V.tensor_scalar(acc[:, tt, :], acc[:, tt, :], mean_var[:, tt, 0:1], sd[:, tt:tt + 1],
                                ALU.subtract, ALU.mult).then_inc(scaled, 1)

            for tt in range(TT):
                for b in range(2):
                    add(GROUPS - 1, 2 * tt + b)
                dve.wait_ge(added, OUTS * (GROUPS - 1) + 2 * tt + 2 + OUT_FREE)
                layer_norm_stats(nc, dve, step, acc[:, tt, :], stats[:, tt, :, :], mean_var[:, tt, :]).then_inc(var_done, 1)
                if tt:
                    normalise(tt - 1)
            normalise(TT - 1)

        @block.gpsimd
        def _(pool):
            G = nc.gpsimd
            step = Steps(pool, pool_step)
            pool.wait_ge(rows_in, 32)
            for tt in range(TT):
                pool.wait_ge(scaled, tt + 1)
                step.mark(G.tensor_tensor(acc[:, tt, :], acc[:, tt, :], gain[:], ALU.mult))
                step.wait()
                G.tensor_tensor(acc[:, tt, :], acc[:, tt, :], bias[:], ALU.add).then_inc(normed, 1)


def build(nc, t, out, debug=None):
    mem = Memory(nc)

    class K:
        pass

    k = K()
    k.ident = mem.at("ident", 0, [P, P])
    k.cols = mem.at("cols", 0.5, [P, NCOLS])
    k.keep = mem.at("keep", 0.75, [P, SLABS])
    k.hT = mem.at("hT", 38, [P, SLABS, S])
    k.ym_hi = mem.at("ym_hi", 6, [P, RT, S], F32R)
    k.ym_lo = mem.at("ym_lo", 22, [P, RT, S], F32R)
    k.beta = mem.at("beta", 159, [P, RT, S])
    k.cum = mem.at("cum", 175, [P, RT, S])
    k.kk = mem.at("kk", 191, [P, RT, S])
    k.yr_hi = mem.at("yr_hi", 94, [P, RT, S], F32R)
    k.yr_lo = mem.at("yr_lo", 110, [P, RT, S], F32R)
    k.ones_block = mem.at("ones_block", 1, [P, P])
    k.chunk_mask = mem.at("chunk_mask", 1.5, [P, P])
    k.gate = mem.at("gate", 2, [P, RW])
    k.one = mem.at("one", 4, [P, 8])
    k.merge = mem.at("merge", 153, [P, 12, P], I32)
    k.x1 = mem.at("x1", 38, [P, TT, D])
    k.d_ident, k.d_cols = t["ident"], t["cols"]
    with ExitStack() as ctx:
        k.ps = ctx.enter_context(nc.psum_tensor("banks", [P, 8, HALF], F32))
        project_in(nc, mem, k, t["x"], t["w_in"])
        mla(nc, mem, k, t)
        rwkv_inputs(nc, mem, k, t)
        rwkv_chunks(nc, mem, k)
        rwkv_outputs(nc, mem, k)
        mix_out(nc, mem, k, t)
        ffn(nc, mem, k, t, out)


def lay_out(i):
    columns = lambda a: a.reshape(-1, P).T
    swap = np.r_[ROPE // 2:ROPE, 0:ROPE // 2]

    w_in = i["w_in"][0]
    main, pe = w_in[:, :T_PE * P], w_in[:, T_PE * P:]
    last = np.concatenate([np.zeros((D, HD), np.float32), pe, pe[:, swap]], axis=1)
    w_in = np.concatenate([main, last], axis=1)
    w_in = w_in.reshape(KT, P, SLABS, P).transpose(2, 1, 0, 3)

    w_uq = i["w_uq"][0].reshape(QLT, P, NH, HD + ROPE)
    w_uq = np.concatenate([w_uq, w_uq[..., HD + swap]], axis=-1).transpose(2, 1, 0, 3)
    w_ukv = i["w_ukv"][0].reshape(KVLT, P, NH, 2 * HD).transpose(2, 1, 0, 3)

    freq = (np.float32(10000.0) ** (-np.arange(0, ROPE, 2, dtype=np.float32) / ROPE)).astype(np.float32)
    rotary = np.zeros((P, 2), np.float32)
    rotary[HD:, 0] = np.tile(freq, 4)
    rotary[HD:, 1] = np.tile(np.repeat([-1.0, 1.0], ROPE // 2), 2)
    cols = np.concatenate([
        columns(i["shift_mu"][0]), np.zeros((P, SLABS - T_CQ), np.float32)]
        + [columns(i[n][0].reshape(-1)) for n in ("decay_w0", "iclr_a0", "k_k", "k_a", "r_k", "lnx_g", "lnx_b",
                                                  "q_norm_g", "kv_norm_g")] + [rotary], axis=1)

    row, col = np.arange(P)[:, None], np.arange(P)[None, :]
    rc, cc = row % CH, col % CH
    same = (row // CH) == (col // CH)
    chunk_mask = np.where(col < CH, rc < cc, rc <= cc).astype(np.float32)
    merge = [(same & (rc // b % 2 == 1) & (cc // b == rc // b - 1)) for b in (1, 2, 4, 8, 16, 32)]
    merge = np.stack([m for mm in merge for m in (mm, mm.T)], axis=1).astype(np.int32)
    return {
        "x": i["x"], "positions": i["positions"], "w_in": w_in, "cols": cols,
        "ident": np.eye(P, dtype=np.float32), "ones_block": same.astype(np.float32),
        "causal": np.where(row > col, NEG, 0.0).astype(np.float32),
        "chunk_mask": chunk_mask, "merge": merge,
        "w_uq": w_uq, "w_ukv": w_ukv,
        "w_lora": np.concatenate([i["decay_w2"][0], i["iclr_a2"][0]], axis=0), "gate_g2": i["gate_g2"][0],
        "w_out": i["w_out"][0].reshape(KT, P, D),
        "w_ffn1": i["w_ffn1"][0].reshape(KT, P, DFF // P, P).transpose(2, 1, 0, 3),
        "w_ffn2": i["w_ffn2"][0].reshape(DFF // (2 * P), 2, P, D).transpose(0, 2, 1, 3),
        "ln": np.stack([i[n][0] for n in ("ln1_g", "ln1_b", "ln2_g", "ln2_b")]),
    }


def kernel(**inputs):
    import concourse.bacc as bacc
    from concourse.bass_utils import run_bass_kernel_spmd as run

    nc = bacc.Bacc("TRN2", target_bir_lowering=False, num_devices=1)
    arrays, args = {}, {}
    for name, a in lay_out({n: np.asarray(a) for n, a in inputs.items()}).items():
        arrays[f"in_{name}"] = a = np.ascontiguousarray(a)
        args[name] = nc.dram_tensor(f"in_{name}", a.shape, mybir.dt.from_np(a.dtype), kind="ExternalInput").ap()
    out = nc.dram_tensor("layer_out", OUT_SHAPE, F32, kind="ExternalOutput").ap()
    build(nc, args, out)
    return run(nc, [arrays], core_ids=[0]).results[0]["layer_out"]
```

```python
from contextlib import ExitStack

import numpy as np

import concourse.bass as bass
from concourse import mybir

ALU = mybir.AluOpType
ACT = mybir.ActivationFunctionType
F32 = mybir.dt.float32
F32R = mybir.dt.float32r
I32 = mybir.dt.int32
AX_X = mybir.AxisListType.X

P = 128
D = 1024
S = 1024
KT = D // P
TT = S // P
HALF = 512
NH = 8
HD = 64
ROPE = 32
RW = NH * HD
RT = RW // P
QL, KVL = 384, 256
QLT, KVLT = QL // P, KVL // P
SLABS = 20
T_R, T_K, T_V, T_WA, T_G, T_CQ, T_CKV, T_PE = 0, 4, 8, 12, 13, 14, 17, 19
DFF = 4096
ALPHA = 2.0 ** 0.25
LN_EPS, RMS_EPS, GN_EPS = 1e-5, 1e-6, 64e-5
CH = 64
NC_ = S // CH
EXP_M05 = float(np.exp(-0.5))
SCALE = float((HD + ROPE) ** -0.5)
NEG = -1.0e30

C_MU = 0
C_W0 = C_MU + SLABS
C_A0 = C_W0 + RT
C_KK = C_A0 + RT
C_KA = C_KK + RT
C_RK = C_KA + RT
C_LG = C_RK + RT
C_LB = C_LG + RT
C_QG = C_LB + RT
C_KVG = C_QG + QLT
C_FREQ = C_KVG + KVLT
C_SIGN = C_FREQ + 1
C_ROT = C_SIGN + 1
NCOLS = C_ROT

KB = 1024
BASE = 16512


OUT_SHAPE = (1, S, D)


class Steps:

    def __init__(self, sem):
        self.sem, self.base, self.n = sem, 0, 0

    def on(self, eng):
        self.eng, self.base, self.n = eng, self.base + self.n, 0
        return self

    def mark(self, ins):
        ins.then_inc(self.sem, 1)
        self.n += 1
        return self.n

    def wait(self, n=None):
        self.eng.wait_ge(self.sem, self.base + (self.n if n is None else n))

    def enter(self, trip, per):
        self.start, self.per = self.base + self.n, per
        self.base, self.n = self.start + trip * per, 0

    def leave(self, trips):
        assert self.n == self.per, f"the body marks {self.n} steps"
        self.base, self.n = self.start + trips * self.per, 0


class Memory:

    def __init__(self, nc):
        self.nc = nc

    def at(self, name, kb, shape, dtype=F32):
        return self.nc.alloc_sbuf_tensor_at(name, shape, dtype, offset=BASE + int(kb * KB))


def sems(nc, ctx, *names):
    return [ctx.enter_context(nc.semaphore(n)) for n in names]


def project3(nc, outs, w_hi, w_lo, r_hi, r_lo, tiles):
    for kt in range(tiles):
        for n, (w, r) in enumerate(((w_hi, r_hi), (w_hi, r_lo), (w_lo, r_hi))):
            for b, out in enumerate(outs):
                last = nc.tensor.matmul(out, w[:, kt, :], r(kt, b), start=kt == 0 and n == 0,
                                        stop=kt == tiles - 1 and n == 2)
    return last


def split2(nc, dve, raw, hi, lo, hi_sem, count, lo_sem):
    nc.vector.tensor_copy(hi, raw).then_inc(hi_sem, 1)
    dve.wait_ge(hi_sem, count)
    nc.vector.tensor_tensor(lo, raw, hi.bitcast(F32), ALU.subtract).then_inc(lo_sem, 1)


def clear_released(nc):
    numbers = sorted(nc.released_uncleared_semaphores)
    runs = [i for i in range(len(numbers)) if i == 0 or numbers[i] != numbers[i - 1] + 1] + [len(numbers)]
    with nc.Block() as block:

        @block.sync
        def _(sp):
            for a, b in zip(runs, runs[1:]):
                sp.sem_clear(range(numbers[a], numbers[b - 1] + 1))


def project_in(nc, mem, k, x, w_in, positions):
    x_tok = mem.at("x_tok", 38 + 48, [P, TT, D])
    x_hi = mem.at("xT_hi", 118, [P, KT, S], F32R)
    x_lo = mem.at("xT_lo", 150, [P, KT, S], F32R)
    w_raw = [mem.at(f"win_raw{j}", 182 + 4 * j, [P, KT, P]) for j in range(2)]
    w_hi = [mem.at(f"win_hi{j}", 190 + 4 * j, [P, KT, P], F32R) for j in range(2)]
    w_lo = [mem.at(f"win_lo{j}", 198 + 4 * j, [P, KT, P], F32R) for j in range(2)]
    hT, cols, ident, ps = k.hT, k.cols, k.ident, k.ps
    keep = k.keep
    trips = SLABS // 2
    first = T_CQ // 2
    early = trips - first
    ones, trig, key_rot = k.ones, k.trig_in, k.key_rot
    square = mem.at("latent_square", 14, [P, QLT, S])
    root = [mem.at(f"latent_root{n}", 26 + 4 * n, [P, S]) for n in range(2)]
    turns = mem.at("turns", 34, [P, S])
    pos = mem.at("positions", 10, [P, S], I32)
    rms_eps = mem.at("rms_eps", 3.25, [P, 1])
    LATENTS = ((T_CQ, QLT, C_QG, QL), (T_CKV, KVLT, C_KVG, KVL))
    pe32, sw32, rot64 = slice(64, 96), slice(96, 128), slice(64, 128)
    PI2 = 2 * np.pi
    C1 = 6.28125
    C2 = float(np.float32(round((PI2 - C1) * 2 ** 20) / 2 ** 20))
    C3 = float(np.float32(PI2 - C1 - C2))
    MAGIC = 1.5 * 2.0 ** 23
    PI_BELOW = 3.1415925
    with ExitStack() as ctx:
        consts_in, x_in0, x_in1, xT_ready, xhi_done, xlo_done, keep_done = sems(
            nc, ctx, "a_consts_in", "a_x_in0", "a_x_in1", "a_xT_ready", "a_xhi_done", "a_xlo_done", "a_keep_done")
        w_in_sem = sems(nc, ctx, "a_w_loaded0", "a_w_loaded1")
        w_split = sems(nc, ctx, "a_w_split0", "a_w_split1")
        w_whi = sems(nc, ctx, "a_w_hi0", "a_w_hi1")
        slab_mm = sems(nc, ctx, "a_slab_mm0", "a_slab_mm1")
        h_scaled = sems(nc, ctx, "a_h_scaled0", "a_h_scaled1")
        h_mixed = sems(nc, ctx, "a_h_mixed0", "a_h_mixed1")
        pos_in, init, squared, summed, sum_mm, rooted, sin_in, sin_out = sems(
            nc, ctx, "a_pos_in", "a_init", "a_squared", "a_summed", "a_sum_mm", "a_rooted", "a_sin_in", "a_sin_out")
        block = ctx.enter_context(nc.Block())


        @block.sync
        def _(sp):
            sp.dma_start(ident[:], k.d_ident).then_inc(consts_in, 16)
            sp.dma_start(cols[:], k.d_cols).then_inc(consts_in, 16)
            xt = x.rearrange("o (t p) d -> p (o t) d", p=P)
            for g, sem in enumerate((x_in0, x_in1)):
                sp.dma_start(x_tok[:, 4 * g:4 * g + 4, :], xt[:, 4 * g:4 * g + 4, :]).then_inc(sem, 16)
            for j in range(2):
                sp.dma_start(w_raw[j][:], w_in[2 * first + j]).then_inc(w_in_sem[j], 16)
            sp.dma_start(pos[:], positions.to_broadcast([P, S])).then_inc(pos_in, 16)

            def load(i, trip):
                for j in range(2):
                    sp.wait_ge(w_split[j], trip)
                    sp.dma_start(w_raw[j][:], w_in[2 * i + j]).then_inc(w_in_sem[j], 16)

            with sp.Fori(first + 1, trips) as i:
                load(i, i - first)
            with sp.Fori(0, first) as i:
                load(i, i + early)

        @block.tensor
        def _(pe):
            pe.wait_ge(consts_in, 32)
            for g in range(2):
                pe.wait_ge((x_in0, x_in1)[g], 16)
                for kt in range(KT):
                    n = g * KT + kt
                    if n >= 4:
                        pe.wait_ge(xlo_done, n - 3)
                    for t in range(4):
                        last = nc.tensor.transpose(ps[:, n % 4, t * P:(t + 1) * P],
                                                   x_tok[:, 4 * g + t, kt * P:(kt + 1) * P], ident[:])
                    last.then_inc(xT_ready, 1)
            pe.wait_ge(xlo_done, 2 * KT)
            pe.wait_ge(xhi_done, 2 * KT)

            def pair(i, trip):
                for j in range(2):
                    pe.wait_ge(w_split[j], trip + 1)
                    last = project3(nc, [ps[:, 2 * j + b, :] for b in range(2)], w_hi[j], w_lo[j],
                                    lambda kt, b: x_hi[:, kt, b * HALF:(b + 1) * HALF],
                                    lambda kt, b: x_lo[:, kt, b * HALF:(b + 1) * HALF], KT)
                    last.then_inc(slab_mm[j], 1)

            with pe.Fori(first, trips) as i:
                pair(i, i - first)
            with pe.Fori(0, 2) as i:
                pair(i, i + early)
            pe.wait_ge(init, 1)
            for n in range(2):
                pe.wait_ge(summed, n + 1)
                for b in range(2):
                    last = nc.tensor.matmul(ps[:, 4 + 2 * n + b, :], ones[:],
                                            square[:, n, b * HALF:(b + 1) * HALF], start=True, stop=True)
                last.then_inc(sum_mm, 1)
            with pe.Fori(2, first) as i:
                pair(i, i + early)

        @block.scalar
        def _(act):
            for n in range(2 * KT):
                g, kt = divmod(n, KT)
                act.wait_ge(xT_ready, n + 1)
                nc.scalar.activation(x_hi[:, kt, g * HALF:(g + 1) * HALF], ps[:, n % 4, :], ACT.Copy)\
                    .then_inc(xhi_done, 1)
            act.wait_ge(keep_done, 1)

            def pair(i, trip):
                for j in range(2):
                    act.wait_ge(slab_mm[j], trip + 1)
                    nc.scalar.activation(hT[:, 2 * i + j, :], ps[:, 2 * j:2 * j + 2, :].rearrange("p b n -> p (b n)"),
                                         ACT.Identity, scale=keep[:, bass.ds(2 * i + j, 1)]).then_inc(h_scaled[j], 1)

            with act.Fori(first, trips) as i:
                pair(i, i - first)
            for n, (tile0, tiles, _, _) in enumerate(LATENTS):
                if n == 0:
                    for j in range(2):
                        act.wait_ge(h_mixed[j], early)
                else:
                    act.wait_ge(summed, 1)
                nc.scalar.activation(square[:, n:n + tiles, :], hT[:, tile0:tile0 + tiles, :], ACT.Square)\
                    .then_inc(squared, 1)
            with act.Fori(0, 2) as i:
                pair(i, i + early)
            act.wait_ge(sin_in, 1)
            nc.scalar.activation(trig[rot64, :], trig[rot64, :], ACT.Sin).then_inc(sin_out, 1)
            pair(2, 2 + early)
            for n, (_, _, _, width) in enumerate(LATENTS):
                act.wait_ge(sum_mm, n + 1)
                act.wait_ge(init, 2)
                nc.scalar.activation(root[n][:], ps[:, 4 + 2 * n:6 + 2 * n, :].rearrange("p b n -> p (b n)"), ACT.Sqrt,
                                     scale=1.0 / width, bias=rms_eps[:]).then_inc(rooted, 1)
            with act.Fori(3, first) as i:
                pair(i, i + early)

        @block.vector
        def _(dve):
            step = k.dve_steps.on(dve)
            nc.vector.memset(ones[:], 1.0).then_inc(init, 1)
            nc.vector.memset(rms_eps[:], RMS_EPS).then_inc(init, 1)
            dve.wait_ge(consts_in, 32)
            nc.vector.tensor_scalar(keep[:], cols[:, C_MU:C_MU + SLABS], -1.0, 1.0, ALU.mult, ALU.add)\
                .then_inc(keep_done, 1)
            for n in range(2 * KT):
                g, kt = divmod(n, KT)
                cut = slice(g * HALF, (g + 1) * HALF)
                dve.wait_ge(xhi_done, n + 1)
                nc.vector.tensor_tensor(x_lo[:, kt, cut], ps[:, n % 4, :], x_hi[:, kt, cut].bitcast(F32), ALU.subtract)\
                    .then_inc(xlo_done, 1)

            def split(j, trip):
                dve.wait_ge(w_in_sem[j], 16 * (trip + 1))
                split2(nc, dve, w_raw[j][:], w_hi[j][:], w_lo[j][:], w_whi[j], trip + 1, w_split[j])

            def mix(j, i, trip):
                dve.wait_ge(h_scaled[j], trip + 1)
                flat = ps[:, 2 * j:2 * j + 2, :].rearrange("p b n -> p (b n)")
                nc.vector.scalar_tensor_tensor(hT[:, 2 * i + j, 1:S], flat[:, 0:S - 1],
                                               cols[:, bass.ds(C_MU + 2 * i + j, 1)], hT[:, 2 * i + j, 1:S],
                                               ALU.mult, ALU.add).then_inc(h_mixed[j], 1)

            def pair(i, trip):
                for j in range(2):
                    mix(j, i, trip)
                    split(j, trip + 1)

            def angles():
                dve.wait_ge(pos_in, 16)
                V, col = nc.vector, lambda c: cols[rot64, c:c + 1]
                a, u = trig[rot64, :], turns[rot64, :]
                step.mark(V.tensor_copy(a, pos[rot64, :]))
                step.wait()
                step.mark(V.tensor_scalar(a, a, col(C_FREQ), None, ALU.mult))
                step.wait()
                step.mark(V.tensor_scalar(u, a, 1.0 / PI2, MAGIC, ALU.mult, ALU.add))
                step.wait()
                step.mark(V.tensor_scalar(u, u, MAGIC, None, ALU.subtract))
                for c in (C1, C2, C3):
                    step.wait()
                    step.mark(V.scalar_tensor_tensor(a, u, -c, a, ALU.mult, ALU.add))
                step.wait()
                step.mark(V.tensor_scalar(a, a, PI_BELOW, -PI_BELOW, ALU.min, ALU.max))
                step.wait()
                step.mark(V.scalar_tensor_tensor(turns[pe32, :], trig[pe32, :], -1.0, trig[pe32, :], ALU.mult, ALU.max))
                step.wait()
                V.tensor_scalar(trig[pe32, :], turns[pe32, :], -1.0, float(np.pi / 2), ALU.mult, ALU.add)\
                    .then_inc(sin_in, 1)

            def add_squares():
                for j in range(2):
                    dve.wait_ge(h_mixed[j], early)
                for n, (_, tiles, _, _) in enumerate(LATENTS):
                    dve.wait_ge(squared, n + 1)
                    for c in range(1, tiles):
                        if c > 1:
                            step.wait()
                        ins = nc.vector.tensor_tensor(square[:, n, :], square[:, n, :], square[:, n + c, :], ALU.add)
                        if c < tiles - 1:
                            step.mark(ins)
                    ins.then_inc(summed, 1)

            def rotate_key():
                V = nc.vector
                dve.wait_ge(sin_out, 1)
                step.mark(V.tensor_scalar(trig[rot64, :], trig[rot64, :], cols[rot64, C_SIGN:C_SIGN + 1], None, ALU.mult))
                step.wait()
                step.mark(V.tensor_tensor(key_rot[pe32, :], hT[pe32, T_PE, :], trig[pe32, :], ALU.mult))
                step.mark(V.tensor_tensor(turns[pe32, :], hT[sw32, T_PE, :], trig[sw32, :], ALU.mult))
                step.wait()
                V.tensor_tensor(key_rot[pe32, :], key_rot[pe32, :], turns[pe32, :], ALU.add)

            def invert(n):
                dve.wait_ge(rooted, n + 1)
                step.mark(nc.vector.reciprocal(root[n][:], root[n][:]))

            def normalise(n):
                tile0, tiles, gain, _ = LATENTS[n]
                for c in range(tiles):
                    nc.vector.scalar_tensor_tensor(hT[:, tile0 + c, :], hT[:, tile0 + c, :],
                                                   cols[:, gain + c:gain + c + 1], root[n][:], ALU.mult, ALU.mult)

            for j in range(2):
                split(j, 0)
            with dve.Fori(first, trips) as i:
                pair(i, i - first)
            add_squares()
            for a, b, extra in ((0, 1, angles), (1, 2, rotate_key), (2, 4, lambda: invert(0)),
                                (4, 5, lambda: (step.wait(), normalise(0), invert(1))),
                                (5, 6, lambda: (step.wait(), normalise(1)))):
                with dve.Fori(a, b) as i:
                    pair(i, i + early)
                extra()
            for j in range(2):
                mix(j, first - 1, trips - 1)


def mla(nc, mem, k, t):
    hT, cols, ident, ps = k.hT, k.cols, k.ident, k.ps
    ym_hi, ym_lo = k.ym_hi, k.ym_lo
    trig = mem.at("trig", 118, [P, S])
    q_hi = [mem.at(f"q_hi{p}", 126 + 4 * p, [P, S], F32R) for p in range(2)]
    q_lo = [mem.at(f"q_lo{p}", 134 + 4 * p, [P, S], F32R) for p in range(2)]
    k_hi = [mem.at(f"k_hi{p}", 142 + 4 * p, [P, S], F32R) for p in range(2)]
    k_lo = [mem.at(f"k_lo{p}", 150 + 4 * p, [P, S], F32R) for p in range(2)]
    v_one = [mem.at(f"v_one{p}", 158 + 4 * p, [P, TT, P]) for p in range(2)]
    probs = [mem.at(f"probs{n}", 166 + 4 * n, [P, S]) for n in range(3)]
    w_uq = [mem.at(f"w_uq{p}", 178 + 1.5 * p, [P, QLT, P]) for p in range(2)]
    w_ukv = [mem.at(f"w_ukv{p}", 181 + p, [P, KVLT, P]) for p in range(2)]
    rot_a = mem.at("rot_a", 183, [P, S])
    rot_b = mem.at("rot_b", 187, [P, S])
    recip = mem.at("att_recip", 191, [P, S])
    y_full = mem.at("att_y", 195, [P, S])
    att = mem.at("att_sums", 199, [P, S])
    ones = k.ones
    causal = mem.at("causal", 1.5, [P, P])
    causal_r = mem.at("causal_r", 2, [P, P], F32R)
    ident_r = mem.at("ident_r", 2.5, [P, P], F32R)
    top = mem.at("row_max", 3, [P, TT])
    top_r = mem.at("neg_row_max_r", 3.125, [P, TT], F32R)
    A, O = (0, 1), (6, 7)
    T = ((2, 3), (4, 5))
    flat = lambda pair, rows=slice(0, P): ps[rows, pair[0]:pair[0] + 2, :].rearrange("p b n -> p (b n)")
    lo64, hi64, pe32, sw32 = slice(0, 64), slice(64, 128), slice(64, 96), slice(96, 128)
    ONE = slice(96, 97)
    ITEMS = 12
    FREES = ITEMS - 1
    TURNS = {0: ("q", None), 1: (None, "k"), 2: ("v", None), 3: (7, 6), 4: (5, 4), 5: (3, 2), 6: (1, 0), 7: ("m", None)}
    S_ORDER = [x for j in sorted(TURNS) for x in TURNS[j] if type(x) is int]

    with ExitStack() as ctx:
        in_sem, trig_ready, key_ready, causal_rr, ones_set = sems(
            nc, ctx, "b_in", "b_trig_ready", "b_key_ready", "b_causal_r", "b_ones_set")
        w_in = sems(nc, ctx, "b_w_in0", "b_w_in1")
        item, a_free, q_hi_done, k_hi_done, rot_ready, q_ready, m_ready, row_ready = sems(
            nc, ctx, "b_item", "b_a_free", "b_q_hi_done", "b_k_hi_done", "b_rot_ready", "b_q_ready",
            "b_m_ready", "b_row_ready")
        st_ready, exp_done, pv_done, o_read, y_ready, y_done = sems(
            nc, ctx, "b_st_ready", "b_exp_done", "b_pv_done", "b_o_read", "b_y_ready", "b_y_done")
        T_FREE, PROBS_FREE, O_FREE, ATT_FREE, Y_FREE = 2, 3, 1, 1, 2
        block = ctx.enter_context(nc.Block())

        @block.sync
        def _(sp):
            sp.dma_start(causal[:], t["causal"]).then_inc(in_sem, 16)

            def load(h, p):
                sp.dma_start(w_uq[p][:], t["w_uq"][h]).then_inc(w_in[p], 16)
                sp.dma_start(w_ukv[p][:], t["w_ukv"][h]).then_inc(w_in[p], 16)

            load(0, 0)
            load(1, 1)
            with sp.Fori(1, NH // 2) as i:
                for p in range(2):
                    sp.wait_ge(item, ITEMS * (2 * i + p - 2) + 3)
                    load(2 * i + p, p)

        @block.tensor
        def _(pe):
            pe.sem_inc(pv_done, PROBS_FREE)

            def take(h, n):
                pe.wait_ge(a_free, FREES * h + n)

            def q_item(h, p, i, first):
                pe.wait_ge(w_in[p], 32 * (i + 1))
                if not first:
                    take(h, 0)
                for b in range(2):
                    for c in range(QLT):
                        last = nc.tensor.matmul(ps[:, b, :], w_uq[p][:, c, :],
                                                hT[:, T_CQ + c, b * HALF:(b + 1) * HALF],
                                                start=c == 0, stop=c == QLT - 1)
                last.then_inc(item, 1)

            def k_item(h, p):
                take(h, 1)
                for b in range(2):
                    for c in range(KVLT):
                        last = nc.tensor.matmul(ps[lo64, b, :], w_ukv[p][:, c, 0:HD],
                                                hT[:, T_CKV + c, b * HALF:(b + 1) * HALF],
                                                start=c == 0, stop=c == KVLT - 1)
                last.then_inc(item, 1)

            def v_item(h, p):
                take(h, 2)
                for tt in range(TT):
                    for c in range(KVLT):
                        last = nc.tensor.matmul(ps[:, 0, tt * HD:(tt + 1) * HD],
                                                hT[:, T_CKV + c, tt * P:(tt + 1) * P], w_ukv[p][:, c, HD:2 * HD],
                                                start=c == 0, stop=c == KVLT - 1)
                last.then_inc(item, 1)

            def s_item(h, p, qt):
                n = S_ORDER.index(qt)
                take(h, 3 + n)
                if n == 0:
                    pe.wait_ge(q_ready, h + 1)
                q = q_hi[p][0:96, qt * P:(qt + 1) * P]
                for c in range(0, (qt + 1) * P, HALF):
                    end = min(c + HALF, (qt + 1) * P)
                    nc.tensor.matmul(ps[:, c // HALF, 0:end - c], q, k_hi[p][0:96, c:end], start=True,
                                     stop=end < (qt + 1) * P)
                at = qt * P % HALF
                nc.tensor.matmul(ps[:, qt * P // HALF, at:at + P], causal_r[:], ident_r[:],
                                 start=False, stop=True).then_inc(item, 1)

            def m_item(h):
                take(h, 11)
                pe.wait_ge(m_ready, h + 1)
                for qt in range(TT):
                    last = nc.tensor.matmul(ps[0:1, qt // 4, qt % 4 * P:(qt % 4 + 1) * P], top_r[:, qt:qt + 1],
                                            ident_r[:], start=True, stop=True)
                last.then_inc(item, 1)

            def st(h, p, kt):
                g = kt % 2
                pe.wait_ge(exp_done, TT * h + kt - 1 + T_FREE)
                if kt == 0:
                    pe.wait_ge(row_ready, h + 1)
                for b in range(2):
                    lo = max(kt * P, b * HALF)
                    if lo >= (b + 1) * HALF:
                        continue
                    out = ps[:, T[g][b], lo - b * HALF:HALF]
                    q = slice(lo, (b + 1) * HALF)
                    keys = slice(kt * P, (kt + 1) * P)
                    diag = lo == kt * P
                    for n, (kk, qq) in enumerate(((k_hi, q_hi), (k_hi, q_lo), (k_lo, q_hi))):
                        last = nc.tensor.matmul(out, kk[p][0:97, keys], qq[p][0:97, q], start=n == 0,
                                                stop=n == 2 and not diag)
                    if diag:
                        last = nc.tensor.matmul(out[:, 0:P], ident_r[:], causal_r[:], start=False, stop=True)
                last.then_inc(st_ready, 1)

            def pv(h, p, kt):
                pe.wait_ge(exp_done, TT * h + kt + 1 + T_FREE)
                if kt == 0:
                    pe.wait_ge(o_read, h + O_FREE)
                for b in range(2):
                    lo = max(kt * P, b * HALF)
                    if lo >= (b + 1) * HALF:
                        continue
                    last = nc.tensor.matmul(ps[:, O[b], lo - b * HALF:HALF], v_one[p][:, kt, :],
                                            probs[kt % 3][:, lo:(b + 1) * HALF], start=kt == 0,
                                            stop=kt == (3, 7)[b])
                last.then_inc(pv_done, 1)

            def sweep(h, p, i, more):
                def turn(what):
                    nh, np_ = h + 1, 1 - p
                    if what is None or not more:
                        return
                    if what == "q":
                        q_item(nh, np_, i + p, False)
                    elif what == "k":
                        k_item(nh, np_)
                    elif what == "v":
                        v_item(nh, np_)
                    elif what == "m":
                        m_item(nh)
                    else:
                        s_item(nh, np_, what)

                for kt in range(TT):
                    st(h, p, kt)
                    turn(TURNS[kt][0])
                    if kt >= 1:
                        pv(h, p, kt - 1)
                    turn(TURNS[kt][1])
                pv(h, p, TT - 1)

            q_item(0, 0, 0, True)
            k_item(0, 0)
            v_item(0, 0)
            pe.wait_ge(causal_rr, 2)
            pe.wait_ge(key_ready, 1)
            for qt in S_ORDER:
                s_item(0, 0, qt)
            m_item(0)
            pe.wait_ge(ones_set, 1)
            with pe.Fori(0, NH // 2 - 1) as i:
                for p in range(2):
                    sweep(2 * i + p, p, i, True)
            sweep(NH - 2, 0, NH // 2 - 1, True)
            sweep(NH - 1, 1, NH // 2 - 1, False)

        @block.scalar
        def _(act):
            def front(h, p, n):
                if n == 0:
                    act.wait_ge(item, ITEMS * h + 1)
                    nc.scalar.activation(q_hi[p][lo64, :], flat(A, lo64), ACT.Copy).then_inc(q_hi_done, 1)
                if n == 1:
                    act.wait_ge(item, ITEMS * h + 2)
                    nc.scalar.activation(k_hi[p][lo64, :], flat(A, lo64), ACT.Copy).then_inc(k_hi_done, 1)
                if n == 2:
                    act.wait_ge(item, ITEMS * h + 3)
                    nc.scalar.activation(v_one[p][:, :, 0:HD], ps[:, 0, :].rearrange("p (t d) -> p t d", d=HD),
                                         ACT.Copy).then_inc(a_free, 1)
                if n == 3:
                    act.wait_ge(item, ITEMS * h + 12)
                    nc.scalar.activation(q_hi[p][ONE, :], flat(A, slice(0, 1)), ACT.Copy).then_inc(row_ready, 1)

            def sweep(h, p, more):
                for kt in range(TT):
                    act.wait_ge(st_ready, TT * h + kt + 1)
                    act.wait_ge(pv_done, TT * h + kt - 2 + PROBS_FREE)
                    nc.scalar.activation(probs[kt % 3][:, kt * P:S], flat(T[kt % 2])[:, kt * P:S], ACT.Exp,
                                         scale=SCALE).then_inc(exp_done, 1)
                    if more and kt == 0:
                        front(h + 1, 1 - p, 0)
                    if more and kt == 1:
                        front(h + 1, 1 - p, 1)
                    if more and kt == 2:
                        front(h + 1, 1 - p, 2)
                if more:
                    front(h + 1, 1 - p, 3)
                act.wait_ge(pv_done, TT * (h + 1) + PROBS_FREE)
                act.wait_ge(y_ready, h + ATT_FREE)
                nc.scalar.activation(att[:], flat(O), ACT.Copy).then_inc(o_read, 1)

            act.sem_inc(exp_done, T_FREE)
            for n in range(4):
                front(0, 0, n)
            with act.Fori(0, NH // 2 - 1) as i:
                for p in range(2):
                    sweep(2 * i + p, p, True)
            sweep(NH - 2, 0, True)
            sweep(NH - 1, 1, False)

        @block.vector
        def _(dve):
            step = k.dve_steps.on(dve)
            V = nc.vector
            for p in range(2):
                step.mark(V.tensor_copy(k_hi[p][pe32, :], k.key_rot[pe32, :]))
            step.wait()
            for p in range(2):
                last = V.tensor_tensor(k_lo[p][pe32, :], k.key_rot[pe32, :], k_hi[p][pe32, :].bitcast(F32), ALU.subtract)
            last.then_inc(key_ready, 1)
            dve.wait_ge(in_sem, 16)
            V.tensor_copy(causal_r[:], causal[:]).then_inc(causal_rr, 1)
            V.tensor_copy(ident_r[:], ident[:]).then_inc(causal_rr, 1)

            def front_q(h, p, first=False):
                dve.wait_ge(q_hi_done, h + 1)
                V.tensor_tensor(q_lo[p][lo64, :], flat(A, lo64), q_hi[p][lo64, :].bitcast(F32), ALU.subtract)
                if first:
                    dve.wait_ge(trig_ready, 1)
                else:
                    dve.wait_ge(q_ready, h)
                V.tensor_tensor(rot_a[pe32, :], flat(A, pe32), trig[pe32, :], ALU.mult).then_inc(rot_ready, 1)
                V.tensor_tensor(rot_b[pe32, :], flat(A, sw32), trig[sw32, :], ALU.mult).then_inc(a_free, 1)

            def front_k(h, p):
                dve.wait_ge(k_hi_done, h + 1)
                V.tensor_tensor(k_lo[p][lo64, :], flat(A, lo64), k_hi[p][lo64, :].bitcast(F32), ALU.subtract)\
                    .then_inc(a_free, 1)

            def maxima(h):
                for n, qt in enumerate(S_ORDER):
                    dve.wait_ge(item, ITEMS * h + 4 + n)
                    V.reduce_max(top[:, qt:qt + 1], flat(A)[:, 0:(qt + 1) * P], AX_X).then_inc(a_free, 1)
                dve.wait_ge(a_free, FREES * (h + 1))
                V.tensor_scalar(top_r[:], top[:], -1.0, None, ALU.mult).then_inc(m_ready, 1)

            def invert(h, n):
                if n == 0:
                    dve.wait_ge(o_read, h + 1 + O_FREE)
                cut = slice(n * HALF, (n + 1) * HALF)
                step.mark(V.reciprocal(recip[lo64, cut], att[hi64, cut]))

            def leave(h, p):
                step.wait()
                dve.wait_ge(y_done, h - 1 + Y_FREE)
                V.tensor_tensor(y_full[64 * p:64 * p + 64, :], att[lo64, :], recip[lo64, :], ALU.mult)\
                    .then_inc(y_ready, 1)

            dve.sem_inc(o_read, O_FREE)
            dve.sem_inc(y_ready, ATT_FREE)
            for h in range(2):
                front_q(h, h, h == 0)
                front_k(h, h)
                maxima(h)
            with dve.Fori(0, NH // 2 - 1) as i:
                step.enter(i, 4)
                for p in range(2):
                    front_q(2 * i + 2 + p, p)
                    invert(2 * i + p, 0)
                    front_k(2 * i + 2 + p, p)
                    invert(2 * i + p, 1)
                    leave(2 * i + p, p)
                    maxima(2 * i + 2 + p)
                step.leave(NH // 2 - 1)
            for p in range(2):
                for n in range(2):
                    invert(NH - 2 + p, n)
                leave(NH - 2 + p, p)

        @block.gpsimd
        def _(pool):
            step = k.pool_steps.on(pool)
            G = nc.gpsimd

            def rotate(h, p):
                pool.wait_ge(rot_ready, h + 1)
                pool.wait_ge(a_free, FREES * h + 1)
                step.mark(G.tensor_tensor(q_hi[p][pe32, :], rot_a[pe32, :], rot_b[pe32, :], ALU.add))
                step.mark(G.tensor_tensor(rot_a[pe32, :], rot_a[pe32, :], rot_b[pe32, :], ALU.add))
                step.wait()
                G.tensor_tensor(q_lo[p][pe32, :], rot_a[pe32, :], q_hi[p][pe32, :].bitcast(F32), ALU.subtract)\
                    .then_inc(q_ready, 1)

            def store(h, p, i):
                rows = slice(64 * p, 64 * p + 64)
                pool.wait_ge(y_ready, h + 1 + ATT_FREE)
                step.mark(G.tensor_tensor(ym_hi[rows, i, :], y_full[rows, :], ones[rows, 0:1].to_broadcast([64, S]),
                                          ALU.mult))
                step.wait()
                G.tensor_tensor(ym_lo[rows, i, :], y_full[rows, :], ym_hi[rows, i, :].bitcast(F32), ALU.subtract)\
                    .then_inc(y_done, 1)

            pool.sem_inc(y_done, Y_FREE)
            G.tensor_copy(trig[hi64, :], k.trig_in[hi64, :]).then_inc(trig_ready, 1)
            pool.wait_ge(trig_ready, 1)
            for p in range(2):
                G.memset(k_hi[p][ONE, :].bitcast(F32), 1.0)
                G.memset(k_lo[p][ONE, :].bitcast(F32), 0.0)
                last = G.memset(q_lo[p][ONE, :].bitcast(F32), 0.0)
            step.mark(last)
            step.wait()
            for p in range(2):
                last = G.memset(v_one[p][:, :, HD:P], 1.0)
            last.then_inc(ones_set, 1)
            pool.wait_ge(ones_set, 1)
            for h in range(2):
                rotate(h, h)
            with pool.Fori(0, NH // 2 - 1) as i:
                step.enter(i, 6)
                for p in range(2):
                    rotate(2 * i + 2 + p, p)
                    store(2 * i + p, p, i)
                step.leave(NH // 2 - 1)
            store(NH - 2, 0, NH // 2 - 1)
            store(NH - 1, 1, NH // 2 - 1)


def head_stats(nc, out, square, ones_block, c):
    for tt in range(TT):
        last = nc.tensor.matmul(out[:, c, tt, :], square[:, tt * P:(tt + 1) * P], ones_block[:, 0:P:HD],
                                start=True, stop=True)
    return last


def widened(stats, wide, c):
    src = stats[:, c, :, :].rearrange("p t h -> p (t h)").rearrange("p (a o) -> p a o", o=1)
    return wide[:].rearrange("p (a d) -> p a d", d=HD), src.to_broadcast([P, 2 * TT, HD])


def spread_stats(nc, outs, wide, ident):
    for tt in range(TT):
        at = tt % 4 * P
        last = nc.tensor.matmul(outs[tt // 4][:, at:at + P], wide[:, tt * P:(tt + 1) * P], ident[:], start=True, stop=True)
    return last


def rwkv_inputs(nc, mem, k, t):
    hT, cols, ps, ident = k.hT, k.cols, k.ps, k.ident
    w_lora = mem.at("w_lora", 94, [P, 2, RW])
    reset = mem.at("reset", 98, [P, S])
    logw = [mem.at(f"logw{j}", 102 + 4 * j, [P, S]) for j in range(2)]
    rate = [mem.at(f"rate{j}", 110 + 4 * j, [P, S]) for j in range(2)]
    square = mem.at("kk_square", 118, [P, RT, S])
    norm = mem.at("kk_norm", 134, [P, RT, TT, 2])
    wide = [mem.at(f"norm_wide{j}", 136 + 4 * j, [P, S]) for j in range(2)]
    keep_a = mem.at("keep_a", 4.25, [P, RT])
    beta, cum, kk, ones_block = k.beta, k.cum, k.kk, k.ones_block
    flat = lambda b: ps[:, b:b + 2, :].rearrange("p b n -> p (b n)")
    SS = 4
    SPREAD = (6, 4)
    ss = ps[:, SS, 0:RT * TT * 2].rearrange("p (c t h) -> p c t h", c=RT, t=TT)
    with ExitStack() as ctx:
        loaded, tanh_done, z_mm, a_mm, logw_done, rate_done, sq_done, ss_mm, root_done, inverted, spread, cum_done = sems(
            nc, ctx, "c_loaded", "c_tanh", "c_z_mm", "c_a_mm", "c_logw", "c_rate", "c_sq", "c_ss_mm", "c_root",
            "c_inverted", "c_spread", "c_cum")
        kk_done, wide_done, blend_done, later_in = sems(nc, ctx, "c_kk_done", "c_wide", "c_blend", "c_later_in")
        keep_done, key_rate = sems(nc, ctx, "c_keep", "c_key_rate")
        block = ctx.enter_context(nc.Block())

        @block.sync
        def _(sp):
            sp.dma_start(w_lora[:], t["w_lora"]).then_inc(loaded, 16)
            sp.dma_start(ones_block[:], t["ones_block"]).then_inc(loaded, 16)
            sp.dma_start(k.gate[:], t["gate_g2"]).then_inc(later_in, 16)
            sp.dma_start(k.chunk_mask[:], t["chunk_mask"]).then_inc(later_in, 16)
            sp.dma_start(k.merge[:], t["merge"]).then_inc(later_in, 16)
            sp.wait_ge(later_in, 48)

        @block.tensor
        def _(pe):
            def lora(c):
                for n, (done, free) in enumerate(((z_mm, logw_done), (a_mm, rate_done))):
                    if c:
                        pe.wait_ge(free, c)
                    for b in range(2):
                        last = nc.tensor.matmul(ps[:, 2 * n + b, :], w_lora[:, n, c * P:(c + 1) * P],
                                                hT[:, T_WA, b * HALF:(b + 1) * HALF], start=True, stop=True)
                    last.then_inc(done, 1)

            pe.wait_ge(loaded, 32)
            for c in range(RT):
                pe.wait_ge(sq_done, c + 1)
                last = head_stats(nc, ss, square[:, c, :], ones_block, c)
            last.then_inc(ss_mm, 1)
            pe.wait_ge(tanh_done, 1)
            lora(0)
            for c in range(RT):
                if c < RT - 1:
                    lora(c + 1)
                pe.wait_ge(wide_done, c + 1)
                if c >= 2:
                    pe.wait_ge(kk_done, c - 1)
                b = SPREAD[c % 2]
                spread_stats(nc, [ps[:, b, :], ps[:, b + 1, :]], wide[c % 2], ident).then_inc(spread, 1)

        @block.scalar
        def _(act):
            for c in range(RT):
                nc.scalar.activation(square[:, c, :], hT[:, T_K + c, :], ACT.Square,
                                     scale=cols[:, C_KK + c:C_KK + c + 1]).then_inc(sq_done, 1)
            nc.scalar.activation(hT[0:64, T_WA, :], hT[0:64, T_WA, :], ACT.Tanh).then_inc(tanh_done, 1)
            act.wait_ge(ss_mm, 1)
            nc.scalar.activation(norm[:], ss, ACT.Sqrt).then_inc(root_done, 1)
            for c in range(RT):
                act.wait_ge(z_mm, c + 1)
                if c >= 2:
                    act.wait_ge(cum_done, c - 1)
                nc.scalar.activation(logw[c % 2][:], flat(0), ACT.Sigmoid, bias=cols[:, C_W0 + c:C_W0 + c + 1])\
                    .then_inc(logw_done, 1)
                act.wait_ge(a_mm, c + 1)
                nc.scalar.activation(beta[:, c, :], flat(2), ACT.Sigmoid, bias=cols[:, C_A0 + c:C_A0 + c + 1])\
                    .then_inc(rate_done, 1)
                act.wait_ge(rate_done, c + 1)
                act.wait_ge(keep_done, 1)
                if c >= 2:
                    act.wait_ge(blend_done, c - 1)
                nc.scalar.activation(rate[c % 2][:], beta[:, c, :], ACT.Identity, scale=cols[:, C_KA + c:C_KA + c + 1],
                                     bias=keep_a[:, c:c + 1]).then_inc(key_rate, 1)
            nc.scalar.activation(hT[:, T_G, :], hT[:, T_G, :], ACT.Sigmoid)

        @block.vector
        def _(dve):
            V = nc.vector
            step = k.dve_steps.on(dve)
            V.memset(k.one[:], 1.0)
            step.mark(V.memset(reset[:], 1.0))
            step.wait()
            V.memset(reset[:].rearrange("p (n c) -> p n c", c=CH)[:, :, 0:1], 0.0)
            V.tensor_scalar(keep_a[:], cols[:, C_KA:C_KA + RT], -1.0, 1.0, ALU.mult, ALU.add).then_inc(keep_done, 1)
            dve.wait_ge(root_done, 1)
            step.mark(V.tensor_scalar(norm[:], norm[:], 1e-12, None, ALU.max))
            step.wait()
            V.reciprocal(norm[:], norm[:]).then_inc(inverted, 1)
            dve.wait_ge(inverted, 1)
            out, src = widened(norm, wide[0], 0)
            V.tensor_copy(out, src).then_inc(wide_done, 1)

            def decay_sum(c):
                dve.wait_ge(logw_done, c + 1)
                V.tensor_tensor_scan(cum[:, c, :], reset[:], logw[c % 2][:], 0.0, ALU.mult, ALU.add).then_inc(cum_done, 1)

            def keys(c):
                dve.wait_ge(rate_done, c + 1)
                dve.wait_ge(key_rate, c + 1)
                dve.wait_ge(spread, c + 1)
                V.scalar_tensor_tensor(kk[:, c, :], hT[:, T_K + c, :], cols[:, C_KK + c:C_KK + c + 1],
                                       flat(SPREAD[c % 2]), ALU.mult, ALU.mult).then_inc(kk_done, 1)
                dve.wait_ge(kk_done, c + 1)
                V.scalar_tensor_tensor(beta[:, c, :], beta[:, c, :], -1.0, kk[:, c, :], ALU.mult, ALU.mult)

            decay_sum(0)
            for c in range(RT):
                if c < RT - 1:
                    decay_sum(c + 1)
                keys(c)

        @block.gpsimd
        def _(pool):
            def blend(c):
                pool.wait_ge(key_rate, c + 1)
                pool.wait_ge(kk_done, c + 1)
                nc.gpsimd.tensor_tensor(hT[:, T_K + c, :], hT[:, T_K + c, :], rate[c % 2][:], ALU.mult)\
                    .then_inc(blend_done, 1)

            pool.wait_ge(inverted, 1)
            for c in range(RT):
                if c:
                    pool.wait_ge(wide_done, c)
                    if c >= 2:
                        pool.wait_ge(spread, c - 1)
                    out, src = widened(norm, wide[c % 2], c)
                    nc.gpsimd.tensor_copy(out, src).then_inc(wide_done, 1)
                if c:
                    blend(c - 1)
            blend(RT - 1)


def rwkv_chunks(nc, mem, k):
    ident, ps = k.ident, k.ps
    hT, cum, kk_all, beta, mask, merge = k.hT, k.cum, k.kk, k.beta, k.chunk_mask, k.merge
    at = [94.0]

    def new(name, shape, dtype=F32, copies=1):
        out = []
        size = -(-int(np.prod(shape[1:])) * 4 // 32) * 32 / KB
        for n in range(copies):
            out.append(mem.at(f"{name}{n}", at[0], shape, dtype))
            at[0] += size
        return out if copies > 1 else out[0]

    pair = [P, RT, P]
    decay = new("decay", [P, RT, CH + 1], copies=2)
    undecay = new("undecay", [P, RT, CH], copies=2)
    bk = new("bk_chunk", [P, RT, 2, CH], copies=2)
    ar = new("ar_chunk", [P, RT, 2, CH], copies=2)
    v_st = new("v_static", [P, RT, CH], copies=2)
    scores = new("scores", [P, 2, RT, P], copies=2)
    inv_t = new("inverse_t", pair, copies=2)
    bk_tok = new("bk_tok", pair, copies=2)
    uv = new("u_v", [P, 2, RT, CH], copies=2)
    sv = new("s_v", [P, 2, RT, CH], copies=2)
    am = new("a_m", [P, 2, RT, CH], copies=2)
    rho = new("rho", [P, 2, RT, CH], copies=2)
    end = new("end_decay", [64, 2, RT], copies=2)
    low_t = new("lower_t", pair, copies=2)
    inv = new("inverse", pair, copies=2)
    prod = new("product", pair)
    rhs = mem.at("rhs", 38 + 4 * T_WA, [P, RT, CH])
    state_sum = new("state_sum", [64, 2, RT, CH])
    assert at[0] <= 153, at
    LEVELS = 6
    lo, hi = slice(0, 64), slice(64, P)
    half = lambda p: slice(64 * p, 64 * p + 64)
    grp = lambda g: slice(2 * g, 2 * g + 2)
    B_SA, B_RHS = 0, 1
    B_T1, B_X, B_XT = (2, 3), (4, 5), (6, 7)
    B_BKT, B_V = 0, 1
    L_SCORES, L_LOW = 4, 5
    view = lambda bank, n=P, rows=slice(0, P), cols=2: ps[rows, bank, 0:cols * n].rearrange("p (c n) -> p c n", n=n)

    with ExitStack() as ctx:
        exps, bk_ready, x_reset, ar_ready, scores_mm, tr_done, sc_ready, low_ready, am_ready, tok_ready, init = sems(
            nc, ctx, "d_exps", "d_bk_ready", "d_x_reset", "d_ar_ready", "d_scores_mm", "d_tr_done", "d_sc_ready",
            "d_low_ready", "d_am_ready", "d_tok_ready", "d_init")
        t1_mm = sems(nc, ctx, "d_t1_mm0", "d_t1_mm1")
        t1_out = sems(nc, ctx, "d_t1_out0", "d_t1_out1")
        x_mm = sems(nc, ctx, "d_x_mm0", "d_x_mm1")
        xt_mm = sems(nc, ctx, "d_xt_mm0", "d_xt_mm1")
        x_up = sems(nc, ctx, "d_x_up0", "d_x_up1")
        xt_up = sems(nc, ctx, "d_xt_up0", "d_xt_up1")
        rhs_mm, rhs_ready, sa_mm, sa_ready, s_mm, state_ready, y_mm, y_out, passed = sems(
            nc, ctx, "d_rhs_mm", "d_rhs_ready", "d_sa_mm", "d_sa_ready", "d_s_mm", "d_state_ready", "d_y_mm",
            "d_y_out", "d_passed")
        LOOPS = NC_ // 2 - 1
        SLOTS_FREE, Y_FREE = 2, 1
        block = ctx.enter_context(nc.Block())

        def stages(body, eng, enter=None, leave=None):
            body(0, 0, False, True)
            with eng.Fori(0, LOOPS) as i:
                if enter:
                    enter(i)
                body(2 * i + 1, 1, True, True)
                body(2 * i + 2, 0, True, True)
                if leave:
                    leave(LOOPS)
            body(NC_ - 1, 1, True, False)

        @block.tensor
        def _(pe):
            mm = nc.tensor.matmul

            def rhs_step(n, q):
                pe.wait_ge(am_ready, n + 1)
                pe.wait_ge(tok_ready, n + 1)
                pe.wait_ge(state_ready, n + 1)
                for c in range(RT):
                    for p in range(2):
                        last = mm(ps[half(p), B_RHS, c * CH:(c + 1) * CH], am[q][:, p, c, :], sv[q][:, p, c, :],
                                  start=True, stop=True)
                last.then_inc(rhs_mm, 1)

            def sa_step(n, q):
                pe.wait_ge(rhs_ready, n + 1)
                for g in range(2):
                    pe.wait_ge(xt_up[g], LEVELS * (n + 1))
                for c in range(RT):
                    last = mm(ps[:, B_SA, c * CH:(c + 1) * CH], inv_t[q][:, c, :], rhs[:, c, :], start=True, stop=True)
                last.then_inc(sa_mm, 1)

            def state_step(n, q):
                pe.wait_ge(sa_ready, n + 1)
                for p in range(2):
                    for c in range(RT):
                        last = mm(ps[lo, B_SA, (p * RT + c) * CH:(p * RT + c + 1) * CH], bk_tok[q][:, c, half(p)],
                                  uv[q][:, p, c, :], start=True, stop=True)
                last.then_inc(s_mm, 1)

            def y_step(n, q):
                for c in range(RT):
                    for p in range(2):
                        out = ps[half(p), B_RHS, c * CH:(c + 1) * CH]
                        mm(out, sv[q][:, p, c, :], rho[q][:, p, c, :], start=True, stop=False)
                        last = mm(out, uv[q][:, p, c, :], scores[q][:, p, c, CH:P], start=False, stop=True)
                last.then_inc(y_mm, 1)

            def scores_step(m, q):
                pe.wait_ge(bk_ready, m + 1)
                pe.wait_ge(ar_ready, m + 1)
                if not (type(m) is int and m == 0):
                    pe.wait_ge(y_out, m - 1 + Y_FREE)
                    pe.wait_ge(state_ready, m)
                for c in range(RT):
                    for p in range(2):
                        last = mm(ps[:, p, c * P:(c + 1) * P], bk[q][half(p), c, :, :].rearrange("p a t -> p (a t)"),
                                  ar[q][half(p), c, :, :].rearrange("p a t -> p (a t)"), start=True, stop=True)
                last.then_inc(scores_mm, 1)

            def transposes(m, q):
                pe.wait_ge(sc_ready, m + 1)
                for c in range(RT):
                    nc.tensor.transpose(ps[:, B_BKT, c * P:(c + 1) * P],
                                        bk[q][:, c, :, :].rearrange("p a t -> p (a t)"), ident[:])
                for c in range(RT):
                    last = nc.tensor.transpose(ps[lo, B_V, c * P:(c + 1) * P], v_st[q][:, c, :], ident[:])
                last.then_inc(tr_done, 1)

            def stage(m, q, chain, ahead):
                n, qn = m - 1, 1 - q
                pe.wait_ge(low_ready, m + 1)
                for g in range(2):
                    for c in range(2):
                        last = nc.tensor.transpose(ps[:, B_T1[g], c * P:(c + 1) * P], low_t[q][:, 2 * g + c, :], ident[:])
                    last.then_inc(t1_mm[g], 1)
                if chain:
                    pe.wait_ge(tok_ready, m + 1)
                    rhs_step(n, qn)
                for l in range(1, LEVELS):
                    for g in range(2):
                        pe.wait_ge(x_up[g], (LEVELS - 1) * m + l)
                        for c in range(2):
                            last = mm(ps[:, B_T1[g], c * P:(c + 1) * P], low_t[q][:, 2 * g + c, :], inv[q][:, 2 * g + c, :],
                                      start=True, stop=True)
                        last.then_inc(t1_mm[g], 1)
                    if chain and l == 1:
                        sa_step(n, qn)
                    if chain and l == 2:
                        state_step(n, qn)
                    if chain and l == 3:
                        y_step(n, qn)
                    if ahead and l == L_SCORES:
                        scores_step(m + 1, 1 - q)
                    for g in range(2):
                        pe.wait_ge(t1_out[g], (LEVELS - 1) * m + l)
                        pe.wait_ge(xt_up[g], LEVELS * m + l)
                        if l < LEVELS - 1:
                            for c in range(2):
                                last = mm(ps[:, B_X[g], c * P:(c + 1) * P], inv_t[q][:, 2 * g + c, :], prod[:, 2 * g + c, :],
                                          start=True, stop=True)
                            last.then_inc(x_mm[g], 1)
                        for c in range(2):
                            last = mm(ps[:, B_XT[g], c * P:(c + 1) * P], prod[:, 2 * g + c, :], inv_t[q][:, 2 * g + c, :],
                                      start=True, stop=True)
                        last.then_inc(xt_mm[g], 1)
                if ahead:
                    transposes(m + 1, 1 - q)

            pe.wait_ge(init, 1)
            pe.sem_inc(y_mm, SLOTS_FREE)
            scores_step(0, 0)
            transposes(0, 0)
            stages(stage, pe)
            n, q = NC_ - 1, 1
            pe.wait_ge(y_out, n + Y_FREE)
            rhs_step(n, q)
            sa_step(n, q)
            state_step(n, q)
            y_step(n, q)

        @block.scalar
        def _(act):
            A = nc.scalar.activation

            def exp_step(m, q):
                if not (type(m) is int and m < 2):
                    act.wait_ge(ar_ready, m - 1)
                    act.wait_ge(bk_ready, m - 1)
                A(decay[q][:, :, 1:CH + 1], cum[:, :, bass.ds(m * CH, CH)], ACT.Exp, scale=-EXP_M05)
                A(undecay[q][:], cum[:, :, bass.ds(m * CH, CH)], ACT.Exp, scale=EXP_M05).then_inc(exps, 1)

            def u_step(n, q):
                act.wait_ge(sa_mm, n + 1)
                for p in range(2):
                    last = A(uv[q][lo, p, :, :], view(B_SA, CH, half(p), RT), ACT.Copy)
                last.then_inc(sa_ready, 1)

            def y_leave(n, q):
                act.wait_ge(y_mm, n + 1 + SLOTS_FREE)
                A(cum[:, :, bass.ds(n * CH, CH)], view(B_RHS, CH, cols=RT), ACT.Copy).then_inc(y_out, 1)

            def rows_step(m, q):
                act.wait_ge(y_mm, m - 1 + SLOTS_FREE)
                act.wait_ge(ar_ready, m + 1)
                for p in range(2):
                    A(am[q][lo, p, :, :], ar[q][half(p), :, 0, :], ACT.Copy)
                    A(rho[q][lo, p, :, :], ar[q][half(p), :, 1, :], ACT.Copy)
                    A(end[q][:, p, :], decay[q][half(p), :, CH], ACT.Copy)

            def low_step(m, q):
                act.wait_ge(sc_ready, m + 1)
                for p in range(2):
                    last = A(low_t[q][half(p), :, half(p)], scores[q][lo, p, :, 0:CH], ACT.Copy)
                last.then_inc(low_ready, 1)

            def tokens_step(m, q):
                act.wait_ge(tr_done, m + 1)
                A(bk_tok[q][:], view(B_BKT, cols=RT), ACT.Copy)
                v_tok = ps[lo, B_V, :].rearrange("p (c a d) -> p a c d", a=2, d=HD)
                A(sv[q][hi, :, :, :], v_tok, ACT.Copy)
                A(uv[q][hi, :, :, :], v_tok, ACT.Copy).then_inc(tok_ready, 1)
                A(am[q][hi, :, :, :].rearrange("p a c t -> p (a c) t"),
                  scores[q][hi, :, :, 0:CH].rearrange("p a c t -> p (a c) t"), ACT.Copy).then_inc(am_ready, 1)

            def stage(m, q, chain, ahead):
                n, qn = m - 1, 1 - q
                for l in range(1, LEVELS):
                    for g in range(2):
                        act.wait_ge(t1_mm[g], LEVELS * m + l + 1)
                        A(prod[:, grp(g), :], view(B_T1[g]), ACT.Copy).then_inc(t1_out[g], 1)
                    if chain and l == 1:
                        u_step(n, qn)
                    if ahead and l == 1:
                        exp_step(m + 1, 1 - q)
                    if chain and l == 3:
                        y_leave(n, qn)
                    if ahead and l == L_SCORES:
                        rows_step(m + 1, 1 - q)
                    if ahead and l == L_LOW:
                        low_step(m + 1, 1 - q)
                        tokens_step(m + 1, 1 - q)

            act.wait_ge(init, 1)
            exp_step(0, 0)
            rows_step(0, 0)
            low_step(0, 0)
            tokens_step(0, 0)
            stages(stage, act)
            u_step(NC_ - 1, 1)
            y_leave(NC_ - 1, 1)

        @block.vector
        def _(dve):
            V = nc.vector
            step = k.dve_steps.on(dve)

            def ar_step(m, q):
                if not (type(m) is int and m < 2):
                    dve.wait_ge(scores_mm, m - 1)
                    dve.wait_ge(am_ready, m - 1)
                dve.wait_ge(exps, m + 1)
                now = bass.ds(m * CH, CH)
                V.tensor_tensor(ar[q][:, :, 0, :], kk_all[:, :, now], decay[q][:, :, 0:CH], ALU.mult)
                V.tensor_tensor(ar[q][:, :, 1, :], hT[:, T_R:T_R + RT, now], decay[q][:, :, 1:CH + 1], ALU.mult)\
                    .then_inc(ar_ready, 1)

            def rhs_out(n, q):
                dve.wait_ge(rhs_mm, n + 1)
                V.tensor_copy(rhs[:], view(B_RHS, CH, cols=RT)).then_inc(rhs_ready, 1)

            def state_out(n, q):
                dve.wait_ge(s_mm, n + 1)
                flat = lambda x: x.rearrange("p a c d -> p (a c) d")
                step.mark(V.tensor_tensor(flat(state_sum[:]), flat(sv[q][lo, :, :, :]), view(B_SA, CH, lo, 2 * RT), ALU.add))
                step.wait()
                V.tensor_tensor(flat(sv[1 - q][lo, :, :, :]), flat(state_sum[:]),
                                end[q][:].rearrange("p a (c o) -> p (a c) o", o=1).to_broadcast([64, 2 * RT, CH]),
                                ALU.mult).then_inc(state_ready, 1)

            def wait_alone(sem, value):
                dve.wait_ge(sem, value).then_inc(passed, 1)

            def merged(x, l, transposed, new, g):
                m01 = merge[:, 2 * l + transposed:2 * l + transposed + 1, :].to_broadcast([P, 2, P])
                return V.copy_predicated(x[:, grp(g), :], m01, new)

            def mask_step(m, q):
                dve.wait_ge(scores_mm, m + 1)
                dve.wait_ge(y_mm, m - 1 + SLOTS_FREE)
                for p in range(2):
                    last = V.tensor_tensor(scores[q][:, p, :, :], view(p, cols=RT),
                                           mask[:].rearrange("p (o n) -> p o n", o=1).to_broadcast([P, RT, P]), ALU.mult)
                last.then_inc(sc_ready, 1)

            def stage(m, q, chain, ahead):
                n, qn = m - 1, 1 - q
                wait_alone(x_reset, m + 1)
                wait_alone(low_ready, m + 1)
                for g in range(2):
                    merged(inv_t[q], 0, 1, low_t[q][:, grp(g), :], g).then_inc(xt_up[g], 1)
                for g in range(2):
                    wait_alone(t1_mm[g], LEVELS * m + 1)
                    merged(inv[q], 0, 0, view(B_T1[g]), g).then_inc(x_up[g], 1)
                if chain:
                    rhs_out(n, qn)
                for l in range(1, LEVELS):
                    for g in range(2):
                        if l < LEVELS - 1:
                            wait_alone(x_mm[g], (LEVELS - 2) * m + l)
                            merged(inv[q], l, 0, view(B_X[g]), g).then_inc(x_up[g], 1)
                        wait_alone(xt_mm[g], (LEVELS - 1) * m + l)
                        merged(inv_t[q], l, 1, view(B_XT[g]), g).then_inc(xt_up[g], 1)
                    if chain and l == 2:
                        state_out(n, qn)
                    if ahead and l == 2:
                        ar_step(m + 1, 1 - q)
                    if ahead and l == L_SCORES:
                        mask_step(m + 1, 1 - q)

            for q in range(2):
                V.memset(decay[q][:, :, 0:1], 1.0)
                V.memset(rho[q][hi, :, :, :], 0.0)
            V.memset(sv[0][lo, :, :, :], 0.0).then_inc(state_ready, 1)
            V.memset(low_t[0][:], 0.0)
            V.memset(low_t[1][:], 0.0).then_inc(init, 1)
            ar_step(0, 0)
            mask_step(0, 0)
            stages(stage, dve, lambda i: step.enter(i, 2), step.leave)
            rhs_out(NC_ - 1, 1)
            state_out(NC_ - 1, 1)

        @block.gpsimd
        def _(pool):
            G = nc.gpsimd

            def bk_step(m, q):
                if not (type(m) is int and m < 2):
                    pool.wait_ge(tr_done, m - 1)
                pool.wait_ge(exps, m + 1)
                now = bass.ds(m * CH, CH)
                G.tensor_tensor(bk[q][:, :, 0, :], beta[:, :, now], undecay[q][:], ALU.mult)
                G.tensor_tensor(bk[q][:, :, 1, :], hT[:, T_K:T_K + RT, now], undecay[q][:], ALU.mult)
                G.tensor_copy(v_st[q][:], hT[:, T_V:T_V + RT, now]).then_inc(bk_ready, 1)

            def stage(m, q, chain, ahead):
                if chain:
                    pool.wait_ge(y_mm, m - 1 + SLOTS_FREE)
                eye = ident[:].rearrange("p (o n) -> p o n", o=1).to_broadcast([P, RT, P])
                one = k.one[:, 0:1].rearrange("p (a b) -> p a b", a=1).to_broadcast([P, RT, P])
                G.tensor_tensor(inv_t[q][:], eye, one, ALU.mult)
                G.tensor_tensor(inv[q][:], eye, one, ALU.mult).then_inc(x_reset, 1)
                if ahead:
                    bk_step(m + 1, 1 - q)

            pool.sem_inc(y_out, Y_FREE)
            bk_step(0, 0)
            stages(stage, pool)


def rwkv_outputs(nc, mem, k, t):
    hT, cols, ps, y, ones_block, ident = k.hT, k.cols, k.ps, k.cum, k.ones_block, k.ident
    square = [mem.at(f"dev_square{j}", 126 + 4 * j, [P, S]) for j in range(2)]
    dot = [mem.at(f"bonus{j}", 134 + 4 * j, [P, S]) for j in range(RT)]
    full = [mem.at(f"yr_full{j}", 150 + 4 * j, [P, S]) for j in range(2)]
    scale = mem.at("gn_scale", 158, [P, RT, TT, 2])
    gn_eps = mem.at("gn_eps", 4.5, [P, 1])
    flat = lambda b: ps[:, b:b + 2, :].rearrange("p b n -> p (b n)")
    MEAN, DOT, VAR = 0, 2, 4
    SPREAD, GATE = (0, 2), (4, 6)
    var = ps[:, VAR, 0:RT * TT * 2].rearrange("p (c t h) -> p c t h", c=RT, t=TT)
    with ExitStack() as ctx:
        init, mean_mm, dot_in, dot_mm, gate_mm, dev, bonus, sq_done, var_mm, root_done, scaled, spread, done, hi_done, lo_done, wide_done, w_out_in = sems(
            nc, ctx, "e_init", "e_mean_mm", "e_dot_in", "e_dot_mm", "e_gate_mm", "e_dev", "e_bonus", "e_sq",
            "e_var_mm", "e_root", "e_scaled", "e_spread", "e_done", "e_hi", "e_lo", "e_wide", "e_w_out_in")
        block = ctx.enter_context(nc.Block())

        @block.sync
        def _(sp):
            for kt, raw in enumerate(k.wout_raw):
                sp.dma_start(raw[:], t["w_out"][kt]).then_inc(w_out_in, 16)
            sp.wait_ge(w_out_in, 16 * len(k.wout_raw))

        @block.tensor
        def _(pe):
            def product(bank, w, r):
                for b in range(2):
                    last = nc.tensor.matmul(ps[:, bank + b, :], w, r[:, b * HALF:(b + 1) * HALF], start=True, stop=True)
                return last

            def variance(c):
                pe.wait_ge(sq_done, c + 1)
                head_stats(nc, var, square[c % 2], ones_block, c).then_inc(var_mm, 1)

            for c in range(RT):
                if c:
                    pe.wait_ge(dev, c)
                product(MEAN, ones_block[:], y[:, c, :]).then_inc(mean_mm, 1)
                pe.wait_ge(dot_in, c + 1)
                if c:
                    pe.wait_ge(bonus, c)
                product(DOT, ones_block[:], dot[c]).then_inc(dot_mm, 1)
                if c:
                    variance(c - 1)
            variance(RT - 1)
            for c in range(RT):
                if c == 0:
                    pe.wait_ge(root_done, 1)
                if c >= 2:
                    pe.wait_ge(done, c - 1)
                product(GATE[c % 2], k.gate[:, c * P:(c + 1) * P], hT[:, T_G, :]).then_inc(gate_mm, 1)
                if c == 0:
                    pe.wait_ge(dev, RT)
                    pe.wait_ge(bonus, RT)
                pe.wait_ge(wide_done, c + 1)
                b = SPREAD[c % 2]
                spread_stats(nc, [ps[:, b, :], ps[:, b + 1, :]], square[c % 2], ident).then_inc(spread, 1)

        @block.scalar
        def _(act):
            act.wait_ge(init, 1)
            for c in range(RT):
                act.wait_ge(dev, c + 1)
                if c >= 2:
                    act.wait_ge(var_mm, c - 1)
                nc.scalar.activation(square[c % 2][:], y[:, c, :], ACT.Square).then_inc(sq_done, 1)
            act.wait_ge(var_mm, RT)
            nc.scalar.activation(scale[:], var, ACT.Sqrt, scale=1.0 / HD, bias=gn_eps[:]).then_inc(root_done, 1)
            act.wait_ge(scaled, 1)
            for c in range(RT + 1):
                if c < RT:
                    if c >= 2:
                        act.wait_ge(spread, c - 1)
                    out, src = widened(scale, square[c % 2], c)
                    nc.scalar.activation(out, src, ACT.Copy).then_inc(wide_done, 1)
                if c:
                    act.wait_ge(done, c)
                    nc.scalar.activation(k.yr_hi[:, c - 1, :], full[(c - 1) % 2][:], ACT.Copy).then_inc(hi_done, 1)

        @block.vector
        def _(dve):
            V = nc.vector
            step = k.dve_steps.on(dve)
            V.memset(gn_eps[:], GN_EPS).then_inc(init, 1)

            def dot_step(c):
                V.scalar_tensor_tensor(dot[c][:], hT[:, T_R + c, :], cols[:, C_RK + c:C_RK + c + 1],
                                       hT[:, T_K + c, :], ALU.mult, ALU.mult).then_inc(dot_in, 1)

            dot_step(0)
            for c in range(RT):
                dve.wait_ge(mean_mm, c + 1)
                V.scalar_tensor_tensor(y[:, c, :], flat(MEAN), -1.0 / HD, y[:, c, :], ALU.mult, ALU.add).then_inc(dev, 1)
                if c < RT - 1:
                    dot_step(c + 1)
                dve.wait_ge(dot_mm, c + 1)
                V.tensor_tensor(dot[c][:], flat(DOT), hT[:, T_V + c, :], ALU.mult).then_inc(bonus, 1)
            dve.wait_ge(root_done, 1)
            V.reciprocal(scale[:], scale[:]).then_inc(scaled, 1)
            for c in range(RT):
                dve.wait_ge(spread, c + 1)
                step.mark(V.scalar_tensor_tensor(y[:, c, :], y[:, c, :], cols[:, C_LG + c:C_LG + c + 1],
                                                 flat(SPREAD[c % 2]), ALU.mult, ALU.mult))
                step.wait()
                step.mark(V.scalar_tensor_tensor(y[:, c, :], y[:, c, :], cols[:, C_LB + c:C_LB + c + 1], dot[c][:],
                                                 ALU.add, ALU.add))
                step.wait()
                dve.wait_ge(gate_mm, c + 1)
                if c >= 2:
                    dve.wait_ge(lo_done, c - 1)
                V.tensor_tensor(full[c % 2][:], flat(GATE[c % 2]), y[:, c, :], ALU.mult).then_inc(done, 1)

        @block.gpsimd
        def _(pool):
            for c in range(RT):
                pool.wait_ge(hi_done, c + 1)
                nc.gpsimd.tensor_tensor(k.yr_lo[:, c, :], full[c % 2][:], k.yr_hi[:, c, :].bitcast(F32), ALU.subtract)\
                    .then_inc(lo_done, 1)


def layer_norm_stats(nc, dve, step, rows, stats, mean_var):
    a = step.mark(nc.vector.bn_stats(stats[:, 0, :], rows[:, 0:HALF]))
    step.mark(nc.vector.bn_stats(stats[:, 1, :], rows[:, HALF:D]))
    step.wait()
    return nc.vector.bn_aggr(mean_var, stats[:].rearrange("p a n -> p (a n)"))


def mix_out(nc, mem, k, t):
    ps, x1 = k.ps, k.x1
    w_hi = mem.at("wout_hi", 126, [P, KT, D], F32R)
    w_lo = mem.at("wout_lo", 158, [P, KT, D], F32R)
    w_raw, AHEAD = k.wout_raw, len(k.wout_raw)
    x_hi, x_lo, w1_raw, w1_hi, w1_lo = k.x1T_hi, k.x1T_lo, k.w1_raw, k.w1_hi, k.w1_lo
    gain = mem.at("ln1_gain", 70, [P, D])
    bias = mem.at("ln1_bias", 74, [P, D])
    stats = mem.at("ln1_stats", 2.5, [P, TT, 2, 6])
    mean_var = mem.at("ln1_mean_var", 2.875, [P, TT, 2])
    sd = mem.at("ln1_sd", 3, [P, TT])
    eps = mem.at("ln1_eps", 3.125, [P, 1])
    y = lambda kt: (k.yr_hi, k.yr_lo) if kt < RT else (k.ym_hi, k.ym_lo)
    with ExitStack() as ctx:
        x_in, rows_in, init, w_whi, w_split, mix_mm, mixed, var_done, sd_done, scaled, normed, last_normed = sems(
            nc, ctx, "f_x_in", "f_rows_in", "f_init", "f_w_hi", "f_w_split", "f_mix_mm", "f_mixed", "f_var",
            "f_sd", "f_scaled", "f_normed", "f_last_normed")
        w_in = sems(nc, ctx, *(f"f_w_in{j}" for j in range(AHEAD)))
        w1_in, w1_whi, w1_split, xT_ready, xhi_done, xlo_done = sems(
            nc, ctx, "f_w1_in", "f_w1_hi", "f_w1_split", "f_xT_ready", "f_xhi", "f_xlo")
        block = ctx.enter_context(nc.Block())

        @block.sync
        def _(sp):
            for kt in range(AHEAD, KT):
                sp.wait_ge(w_split, kt - AHEAD + 1)
                sp.dma_start(w_raw[kt % AHEAD][:], t["w_out"][kt]).then_inc(w_in[kt % AHEAD], 16)
            sp.dma_start(gain[:], t["ln"][0:1, :].to_broadcast([P, D])).then_inc(rows_in, 16)
            sp.dma_start(bias[:], t["ln"][1:2, :].to_broadcast([P, D])).then_inc(rows_in, 16)
            sp.dma_start(x1[:], t["x"].rearrange("o (t p) d -> p (o t) d", p=P)).then_inc(x_in, 16)
            for j in range(2):
                sp.dma_start(w1_raw[j][:], t["w_ffn1"][j]).then_inc(w1_in, 16)

        @block.tensor
        def _(pe):
            def products(tt, bank, kt):
                y_hi, y_lo = y(kt)
                tok = slice(tt * P, (tt + 1) * P)
                for n, (a, w) in enumerate(((y_hi, w_hi), (y_hi, w_lo), (y_lo, w_hi))):
                    for b in range(2):
                        last = nc.tensor.matmul(ps[:, bank + b, :], a[:, kt % RT, tok], w[:, kt, b * HALF:(b + 1) * HALF],
                                                start=kt == 0 and n == 0, stop=kt == KT - 1 and n == 2)
                return last

            for kt in range(KT):
                pe.wait_ge(w_split, kt + 1)
                for tt in range(4):
                    last = products(tt, 2 * tt, kt)
                    if kt == KT - 1:
                        last.then_inc(mix_mm, 1)
            for tt in range(4, TT):
                pe.wait_ge(mixed, tt - 3)
                for kt in range(KT):
                    last = products(tt, 2 * (tt - 4), kt)
                last.then_inc(mix_mm, 1)
            for n in range(2 * KT):
                h, kt = divmod(n, KT)
                if n == 0:
                    pe.wait_ge(mixed, 6)
                if kt == 0:
                    pe.wait_ge(normed, 4 * h + 4 if h == 0 else TT - 1)
                    if h:
                        pe.wait_ge(last_normed, 1)
                if n >= 4:
                    pe.wait_ge(xlo_done, n - 3)
                for tt in range(4):
                    last = nc.tensor.transpose(ps[:, n % 4, tt * P:(tt + 1) * P],
                                               x1[:, 4 * h + tt, kt * P:(kt + 1) * P], k.ident[:])
                last.then_inc(xT_ready, 1)

        @block.scalar
        def _(act):
            act.wait_ge(init, 1)
            for tt in range(TT):
                act.wait_ge(var_done, tt + 1)
                nc.scalar.activation(sd[:, tt:tt + 1], mean_var[:, tt, 1:2], ACT.Sqrt, bias=eps[:]).then_inc(sd_done, 1)
            for n in range(2 * KT):
                h, kt = divmod(n, KT)
                act.wait_ge(xT_ready, n + 1)
                nc.scalar.activation(x_hi[:, kt, h * HALF:(h + 1) * HALF], ps[:, n % 4, :], ACT.Copy)\
                    .then_inc(xhi_done, 1)

        @block.vector
        def _(dve):
            V = nc.vector
            step = k.dve_steps.on(dve)
            V.memset(eps[:], LN_EPS).then_inc(init, 1)
            for kt in range(KT):
                if kt >= AHEAD:
                    dve.wait_ge(w_in[kt % AHEAD], 16 * (kt // AHEAD))
                split2(nc, dve, w_raw[kt % AHEAD][:], w_hi[:, kt, :], w_lo[:, kt, :], w_whi, kt + 1, w_split)
            dve.wait_ge(w1_in, 32)
            for j in range(2):
                split2(nc, dve, w1_raw[j][:], w1_hi[j][:], w1_lo[j][:], w1_whi, j + 1, w1_split)
            dve.wait_ge(x_in, 16)

            def normalise(tt):
                dve.wait_ge(sd_done, tt + 1)
                step.mark(V.reciprocal(sd[:, tt:tt + 1], sd[:, tt:tt + 1]))
                step.wait()
                V.tensor_scalar(x1[:, tt, :], x1[:, tt, :], mean_var[:, tt, 0:1], sd[:, tt:tt + 1],
                                ALU.subtract, ALU.mult).then_inc(scaled, 1)

            for tt in range(TT):
                dve.wait_ge(mix_mm, tt + 1)
                bank = 2 * (tt % 4)
                V.scalar_tensor_tensor(x1[:, tt, :], x1[:, tt, :], ALPHA,
                                       ps[:, bank:bank + 2, :].rearrange("p b n -> p (b n)"), ALU.mult, ALU.add)\
                    .then_inc(mixed, 1)
                dve.wait_ge(mixed, tt + 1)
                layer_norm_stats(nc, dve, step, x1[:, tt, :], stats[:, tt, :, :], mean_var[:, tt, :]).then_inc(var_done, 1)
                if tt:
                    normalise(tt - 1)
            normalise(TT - 1)
            dve.wait_ge(scaled, TT)
            dve.wait_ge(rows_in, 32)
            rows = x1[:, TT - 1, :]
            step.mark(V.tensor_tensor(rows, rows, gain[:], ALU.mult))
            step.wait()
            V.tensor_tensor(rows, rows, bias[:], ALU.add).then_inc(last_normed, 1)
            for n in range(2 * KT):
                h, kt = divmod(n, KT)
                cut = slice(h * HALF, (h + 1) * HALF)
                dve.wait_ge(xhi_done, n + 1)
                V.tensor_tensor(x_lo[:, kt, cut], ps[:, n % 4, :], x_hi[:, kt, cut].bitcast(F32), ALU.subtract)\
                    .then_inc(xlo_done, 1)

        @block.gpsimd
        def _(pool):
            G = nc.gpsimd
            step = k.pool_steps.on(pool)
            pool.wait_ge(rows_in, 32)
            for tt in range(TT - 1):
                pool.wait_ge(scaled, tt + 1)
                step.mark(G.tensor_tensor(x1[:, tt, :], x1[:, tt, :], gain[:], ALU.mult))
                step.wait()
                G.tensor_tensor(x1[:, tt, :], x1[:, tt, :], bias[:], ALU.add).then_inc(normed, 1)


def ffn(nc, mem, k, t, out):
    ps, acc, ident = k.ps, k.x1, k.ident
    GRP = 2
    GROUPS = DFF // P // GRP
    OUTS = 2 * TT
    x_hi, x_lo, w1_raw, w1_hi, w1_lo = k.x1T_hi, k.x1T_lo, k.w1_raw, k.w1_hi, k.w1_lo
    hid_hi = [mem.at(f"hid_hi{q}", 134 + 8 * q, [P, GRP, S], F32R) for q in range(2)]
    hid_lo = [mem.at(f"hid_lo{q}", 150 + 8 * q, [P, GRP, S], F32R) for q in range(2)]
    w2_hi = mem.at("w2_hi", 166, [P, GRP, D], F32R)
    w2_lo = mem.at("w2_lo", 174, [P, GRP, D], F32R)
    w2_raw = mem.at("w2_raw", 182, [P, GRP, D])
    gain = mem.at("ln2_gain", 86, [P, D])
    bias = mem.at("ln2_bias", 90, [P, D])
    relu = [mem.at(f"relu{j}", 70 + 4 * j, [P, S]) for j in range(GRP)]
    squared = [mem.at(f"squared{j}", 94 + 4 * j, [P, S]) for j in range(GRP)]
    stats = mem.at("ln2_stats", 1, [P, TT, 2, 6])
    mean_var = mem.at("ln2_mean_var", 1.5, [P, TT, 2])
    sd = mem.at("ln2_sd", 2, [P, TT])
    eps = mem.at("ln2_eps", 2.25, [P, 1])
    flat = lambda b: ps[:, b:b + 2, :].rearrange("p b n -> p (b n)")
    with ExitStack() as ctx:
        rows_in, init, relu_done, square_done, hid_ready, out_mm, added = sems(
            nc, ctx, "g_rows_in", "g_init", "g_relu", "g_square",
            "g_hid_ready", "g_out_mm", "g_added")
        var_done, sd_done, scaled, normed, stored, w2_in, w2_whi, w2_split = sems(
            nc, ctx, "g_var", "g_sd", "g_scaled", "g_normed", "g_stored", "g_w2_in",
            "g_w2_hi", "g_w2_split")
        relu_free, = sems(nc, ctx, "g_relu_free")
        w1_in = sems(nc, ctx, "g_w1_in0", "g_w1_in1")
        w1_whi = sems(nc, ctx, "g_w1_hi0", "g_w1_hi1")
        w1_split = sems(nc, ctx, "g_w1_split0", "g_w1_split1")
        slab_mm = sems(nc, ctx, "g_slab_mm0", "g_slab_mm1")
        SLAB_FREE, OUT_FREE = GRP, 4
        block = ctx.enter_context(nc.Block())
        loops = GROUPS // 2 - 1

        @block.sync
        def _(sp):
            load2 = lambda g: sp.dma_start(w2_raw[:], t["w_ffn2"][g]).then_inc(w2_in, 16)
            load2(0)
            sp.dma_start(gain[:], t["ln"][2:3, :].to_broadcast([P, D])).then_inc(rows_in, 16)
            sp.dma_start(bias[:], t["ln"][3:4, :].to_broadcast([P, D])).then_inc(rows_in, 16)
            for j in range(GRP):
                sp.sem_inc(w1_in[j], 16)
            with sp.Fori(1, GROUPS) as g:
                for j in range(GRP):
                    sp.wait_ge(w1_split[j], g)
                    sp.dma_start(w1_raw[j][:], t["w_ffn1"][GRP * g + j]).then_inc(w1_in[j], 16)
                sp.wait_ge(w2_split, g)
                load2(g)
            for tt in range(TT):
                sp.wait_ge(normed, tt + 1)
                sp.dma_start(out[0, tt * P:(tt + 1) * P, :], acc[:, tt, :]).then_inc(stored, 16)
            sp.wait_ge(stored, 16 * TT)

        @block.tensor
        def _(pe):
            def first(g):
                for j in range(GRP):
                    pe.wait_ge(w1_split[j], g + 1)
                    pe.wait_ge(relu_done, GRP * (g - 1) + j + 1 + SLAB_FREE)
                    project3(nc, [ps[:, 2 * j + b, :] for b in range(2)], w1_hi[j], w1_lo[j],
                             lambda kt, b: x_hi[:, kt, b * HALF:(b + 1) * HALF],
                             lambda kt, b: x_lo[:, kt, b * HALF:(b + 1) * HALF], KT).then_inc(slab_mm[j], 1)

            def second(g, q):
                pe.wait_ge(w2_split, g + 1)
                pe.wait_ge(hid_ready, GRP * (g + 1))
                for n in range(OUTS):
                    tt, b = divmod(n, 2)
                    tok, col = slice(tt * P, (tt + 1) * P), slice(b * HALF, (b + 1) * HALF)
                    pe.wait_ge(added, OUTS * g + n - 3 + OUT_FREE)
                    for j in range(GRP):
                        for m, (a, w) in enumerate(((hid_hi, w2_hi), (hid_hi, w2_lo), (hid_lo, w2_hi))):
                            last = nc.tensor.matmul(ps[:, 4 + n % 4, :], a[q][:, j, tok], w[:, j, col],
                                                    start=j == 0 and m == 0, stop=j == GRP - 1 and m == 2)
                    last.then_inc(out_mm, 1)

            first(0)
            with pe.Fori(0, loops) as i:
                for q in range(2):
                    first(2 * i + q + 1)
                    second(2 * i + q, q)
            first(GROUPS - 1)
            second(GROUPS - 2, 0)
            second(GROUPS - 1, 1)

        @block.scalar
        def _(act):
            A = nc.scalar.activation
            act.sem_inc(relu_done, SLAB_FREE)
            def first(g, q):
                for j in range(GRP):
                    act.wait_ge(slab_mm[j], g + 1)
                    act.wait_ge(relu_free, GRP * (g - 1) + j + 1 + GRP)
                    A(relu[j][:], flat(2 * j), ACT.Relu).then_inc(relu_done, 1)
                    act.wait_ge(relu_done, GRP * g + j + 1 + SLAB_FREE)
                    A(hid_hi[q][:, j, :], relu[j][:], ACT.Square).then_inc(square_done, 1)

            first(0, 0)
            with act.Fori(0, loops) as i:
                for q in range(2):
                    first(2 * i + q + 1, 1 - q)
            first(GROUPS - 1, 1)
            act.wait_ge(init, 1)
            for tt in range(TT):
                act.wait_ge(var_done, tt + 1)
                A(sd[:, tt:tt + 1], mean_var[:, tt, 1:2], ACT.Sqrt, bias=eps[:]).then_inc(sd_done, 1)

        @block.vector
        def _(dve):
            V = nc.vector
            step = k.dve_steps.on(dve)
            V.memset(eps[:], LN_EPS).then_inc(init, 1)

            def split1(g, j):
                dve.wait_ge(w1_in[j], 16 * (g + 1))
                split2(nc, dve, w1_raw[j][:], w1_hi[j][:], w1_lo[j][:], w1_whi[j], g + 1, w1_split[j])

            def first(g, q):
                for j in range(GRP):
                    dve.wait_ge(relu_done, GRP * g + j + 1 + SLAB_FREE)
                    V.tensor_tensor(squared[j][:], relu[j][:], relu[j][:], ALU.mult).then_inc(relu_free, 1)
                    dve.wait_ge(relu_free, GRP * g + j + 1 + GRP)
                    dve.wait_ge(square_done, GRP * g + j + 1)
                    V.tensor_tensor(hid_lo[q][:, j, :], squared[j][:], hid_hi[q][:, j, :].bitcast(F32), ALU.subtract)\
                        .then_inc(hid_ready, 1)
                    yield j

            def split_second(g):
                dve.wait_ge(w2_in, 16 * (g + 1))
                split2(nc, dve, w2_raw[:], w2_hi[:], w2_lo[:], w2_whi, g + 1, w2_split)

            def add(g, n):
                tt, b = divmod(n, 2)
                piece = acc[:, tt, b * HALF:(b + 1) * HALF]
                dve.wait_ge(out_mm, OUTS * g + n + 1)
                return V.tensor_tensor(piece, ps[:, 4 + n % 4, :], piece, ALU.add).then_inc(added, 1)

            def stage(g, q, more, ahead):
                if more:
                    for j in first(g + 1, 1 - q):
                        if ahead:
                            split1(g + 2, j)
                for n in range(OUTS):
                    add(g, n)
                if more:
                    split_second(g + 1)

            dve.sem_inc(relu_free, GRP)
            for j in range(GRP):
                dve.sem_inc(w1_whi[j], 1)
                dve.sem_inc(w1_split[j], 1)
            step.mark(V.tensor_scalar(acc[:], acc[:], ALPHA, None, ALU.mult))
            step.wait()
            dve.sem_inc(added, OUT_FREE)
            split_second(0)
            for j in first(0, 0):
                split1(1, j)
            with dve.Fori(0, loops) as i:
                for q in range(2):
                    stage(2 * i + q, q, True, True)
            stage(GROUPS - 2, 0, True, False)

            def normalise(tt):
                dve.wait_ge(sd_done, tt + 1)
                step.mark(V.reciprocal(sd[:, tt:tt + 1], sd[:, tt:tt + 1]))
                step.wait()
                V.tensor_scalar(acc[:, tt, :], acc[:, tt, :], mean_var[:, tt, 0:1], sd[:, tt:tt + 1],
                                ALU.subtract, ALU.mult).then_inc(scaled, 1)

            for tt in range(TT):
                for b in range(2):
                    add(GROUPS - 1, 2 * tt + b)
                dve.wait_ge(added, OUTS * (GROUPS - 1) + 2 * tt + 2 + OUT_FREE)
                layer_norm_stats(nc, dve, step, acc[:, tt, :], stats[:, tt, :, :], mean_var[:, tt, :]).then_inc(var_done, 1)
                if tt:
                    normalise(tt - 1)
            normalise(TT - 1)

        @block.gpsimd
        def _(pool):
            G = nc.gpsimd
            step = k.pool_steps.on(pool)
            pool.wait_ge(rows_in, 32)
            for tt in range(TT):
                pool.wait_ge(scaled, tt + 1)
                step.mark(G.tensor_tensor(acc[:, tt, :], acc[:, tt, :], gain[:], ALU.mult))
                step.wait()
                G.tensor_tensor(acc[:, tt, :], acc[:, tt, :], bias[:], ALU.add).then_inc(normed, 1)


def build(nc, t, out, debug=None):
    mem = Memory(nc)

    class K:
        pass

    k = K()
    k.ident = mem.at("ident", 0, [P, P])
    k.cols = mem.at("cols", 0.5, [P, NCOLS])
    k.keep = mem.at("keep", 0.75, [P, SLABS])
    k.hT = mem.at("hT", 38, [P, SLABS, S])
    k.ym_hi = mem.at("ym_hi", 6, [P, RT, S], F32R)
    k.ym_lo = mem.at("ym_lo", 22, [P, RT, S], F32R)
    k.beta = mem.at("beta", 159, [P, RT, S])
    k.cum = mem.at("cum", 175, [P, RT, S])
    k.kk = mem.at("kk", 191, [P, RT, S])
    k.yr_hi = mem.at("yr_hi", 94, [P, RT, S], F32R)
    k.yr_lo = mem.at("yr_lo", 110, [P, RT, S], F32R)
    k.ones_block = mem.at("ones_block", 1, [P, P])
    k.chunk_mask = mem.at("chunk_mask", 1.5, [P, P])
    k.gate = mem.at("gate", 2, [P, RW])
    k.one = mem.at("one", 4, [P, 8])
    k.merge = mem.at("merge", 153, [P, 12, P], I32)
    k.ones = mem.at("ones_full", 1, [P, P])
    k.trig_in = mem.at("trig_in", 6, [P, S])
    k.key_rot = mem.at("key_rot", 10, [P, S])
    k.wout_raw = [mem.at(f"wout_raw{j}", 191 + 4 * j, [P, D]) for j in range(4)]
    k.x1T_hi = mem.at("x1T_hi", 6, [P, KT, S], F32R)
    k.x1T_lo = mem.at("x1T_lo", 102, [P, KT, S], F32R)
    k.w1_raw = [mem.at(f"w1_raw{j}", 78 + 4 * j, [P, KT, P]) for j in range(2)]
    k.w1_hi = [mem.at(f"w1_hi{j}", 190 + 4 * j, [P, KT, P], F32R) for j in range(2)]
    k.w1_lo = [mem.at(f"w1_lo{j}", 198 + 4 * j, [P, KT, P], F32R) for j in range(2)]
    k.x1 = mem.at("x1", 38, [P, TT, D])
    k.d_ident, k.d_cols = t["ident"], t["cols"]
    with ExitStack() as ctx:
        k.dve_steps, k.pool_steps = (Steps(s) for s in sems(nc, ctx, "dve_steps", "pool_steps"))
        k.ps = ctx.enter_context(nc.psum_tensor("banks", [P, 8, HALF], F32))
        project_in(nc, mem, k, t["x"], t["w_in"], t["positions"])
        mla(nc, mem, k, t)
        clear_released(nc)
        rwkv_inputs(nc, mem, k, t)
        rwkv_chunks(nc, mem, k)
        rwkv_outputs(nc, mem, k, t)
        mix_out(nc, mem, k, t)
        ffn(nc, mem, k, t, out)


def lay_out(i):
    columns = lambda a: a.reshape(-1, P).T
    swap = np.r_[ROPE // 2:ROPE, 0:ROPE // 2]

    w_in = i["w_in"][0]
    main, pe = w_in[:, :T_PE * P], w_in[:, T_PE * P:]
    last = np.concatenate([np.zeros((D, HD), np.float32), pe, pe[:, swap]], axis=1)
    w_in = np.concatenate([main, last], axis=1)
    w_in = w_in.reshape(KT, P, SLABS, P).transpose(2, 1, 0, 3)

    w_uq = i["w_uq"][0].reshape(QLT, P, NH, HD + ROPE)
    w_uq = np.concatenate([w_uq, w_uq[..., HD + swap]], axis=-1).transpose(2, 1, 0, 3)
    w_ukv = i["w_ukv"][0].reshape(KVLT, P, NH, 2 * HD).transpose(2, 1, 0, 3)

    freq = (np.float32(10000.0) ** (-np.arange(0, ROPE, 2, dtype=np.float32) / ROPE)).astype(np.float32)
    rotary = np.zeros((P, 2), np.float32)
    rotary[HD:, 0] = np.tile(freq, 4)
    rotary[HD:HD + ROPE, 1] = 1.0
    rotary[HD + ROPE:, 1] = np.repeat([-1.0, 1.0], ROPE // 2)
    cols = np.concatenate([
        columns(i["shift_mu"][0]), np.zeros((P, SLABS - T_CQ), np.float32)]
        + [columns(i[n][0].reshape(-1)) for n in ("decay_w0", "iclr_a0", "k_k", "k_a", "r_k", "lnx_g", "lnx_b",
                                                  "q_norm_g", "kv_norm_g")] + [rotary], axis=1)

    row, col = np.arange(P)[:, None], np.arange(P)[None, :]
    rc, cc = row % CH, col % CH
    same = (row // CH) == (col // CH)
    chunk_mask = np.where(col < CH, rc < cc, rc <= cc).astype(np.float32)
    merge = [(same & (rc // b % 2 == 1) & (cc // b == rc // b - 1)) for b in (1, 2, 4, 8, 16, 32)]
    merge = np.stack([m for mm in merge for m in (mm, mm.T)], axis=1).astype(np.int32)
    return {
        "x": i["x"], "positions": i["positions"], "w_in": w_in, "cols": cols,
        "ident": np.eye(P, dtype=np.float32), "ones_block": same.astype(np.float32),
        "causal": np.where(row > col, NEG, 0.0).astype(np.float32),
        "chunk_mask": chunk_mask, "merge": merge,
        "w_uq": w_uq, "w_ukv": w_ukv,
        "w_lora": np.stack([np.pad(i["decay_w2"][0], ((0, HD), (0, 0))), np.pad(i["iclr_a2"][0], ((HD, 0), (0, 0)))],
                           axis=1), "gate_g2": i["gate_g2"][0],
        "w_out": i["w_out"][0].reshape(KT, P, D),
        "w_ffn1": i["w_ffn1"][0].reshape(KT, P, DFF // P, P).transpose(2, 1, 0, 3),
        "w_ffn2": i["w_ffn2"][0].reshape(DFF // (2 * P), 2, P, D).transpose(0, 2, 1, 3),
        "ln": np.stack([i[n][0] for n in ("ln1_g", "ln1_b", "ln2_g", "ln2_b")]),
    }


def kernel(**inputs):
    import concourse.bacc as bacc
    from concourse.bass_utils import run_bass_kernel_spmd as run

    nc = bacc.Bacc("TRN2", target_bir_lowering=False, num_devices=1)
    arrays, args = {}, {}
    for name, a in lay_out({n: np.asarray(a) for n, a in inputs.items()}).items():
        arrays[f"in_{name}"] = a = np.ascontiguousarray(a)
        args[name] = nc.dram_tensor(f"in_{name}", a.shape, mybir.dt.from_np(a.dtype), kind="ExternalInput").ap()
    out = nc.dram_tensor("layer_out", OUT_SHAPE, F32, kind="ExternalOutput").ap()
    build(nc, args, out)
    return run(nc, [arrays], core_ids=[0]).results[0]["layer_out"]
```

```python
from contextlib import ExitStack

import numpy as np

import concourse.bass as bass
from concourse import mybir

ALU = mybir.AluOpType
ACT = mybir.ActivationFunctionType
F32 = mybir.dt.float32
F32R = mybir.dt.float32r
I32 = mybir.dt.int32
AX_X = mybir.AxisListType.X

P = 128
D = 1024
S = 1024
KT = D // P
TT = S // P
HALF = 512
NH = 8
HD = 64
ROPE = 32
RW = NH * HD
RT = RW // P
QL, KVL = 384, 256
QLT, KVLT = QL // P, KVL // P
SLABS = 20
T_R, T_K, T_V, T_WA, T_G, T_CQ, T_CKV, T_PE = 0, 4, 8, 12, 13, 14, 17, 19
DFF = 4096
ALPHA = 2.0 ** 0.25
LN_EPS, RMS_EPS, GN_EPS = 1e-5, 1e-6, 64e-5
CH = 64
NC_ = S // CH
EXP_M05 = float(np.exp(-0.5))
SCALE = float((HD + ROPE) ** -0.5)
NEG = -1.0e30

C_MU = 0
C_W0 = C_MU + SLABS
C_A0 = C_W0 + RT
C_KK = C_A0 + RT
C_KA = C_KK + RT
C_RK = C_KA + RT
C_LG = C_RK + RT
C_LB = C_LG + RT
C_QG = C_LB + RT
C_KVG = C_QG + QLT
C_FREQ = C_KVG + KVLT
C_SIGN = C_FREQ + 1
C_ROT = C_SIGN + 1
NCOLS = C_ROT

KB = 1024
BASE = 16512


OUT_SHAPE = (1, S, D)


class Steps:

    def __init__(self, sem):
        self.sem, self.base, self.n = sem, 0, 0

    def on(self, eng):
        self.eng, self.base, self.n = eng, self.base + self.n, 0
        return self

    def mark(self, ins):
        ins.then_inc(self.sem, 1)
        self.n += 1
        return self.n

    def wait(self, n=None):
        self.eng.wait_ge(self.sem, self.base + (self.n if n is None else n))

    def enter(self, trip, per):
        self.start, self.per = self.base + self.n, per
        self.base, self.n = self.start + trip * per, 0

    def leave(self, trips):
        assert self.n == self.per, f"the body marks {self.n} steps"
        self.base, self.n = self.start + trips * self.per, 0


class Memory:

    def __init__(self, nc):
        self.nc = nc

    def at(self, name, kb, shape, dtype=F32):
        return self.nc.alloc_sbuf_tensor_at(name, shape, dtype, offset=BASE + int(kb * KB))


def sems(nc, ctx, *names):
    return [ctx.enter_context(nc.semaphore(n)) for n in names]


def project3(nc, outs, w_hi, w_lo, r_hi, r_lo, tiles):
    for kt in range(tiles):
        for n, (w, r) in enumerate(((w_hi, r_hi), (w_hi, r_lo), (w_lo, r_hi))):
            for b, out in enumerate(outs):
                last = nc.tensor.matmul(out, w[:, kt, :], r(kt, b), start=kt == 0 and n == 0,
                                        stop=kt == tiles - 1 and n == 2)
    return last


def split2(nc, dve, raw, hi, lo, hi_sem, count, lo_sem):
    nc.vector.tensor_copy(hi, raw).then_inc(hi_sem, 1)
    dve.wait_ge(hi_sem, count)
    nc.vector.tensor_tensor(lo, raw, hi.bitcast(F32), ALU.subtract).then_inc(lo_sem, 1)


def clear_released(nc):
    numbers = sorted(nc.released_uncleared_semaphores)
    runs = [i for i in range(len(numbers)) if i == 0 or numbers[i] != numbers[i - 1] + 1] + [len(numbers)]
    with nc.Block() as block:

        @block.sync
        def _(sp):
            for a, b in zip(runs, runs[1:]):
                sp.sem_clear(range(numbers[a], numbers[b - 1] + 1))


def head_stats(nc, out, square, ones_block, c):
    for tt in range(TT):
        last = nc.tensor.matmul(out[:, c, tt, :], square[:, tt * P:(tt + 1) * P], ones_block[:, 0:P:HD],
                                start=True, stop=True)
    return last


def project_in(nc, mem, k, x, w_in, positions):
    x_tok = mem.at("x_tok", 38 + 48, [P, TT, D])
    x_hi = mem.at("xT_hi", 118, [P, KT, S], F32R)
    x_lo = mem.at("xT_lo", 150, [P, KT, S], F32R)
    w_raw = [mem.at(f"win_raw{j}", 182 + 4 * j, [P, KT, P]) for j in range(2)]
    w_hi = [mem.at(f"win_hi{j}", 190 + 4 * j, [P, KT, P], F32R) for j in range(2)]
    w_lo = [mem.at(f"win_lo{j}", 198 + 4 * j, [P, KT, P], F32R) for j in range(2)]
    hT, cols, ident, ps = k.hT, k.cols, k.ident, k.ps
    keep = k.keep
    trips = SLABS // 2
    sums = ps[:, 4, 0:RT * TT * 2].rearrange("p (c t h) -> p c t h", c=RT, t=TT)
    first = T_CQ // 2
    early = trips - first
    ones, trig, key_rot = k.ones, k.trig_in, k.key_rot
    square = mem.at("latent_square", 14, [P, QLT, S])
    root = [mem.at(f"latent_root{n}", 26 + 4 * n, [P, S]) for n in range(2)]
    turns = mem.at("turns", 34, [P, S])
    pos = mem.at("positions", 10, [P, S], I32)
    key_square = [mem.at(f"key_square{c}", kb, [P, S]) for c, kb in enumerate((14, 18, 22, 34))]
    rms_eps = mem.at("rms_eps", 3.25, [P, 1])
    LATENTS = ((T_CQ, QLT, C_QG, QL), (T_CKV, KVLT, C_KVG, KVL))
    pe32, sw32, rot64 = slice(64, 96), slice(96, 128), slice(64, 128)
    PI2 = 2 * np.pi
    C1 = 6.28125
    C2 = float(np.float32(round((PI2 - C1) * 2 ** 20) / 2 ** 20))
    C3 = float(np.float32(PI2 - C1 - C2))
    MAGIC = 1.5 * 2.0 ** 23
    PI_BELOW = 3.1415925
    with ExitStack() as ctx:
        consts_in, cols_in, xT_ready, xhi_done, xlo_done, keep_done = sems(
            nc, ctx, "a_consts_in", "a_cols_in", "a_xT_ready", "a_xhi_done", "a_xlo_done", "a_keep_done")
        x_in = sems(nc, ctx, *(f"a_x_in{j}" for j in range(TT)))
        w_in_sem = sems(nc, ctx, "a_w_loaded0", "a_w_loaded1")
        w_split = sems(nc, ctx, "a_w_split0", "a_w_split1")
        w_whi = sems(nc, ctx, "a_w_hi0", "a_w_hi1")
        slab_mm = sems(nc, ctx, "a_slab_mm0", "a_slab_mm1")
        h_scaled = sems(nc, ctx, "a_h_scaled0", "a_h_scaled1")
        h_mixed = sems(nc, ctx, "a_h_mixed0", "a_h_mixed1")
        pos_in, init, squared, summed, sum_mm, rooted, sin_in, sin_out = sems(
            nc, ctx, "a_pos_in", "a_init", "a_squared", "a_summed", "a_sum_mm", "a_rooted", "a_sin_in", "a_sin_out")
        keys_squared, keys_summed, keys_rooted, rotated, ones_in = sems(
            nc, ctx, "a_keys_squared", "a_keys_summed", "a_keys_rooted", "a_rotated", "a_ones_in")
        block = ctx.enter_context(nc.Block())


        @block.sync
        def _(sp):
            sp.dma_start(ident[:], k.d_ident).then_inc(consts_in, 16)
            xt = x.rearrange("o (t p) d -> p (o t) d", p=P)
            for tt in range(TT):
                sp.dma_start(x_tok[:, tt, :], xt[:, tt, :]).then_inc(x_in[tt], 16)
                if tt % 4 == 3:
                    j = tt // 4
                    sp.dma_start(w_raw[j][:], w_in[2 * first + j]).then_inc(w_in_sem[j], 16)
            sp.dma_start(cols[:], k.d_cols).then_inc(cols_in, 16)
            sp.dma_start(k.ones_block[:], k.d_ones_block).then_inc(ones_in, 16)
            sp.dma_start(pos[:], positions.to_broadcast([P, S])).then_inc(pos_in, 16)

            def load(i, trip):
                for j in range(2):
                    sp.wait_ge(w_split[j], trip)
                    sp.dma_start(w_raw[j][:], w_in[2 * i + j]).then_inc(w_in_sem[j], 16)

            with sp.Fori(first + 1, trips) as i:
                load(i, i - first)
            with sp.Fori(0, first) as i:
                load(i, i + early)

        @block.tensor
        def _(pe):
            pe.wait_ge(consts_in, 16)
            for g in range(2):
                for tt in range(4):
                    pe.wait_ge(x_in[4 * g + tt], 16)
                    for kt in range(KT):
                        if g and tt == 0:
                            pe.wait_ge(xlo_done, kt + 1)
                        last = nc.tensor.transpose(ps[:, kt, tt * P:(tt + 1) * P],
                                                   x_tok[:, 4 * g + tt, kt * P:(kt + 1) * P], ident[:])
                        if tt == 3:
                            last.then_inc(xT_ready, 1)
            pe.wait_ge(xlo_done, 2 * KT)
            pe.wait_ge(xhi_done, 2 * KT)

            def pair(i, trip):
                for j in range(2):
                    pe.wait_ge(w_split[j], trip + 1)
                    last = project3(nc, [ps[:, 2 * j + b, :] for b in range(2)], w_hi[j], w_lo[j],
                                    lambda kt, b: x_hi[:, kt, b * HALF:(b + 1) * HALF],
                                    lambda kt, b: x_lo[:, kt, b * HALF:(b + 1) * HALF], KT)
                    last.then_inc(slab_mm[j], 1)

            with pe.Fori(first, trips) as i:
                pair(i, i - first)
            with pe.Fori(0, 2) as i:
                pair(i, i + early)
            pe.wait_ge(init, 1)
            for n in range(2):
                pe.wait_ge(summed, n + 1)
                for b in range(2):
                    last = nc.tensor.matmul(ps[:, 4 + 2 * n + b, :], ones[:],
                                            square[:, n, b * HALF:(b + 1) * HALF], start=True, stop=True)
                last.then_inc(sum_mm, 1)
            with pe.Fori(2, 5) as i:
                pair(i, i + early)
            pe.wait_ge(keys_squared, RT)
            pe.wait_ge(ones_in, 16)
            pe.wait_ge(rooted, 1)
            for c in range(RT):
                last = head_stats(nc, sums, key_square[c], k.ones_block, c)
            last.then_inc(keys_summed, 1)
            with pe.Fori(5, first) as i:
                pair(i, i + early)

        @block.scalar
        def _(act):
            for n in range(2 * KT):
                g, kt = divmod(n, KT)
                act.wait_ge(xT_ready, n + 1)
                nc.scalar.activation(x_hi[:, kt, g * HALF:(g + 1) * HALF], ps[:, kt, :], ACT.Copy)\
                    .then_inc(xhi_done, 1)
            act.wait_ge(keep_done, 1)

            def pair(i, trip):
                for j in range(2):
                    act.wait_ge(slab_mm[j], trip + 1)
                    nc.scalar.activation(hT[:, 2 * i + j, :], ps[:, 2 * j:2 * j + 2, :].rearrange("p b n -> p (b n)"),
                                         ACT.Identity, scale=keep[:, bass.ds(2 * i + j, 1)]).then_inc(h_scaled[j], 1)

            with act.Fori(first, trips) as i:
                pair(i, i - first)
            for n, (tile0, tiles, _, _) in enumerate(LATENTS):
                if n == 0:
                    for j in range(2):
                        act.wait_ge(h_mixed[j], early)
                else:
                    act.wait_ge(summed, 1)
                nc.scalar.activation(square[:, n:n + tiles, :], hT[:, tile0:tile0 + tiles, :], ACT.Square)\
                    .then_inc(squared, 1)
            with act.Fori(0, 2) as i:
                pair(i, i + early)
            act.wait_ge(sin_in, 1)
            nc.scalar.activation(trig[rot64, :], trig[rot64, :], ACT.Sin).then_inc(sin_out, 1)
            pair(2, 2 + early)
            for n, (_, _, _, width) in enumerate(LATENTS):
                act.wait_ge(sum_mm, n + 1)
                act.wait_ge(init, 2)
                nc.scalar.activation(root[n][:], ps[:, 4 + 2 * n:6 + 2 * n, :].rearrange("p b n -> p (b n)"), ACT.Sqrt,
                                     scale=1.0 / width, bias=rms_eps[:]).then_inc(rooted, 1)
            pair(3, 3 + early)
            for j in range(2):
                act.wait_ge(h_mixed[j], early + (T_K + RT) // 2)
            act.wait_ge(rotated, 1)
            act.wait_ge(sum_mm, 2)
            for c in range(RT):
                nc.scalar.activation(key_square[c][:], hT[:, T_K + c, :], ACT.Square,
                                     scale=cols[:, C_KK + c:C_KK + c + 1]).then_inc(keys_squared, 1)
            with act.Fori(4, 6) as i:
                pair(i, i + early)
            act.wait_ge(keys_summed, 1)
            nc.scalar.activation(k.key_norm[:], sums, ACT.Sqrt).then_inc(keys_rooted, 1)
            pair(6, 6 + early)

        @block.vector
        def _(dve):
            step = k.dve_steps.on(dve)
            nc.vector.memset(ones[:], 1.0).then_inc(init, 1)
            nc.vector.memset(rms_eps[:], RMS_EPS).then_inc(init, 1)
            def split(j, trip):
                dve.wait_ge(w_in_sem[j], 16 * (trip + 1))
                split2(nc, dve, w_raw[j][:], w_hi[j][:], w_lo[j][:], w_whi[j], trip + 1, w_split[j])

            def mix(j, i, trip):
                dve.wait_ge(h_scaled[j], trip + 1)
                flat = ps[:, 2 * j:2 * j + 2, :].rearrange("p b n -> p (b n)")
                nc.vector.scalar_tensor_tensor(hT[:, 2 * i + j, 1:S], flat[:, 0:S - 1],
                                               cols[:, bass.ds(C_MU + 2 * i + j, 1)], hT[:, 2 * i + j, 1:S],
                                               ALU.mult, ALU.add).then_inc(h_mixed[j], 1)

            def pair(i, trip):
                for j in range(2):
                    mix(j, i, trip)
                    split(j, trip + 1)

            def angles():
                dve.wait_ge(pos_in, 16)
                V, col = nc.vector, lambda c: cols[rot64, c:c + 1]
                a, u = trig[rot64, :], turns[rot64, :]
                step.mark(V.tensor_copy(a, pos[rot64, :]))
                step.wait()
                step.mark(V.tensor_scalar(a, a, col(C_FREQ), None, ALU.mult))
                step.wait()
                step.mark(V.tensor_scalar(u, a, 1.0 / PI2, MAGIC, ALU.mult, ALU.add))
                step.wait()
                step.mark(V.tensor_scalar(u, u, MAGIC, None, ALU.subtract))
                for c in (C1, C2, C3):
                    step.wait()
                    step.mark(V.scalar_tensor_tensor(a, u, -c, a, ALU.mult, ALU.add))
                step.wait()
                step.mark(V.tensor_scalar(a, a, PI_BELOW, -PI_BELOW, ALU.min, ALU.max))
                step.wait()
                step.mark(V.scalar_tensor_tensor(turns[pe32, :], trig[pe32, :], -1.0, trig[pe32, :], ALU.mult, ALU.max))
                step.wait()
                V.tensor_scalar(trig[pe32, :], turns[pe32, :], -1.0, float(np.pi / 2), ALU.mult, ALU.add)\
                    .then_inc(sin_in, 1)

            def add_squares():
                for j in range(2):
                    dve.wait_ge(h_mixed[j], early)
                for n, (_, tiles, _, _) in enumerate(LATENTS):
                    dve.wait_ge(squared, n + 1)
                    for c in range(1, tiles):
                        if c > 1:
                            step.wait()
                        ins = nc.vector.tensor_tensor(square[:, n, :], square[:, n, :], square[:, n + c, :], ALU.add)
                        if c < tiles - 1:
                            step.mark(ins)
                    ins.then_inc(summed, 1)

            def rotate_key():
                V = nc.vector
                dve.wait_ge(sin_out, 1)
                step.mark(V.tensor_scalar(trig[rot64, :], trig[rot64, :], cols[rot64, C_SIGN:C_SIGN + 1], None, ALU.mult))
                step.wait()
                step.mark(V.tensor_tensor(key_rot[pe32, :], hT[pe32, T_PE, :], trig[pe32, :], ALU.mult))
                step.mark(V.tensor_tensor(turns[pe32, :], hT[sw32, T_PE, :], trig[sw32, :], ALU.mult))
                step.wait()
                V.tensor_tensor(key_rot[pe32, :], key_rot[pe32, :], turns[pe32, :], ALU.add).then_inc(rotated, 1)

            def invert(n):
                dve.wait_ge(rooted, n + 1)
                step.mark(nc.vector.reciprocal(root[n][:], root[n][:]))

            def normalise(n):
                tile0, tiles, gain, _ = LATENTS[n]
                for c in range(tiles):
                    nc.vector.scalar_tensor_tensor(hT[:, tile0 + c, :], hT[:, tile0 + c, :],
                                                   cols[:, gain + c:gain + c + 1], root[n][:], ALU.mult, ALU.mult)

            for g in range(2):
                cut = slice(g * HALF, (g + 1) * HALF)
                for kt in range(KT):
                    dve.wait_ge(xhi_done, g * KT + kt + 1)
                    nc.vector.tensor_tensor(x_lo[:, kt, cut], ps[:, kt, :], x_hi[:, kt, cut].bitcast(F32), ALU.subtract)\
                        .then_inc(xlo_done, 1)
                split(g, 0)
            dve.wait_ge(cols_in, 16)
            nc.vector.tensor_scalar(keep[:], cols[:, C_MU:C_MU + SLABS], -1.0, 1.0, ALU.mult, ALU.add)\
                .then_inc(keep_done, 1)
            with dve.Fori(first, trips) as i:
                pair(i, i - first)
            add_squares()
            for a, b, extra in ((0, 1, angles), (1, 2, rotate_key), (2, 4, lambda: invert(0)),
                                (4, 5, lambda: (step.wait(), normalise(0), invert(1))),
                                (5, 6, lambda: (step.wait(), normalise(1)))):
                with dve.Fori(a, b) as i:
                    pair(i, i + early)
                extra()
            dve.wait_ge(keys_rooted, 1)
            step.mark(nc.vector.tensor_scalar(k.key_norm[:], k.key_norm[:], 1e-12, None, ALU.max))
            step.wait()
            step.mark(nc.vector.reciprocal(k.key_norm[:], k.key_norm[:]))
            for j in range(2):
                mix(j, first - 1, trips - 1)


def mla(nc, mem, k, t):
    hT, cols, ident, ps = k.hT, k.cols, k.ident, k.ps
    ym_hi, ym_lo = k.ym_hi, k.ym_lo
    trig = mem.at("trig", 118, [P, S])
    q_hi = [mem.at(f"q_hi{p}", 126 + 4 * p, [P, S], F32R) for p in range(2)]
    q_lo = [mem.at(f"q_lo{p}", 134 + 4 * p, [P, S], F32R) for p in range(2)]
    k_hi = [mem.at(f"k_hi{p}", 142 + 4 * p, [P, S], F32R) for p in range(2)]
    k_lo = [mem.at(f"k_lo{p}", 150 + 4 * p, [P, S], F32R) for p in range(2)]
    v_one = [mem.at(f"v_one{p}", 158 + 4 * p, [P, TT, P]) for p in range(2)]
    probs = [mem.at(f"probs{n}", 166 + 4 * n, [P, S]) for n in range(3)]
    w_uq = [mem.at(f"w_uq{p}", 178 + 1.5 * p, [P, QLT, P]) for p in range(2)]
    w_ukv = [mem.at(f"w_ukv{p}", 181 + p, [P, KVLT, P]) for p in range(2)]
    rot_a = mem.at("rot_a", 183, [P, S])
    rot_b = mem.at("rot_b", 187, [P, S])
    recip, y_full = k.att_recip, k.att_y
    att = k.att
    q_pe = mem.at("q_pe", 203, [P, S])
    ones = k.ones
    causal = mem.at("causal", 1.5, [P, P])
    causal_r = mem.at("causal_r", 2, [P, P], F32R)
    ident_r = mem.at("ident_r", 2.5, [P, P], F32R)
    top = mem.at("row_max", 3, [P, TT])
    tops = mem.at("row_max_parts", 3.25, [P, 2, TT])
    top_r = mem.at("neg_row_max_r", 3.125, [P, TT], F32R)
    A, O = (0, 1), (6, 7)
    T = ((2, 3), (4, 5))
    flat = lambda pair, rows=slice(0, P): ps[rows, pair[0]:pair[0] + 2, :].rearrange("p b n -> p (b n)")
    lo64, hi64, pe32, sw32 = slice(0, 64), slice(64, 128), slice(64, 96), slice(96, 128)
    ONE = slice(96, 97)
    TURNS = {0: ("q", None), 1: ("k", None), 2: ("v", 7), 3: (6, 5), 4: (4, 3), 5: (2, 1), 6: (0, "m")}
    S_ORDER = [x for j in sorted(TURNS) for x in TURNS[j] if type(x) is int]
    TAKES = [("q", (0, 1)), ("k", (0, 1)), ("v", (0,))]
    TAKES += [(qt, (0, 1) if qt >= TT // 2 else ((TT - 1 - qt) % 2,)) for qt in S_ORDER] + [("m", (0, 1))]
    BANKS = dict(TAKES)
    USES = [sum(b in banks for _, banks in TAKES) for b in range(2)]
    FREES = [n - 1 for n in USES]

    def nth(what, b):
        names = [name for name, _ in TAKES]
        return sum(b in banks for _, banks in TAKES[:names.index(what)])


    with ExitStack() as ctx:
        in_sem, trig_ready, key_ready, causal_rr, ones_set = sems(
            nc, ctx, "b_in", "b_trig_ready", "b_key_ready", "b_causal_r", "b_ones_set")
        q_pe_done, = sems(nc, ctx, "b_q_pe_done")
        w_in = sems(nc, ctx, "b_w_in0", "b_w_in1")
        q_hi_done, k_hi_done, rot_ready, q_ready, m_ready = sems(
            nc, ctx, "b_q_hi_done", "b_k_hi_done", "b_rot_ready", "b_q_ready",
            "b_m_ready")
        item = sems(nc, ctx, "b_item0", "b_item1")
        a_free = sems(nc, ctx, "b_a_free0", "b_a_free1")
        row_ready = sems(nc, ctx, "b_row_ready0", "b_row_ready1")
        st_ready, exp_done, pv_done, o_read, y_ready, y_done = sems(
            nc, ctx, "b_st_ready", "b_exp_done", "b_pv_done", "b_o_read", "b_y_ready", "b_y_done")
        T_FREE, PROBS_FREE, O_FREE, ATT_FREE, Y_FREE = 2, 3, 1, 1, 2
        block = ctx.enter_context(nc.Block())

        @block.sync
        def _(sp):

            def load(h, p):
                sp.dma_start(w_uq[p][:], t["w_uq"][h]).then_inc(w_in[p], 16)
                sp.dma_start(w_ukv[p][:], t["w_ukv"][h]).then_inc(w_in[p], 16)

            load(0, 0)
            sp.dma_start(causal[:], t["causal"]).then_inc(in_sem, 16)
            load(1, 1)
            with sp.Fori(1, NH // 2) as i:
                for p in range(2):
                    sp.wait_ge(item[0], USES[0] * (2 * i + p - 2) + nth("v", 0) + 1)
                    load(2 * i + p, p)

        @block.tensor
        def _(pe):
            pe.sem_inc(pv_done, PROBS_FREE)

            def take(h, what, b):
                pe.wait_ge(a_free[b], FREES[b] * h + nth(what, b))

            def q_item(h, p, i, first):
                pe.wait_ge(w_in[p], 32 * (i + 1))
                for b in range(2):
                    if not first:
                        take(h, "q", b)
                    for c in range(QLT):
                        last = nc.tensor.matmul(ps[:, b, :], w_uq[p][:, c, :],
                                                hT[:, T_CQ + c, b * HALF:(b + 1) * HALF],
                                                start=c == 0, stop=c == QLT - 1)
                    last.then_inc(item[b], 1)

            def k_item(h, p):
                pe.wait_ge(q_pe_done, h + 1)
                for b in range(2):
                    take(h, "k", b)
                    for c in range(KVLT):
                        last = nc.tensor.matmul(ps[lo64, b, :], w_ukv[p][:, c, 0:HD],
                                                hT[:, T_CKV + c, b * HALF:(b + 1) * HALF],
                                                start=c == 0, stop=c == KVLT - 1)
                    last.then_inc(item[b], 1)

            def v_item(h, p):
                take(h, "v", 0)
                for tt in range(TT):
                    for c in range(KVLT):
                        last = nc.tensor.matmul(ps[:, 0, tt * HD:(tt + 1) * HD],
                                                hT[:, T_CKV + c, tt * P:(tt + 1) * P], w_ukv[p][:, c, HD:2 * HD],
                                                start=c == 0, stop=c == KVLT - 1)
                last.then_inc(item[0], 1)

            def s_item(h, p, qt):
                if qt == S_ORDER[0]:
                    pe.wait_ge(q_ready, h + 1)
                q = q_hi[p][0:96, qt * P:(qt + 1) * P]
                for n, b in enumerate(BANKS[qt]):
                    take(h, qt, b)
                    keys = slice(n * HALF, min((n + 1) * HALF, (qt + 1) * P))
                    diag = keys.stop == (qt + 1) * P
                    width = keys.stop - keys.start
                    last = nc.tensor.matmul(ps[:, b, 0:width], q, k_hi[p][0:96, keys], start=True, stop=not diag)
                    if diag:
                        last = nc.tensor.matmul(ps[:, b, width - P:width], causal_r[:], ident_r[:], start=False, stop=True)
                    last.then_inc(item[b], 1)

            def m_item(h):
                for b in range(2):
                    take(h, "m", b)
                    if b == 0:
                        pe.wait_ge(m_ready, h + 1)
                    for n in range(4):
                        last = nc.tensor.matmul(ps[0:1, b, n * P:(n + 1) * P], top_r[:, 4 * b + n:4 * b + n + 1],
                                                ident_r[:], start=True, stop=True)
                    last.then_inc(item[b], 1)

            def st(h, p, kt):
                g = kt % 2
                pe.wait_ge(exp_done, TT * h + kt - 1 + T_FREE)
                if kt == 0:
                    for b in range(2):
                        pe.wait_ge(row_ready[b], h + 1)
                for b in range(2):
                    lo = max(kt * P, b * HALF)
                    if lo >= (b + 1) * HALF:
                        continue
                    out = ps[:, T[g][b], lo - b * HALF:HALF]
                    q = slice(lo, (b + 1) * HALF)
                    keys = slice(kt * P, (kt + 1) * P)
                    diag = lo == kt * P
                    for n, (kk, qq) in enumerate(((k_hi, q_hi), (k_hi, q_lo), (k_lo, q_hi))):
                        last = nc.tensor.matmul(out, kk[p][0:97, keys], qq[p][0:97, q], start=n == 0,
                                                stop=n == 2 and not diag)
                    if diag:
                        last = nc.tensor.matmul(out[:, 0:P], ident_r[:], causal_r[:], start=False, stop=True)
                last.then_inc(st_ready, 1)

            def pv(h, p, kt):
                pe.wait_ge(exp_done, TT * h + kt + 1 + T_FREE)
                if kt == 0:
                    pe.wait_ge(o_read, h + O_FREE)
                for b in range(2):
                    lo = max(kt * P, b * HALF)
                    if lo >= (b + 1) * HALF:
                        continue
                    last = nc.tensor.matmul(ps[:, O[b], lo - b * HALF:HALF], v_one[p][:, kt, :],
                                            probs[kt % 3][:, lo:(b + 1) * HALF], start=kt == 0,
                                            stop=kt == (3, 7)[b])
                last.then_inc(pv_done, 1)

            def sweep(h, p, i, more):
                def turn(what):
                    nh, np_ = h + 1, 1 - p
                    if what is None or not more:
                        return
                    if what == "q":
                        q_item(nh, np_, i + p, False)
                    elif what == "k":
                        k_item(nh, np_)
                    elif what == "v":
                        v_item(nh, np_)
                    elif what == "m":
                        m_item(nh)
                    else:
                        s_item(nh, np_, what)

                for kt in range(TT):
                    st(h, p, kt)
                    turn(TURNS.get(kt, (None, None))[0])
                    if kt >= 1:
                        pv(h, p, kt - 1)
                    turn(TURNS.get(kt, (None, None))[1])
                pv(h, p, TT - 1)

            q_item(0, 0, 0, True)
            k_item(0, 0)
            v_item(0, 0)
            pe.wait_ge(causal_rr, 2)
            pe.wait_ge(key_ready, 1)
            for qt in S_ORDER:
                s_item(0, 0, qt)
            m_item(0)
            pe.wait_ge(ones_set, 1)
            with pe.Fori(0, NH // 2 - 1) as i:
                for p in range(2):
                    sweep(2 * i + p, p, i, True)
            sweep(NH - 2, 0, NH // 2 - 1, True)
            sweep(NH - 1, 1, NH // 2 - 1, False)

        @block.scalar
        def _(act):
            def front(h, p, n):
                if n == 0:
                    for b in range(2):
                        act.wait_ge(item[b], USES[b] * h + nth("q", b) + 1)
                    nc.scalar.activation(q_hi[p][lo64, :], flat(A, lo64), ACT.Copy).then_inc(q_hi_done, 1)
                    if not (type(h) is int and h == 0):
                        act.wait_ge(q_ready, h)
                    nc.scalar.activation(q_pe[hi64, :], flat(A, hi64), ACT.Copy).then_inc(q_pe_done, 1)
                if n == 1:
                    for b in range(2):
                        act.wait_ge(item[b], USES[b] * h + nth("k", b) + 1)
                    nc.scalar.activation(k_hi[p][lo64, :], flat(A, lo64), ACT.Copy).then_inc(k_hi_done, 1)
                if n == 2:
                    act.wait_ge(item[0], USES[0] * h + nth("v", 0) + 1)
                    nc.scalar.activation(v_one[p][:, :, 0:HD], ps[:, 0, :].rearrange("p (t d) -> p t d", d=HD),
                                         ACT.Copy).then_inc(a_free[0], 1)
                if n == 3:
                    act.wait_ge(item[0], USES[0] * (h + 1))
                    nc.scalar.activation(q_hi[p][ONE, 0:HALF], ps[0:1, A[0], :], ACT.Copy).then_inc(row_ready[0], 1)

            def sweep(h, p, more):
                for kt in range(TT):
                    act.wait_ge(st_ready, TT * h + kt + 1)
                    act.wait_ge(pv_done, TT * h + kt - 2 + PROBS_FREE)
                    nc.scalar.activation(probs[kt % 3][:, kt * P:S], flat(T[kt % 2])[:, kt * P:S], ACT.Exp,
                                         scale=SCALE).then_inc(exp_done, 1)
                    if more and kt == 0:
                        front(h + 1, 1 - p, 0)
                    if more and kt == 1:
                        front(h + 1, 1 - p, 1)
                    if more and kt == 2:
                        front(h + 1, 1 - p, 2)
                    if more and kt == 6:
                        front(h + 1, 1 - p, 3)
                act.wait_ge(pv_done, TT * (h + 1) + PROBS_FREE)
                act.wait_ge(y_ready, h + ATT_FREE)
                nc.scalar.activation(att[:], flat(O), ACT.Copy).then_inc(o_read, 1)

            act.sem_inc(exp_done, T_FREE)
            for n in range(4):
                front(0, 0, n)
            with act.Fori(0, NH // 2 - 1) as i:
                for p in range(2):
                    sweep(2 * i + p, p, True)
            sweep(NH - 2, 0, True)
            sweep(NH - 1, 1, False)

        @block.vector
        def _(dve):
            step = k.dve_steps.on(dve)
            V = nc.vector
            for p in range(2):
                step.mark(V.tensor_copy(k_hi[p][pe32, :], k.key_rot[pe32, :]))
            step.wait()
            for p in range(2):
                last = V.tensor_tensor(k_lo[p][pe32, :], k.key_rot[pe32, :], k_hi[p][pe32, :].bitcast(F32), ALU.subtract)
            last.then_inc(key_ready, 1)
            dve.wait_ge(in_sem, 16)
            V.tensor_copy(causal_r[:], causal[:]).then_inc(causal_rr, 1)
            V.tensor_copy(ident_r[:], ident[:]).then_inc(causal_rr, 1)

            def low_part(lo, hi):
                for b in range(2):
                    cut = slice(b * HALF, (b + 1) * HALF)
                    V.tensor_tensor(lo[lo64, cut], ps[lo64, b, :], hi[lo64, cut].bitcast(F32), ALU.subtract)\
                        .then_inc(a_free[b], 1)

            def front_q(h, p, first=False):
                dve.wait_ge(q_hi_done, h + 1)
                low_part(q_lo[p], q_hi[p])
                dve.wait_ge(q_pe_done, h + 1)
                if first:
                    dve.wait_ge(trig_ready, 1)
                else:
                    dve.wait_ge(q_ready, h)
                V.tensor_tensor(rot_a[pe32, :], q_pe[pe32, :], trig[pe32, :], ALU.mult).then_inc(rot_ready, 1)
                V.tensor_tensor(rot_b[pe32, :], q_pe[sw32, :], trig[sw32, :], ALU.mult).then_inc(rot_ready, 1)

            def front_k(h, p):
                dve.wait_ge(k_hi_done, h + 1)
                low_part(k_lo[p], k_hi[p])

            def maxima(h, p):
                for qt in S_ORDER:
                    for n, b in enumerate(BANKS[qt]):
                        dve.wait_ge(item[b], USES[b] * h + nth(qt, b) + 1)
                        width = min(HALF, (qt + 1) * P - n * HALF)
                        V.reduce_max(tops[:, n, qt:qt + 1], ps[:, b, 0:width], AX_X).then_inc(a_free[b], 1)
                for b in range(2):
                    dve.wait_ge(a_free[b], FREES[b] * (h + 1))
                step.mark(V.tensor_tensor(top[:], tops[:, 0, :], tops[:, 1, :], ALU.max))
                step.wait()
                V.tensor_scalar(top_r[:], top[:], -1.0, None, ALU.mult).then_inc(m_ready, 1)
                dve.wait_ge(item[1], USES[1] * (h + 1))
                V.tensor_copy(q_hi[p][ONE, HALF:S], ps[0:1, A[1], :]).then_inc(row_ready[1], 1)

            def invert(h, n):
                if n == 0:
                    dve.wait_ge(o_read, h + 1 + O_FREE)
                cut = (slice(0, S // 4), slice(S // 4, S))[n]
                step.mark(V.reciprocal(recip[lo64, cut], att[hi64, cut]))

            def leave(h, p):
                step.wait()
                dve.wait_ge(y_done, h - 1 + Y_FREE)
                V.tensor_tensor(y_full[64 * p:64 * p + 64, :], att[lo64, :], recip[lo64, :], ALU.mult)\
                    .then_inc(y_ready, 1)

            step.mark(V.memset(tops[:], NEG))
            step.wait()
            dve.sem_inc(o_read, O_FREE)
            dve.sem_inc(y_ready, ATT_FREE)
            for h in range(2):
                front_q(h, h, h == 0)
                front_k(h, h)
                maxima(h, h)
            with dve.Fori(0, NH // 2 - 1) as i:
                step.enter(i, 6)
                for p in range(2):
                    front_q(2 * i + 2 + p, p)
                    invert(2 * i + p, 0)
                    front_k(2 * i + 2 + p, p)
                    invert(2 * i + p, 1)
                    leave(2 * i + p, p)
                    maxima(2 * i + 2 + p, p)
                step.leave(NH // 2 - 1)
            for n in range(2):
                invert(NH - 2, n)
            leave(NH - 2, 0)

        @block.gpsimd
        def _(pool):
            step = k.pool_steps.on(pool)
            G = nc.gpsimd

            def rotate(h, p):
                pool.wait_ge(rot_ready, 2 * h + 2)
                step.mark(G.tensor_tensor(q_hi[p][pe32, :], rot_a[pe32, :], rot_b[pe32, :], ALU.add))
                step.mark(G.tensor_tensor(rot_a[pe32, :], rot_a[pe32, :], rot_b[pe32, :], ALU.add))
                step.wait()
                G.tensor_tensor(q_lo[p][pe32, :], rot_a[pe32, :], q_hi[p][pe32, :].bitcast(F32), ALU.subtract)\
                    .then_inc(q_ready, 1)

            def store(h, p, i):
                rows = slice(64 * p, 64 * p + 64)
                pool.wait_ge(y_ready, h + 1 + ATT_FREE)
                step.mark(G.tensor_tensor(ym_hi[rows, i, :], y_full[rows, :], ones[rows, 0:1].to_broadcast([64, S]),
                                          ALU.mult))
                step.wait()
                G.tensor_tensor(ym_lo[rows, i, :], y_full[rows, :], ym_hi[rows, i, :].bitcast(F32), ALU.subtract)\
                    .then_inc(y_done, 1)

            pool.sem_inc(y_done, Y_FREE)
            G.tensor_copy(trig[hi64, :], k.trig_in[hi64, :]).then_inc(trig_ready, 1)
            pool.wait_ge(trig_ready, 1)
            for p in range(2):
                G.memset(k_hi[p][ONE, :].bitcast(F32), 1.0)
                G.memset(k_lo[p][ONE, :].bitcast(F32), 0.0)
                last = G.memset(q_lo[p][ONE, :].bitcast(F32), 0.0)
            step.mark(last)
            step.wait()
            for p in range(2):
                last = G.memset(v_one[p][:, :, HD:P], 1.0)
            last.then_inc(ones_set, 1)
            pool.wait_ge(ones_set, 1)
            for h in range(2):
                rotate(h, h)
            with pool.Fori(0, NH // 2 - 1) as i:
                step.enter(i, 6)
                for p in range(2):
                    rotate(2 * i + 2 + p, p)
                    store(2 * i + p, p, i)
                step.leave(NH // 2 - 1)
            store(NH - 2, 0, NH // 2 - 1)


def last_head_leaves(nc, k, step):
    V, rows, tile = nc.vector, slice(HD, P), RT - 1
    step.mark(V.reciprocal(k.att_recip[0:HD, :], k.att[rows, :]))
    step.wait()
    step.mark(V.tensor_tensor(k.att_y[rows, :], k.att[0:HD, :], k.att_recip[0:HD, :], ALU.mult))
    step.wait()
    step.mark(V.tensor_copy(k.ym_hi[rows, tile, :], k.att_y[rows, :]))
    step.wait()
    step.mark(V.tensor_tensor(k.ym_lo[rows, tile, :], k.att_y[rows, :], k.ym_hi[rows, tile, :].bitcast(F32), ALU.subtract))



def widened(stats, wide, c):
    src = stats[:, c, :, :].rearrange("p t h -> p (t h)").rearrange("p (a o) -> p a o", o=1)
    return wide[:].rearrange("p (a d) -> p a d", d=HD), src.to_broadcast([P, 2 * TT, HD])


def spread_stats(nc, outs, wide, ident):
    for tt in range(TT):
        at = tt % 4 * P
        last = nc.tensor.matmul(outs[tt // 4][:, at:at + P], wide[:, tt * P:(tt + 1) * P], ident[:], start=True, stop=True)
    return last


def rwkv_inputs(nc, mem, k, t):
    hT, cols, ps, ident = k.hT, k.cols, k.ps, k.ident
    w_lora = mem.at("w_lora", 94, [P, 2, RW])
    reset = mem.at("reset", 98, [P, S])
    logw = [mem.at(f"logw{j}", 102 + 4 * j, [P, S]) for j in range(2)]
    rate = [mem.at(f"rate{j}", 110 + 4 * j, [P, S]) for j in range(2)]
    norm = k.key_norm
    wide = [mem.at(f"norm_wide{c}", 118 + 4 * c, [P, S]) for c in range(RT)]
    keep_a = mem.at("keep_a", 4.25, [P, RT])
    spare = mem.at("spare", 4.75, [P, 1])
    beta, cum, kk = k.beta, k.cum, k.kk
    flat = lambda b: ps[:, b:b + 2, :].rearrange("p b n -> p (b n)")
    SPREAD = (6, 4)
    with ExitStack() as ctx:
        loaded, tanh_done, z_mm, a_mm, logw_done, rate_done, spread, cum_done = sems(
            nc, ctx, "c_loaded", "c_tanh", "c_z_mm", "c_a_mm", "c_logw", "c_rate", "c_spread", "c_cum")
        kk_done, wide_done, blend_done, later_in = sems(nc, ctx, "c_kk_done", "c_wide", "c_blend", "c_later_in")
        keep_done, key_rate = sems(nc, ctx, "c_keep", "c_key_rate")
        block = ctx.enter_context(nc.Block())

        @block.sync
        def _(sp):
            sp.dma_start(w_lora[:], t["w_lora"]).then_inc(loaded, 16)
            sp.dma_start(k.gate[:], t["gate_g2"]).then_inc(later_in, 16)
            sp.dma_start(k.chunk_mask[:], t["chunk_mask"]).then_inc(later_in, 16)
            sp.dma_start(k.merge[:], t["merge"]).then_inc(later_in, 16)
            sp.wait_ge(later_in, 48)

        @block.tensor
        def _(pe):
            def lora(c):
                for n, (done, free) in enumerate(((z_mm, logw_done), (a_mm, rate_done))):
                    if c:
                        pe.wait_ge(free, c)
                    for b in range(2):
                        last = nc.tensor.matmul(ps[:, 2 * n + b, :], w_lora[:, n, c * P:(c + 1) * P],
                                                hT[:, T_WA, b * HALF:(b + 1) * HALF], start=True, stop=True)
                    last.then_inc(done, 1)

            pe.wait_ge(loaded, 16)
            pe.wait_ge(tanh_done, 1)
            lora(0)
            for c in range(RT):
                if c < RT - 1:
                    lora(c + 1)
                pe.wait_ge(wide_done, c + 1)
                if c >= 2:
                    pe.wait_ge(kk_done, c - 1)
                b = SPREAD[c % 2]
                spread_stats(nc, [ps[:, b, :], ps[:, b + 1, :]], wide[c], ident).then_inc(spread, 1)

        @block.scalar
        def _(act):
            nc.scalar.activation(hT[0:64, T_WA, :], hT[0:64, T_WA, :], ACT.Tanh).then_inc(tanh_done, 1)
            for c in range(RT):
                act.wait_ge(z_mm, c + 1)
                if c >= 2:
                    act.wait_ge(cum_done, c - 1)
                nc.scalar.activation(logw[c % 2][:], flat(0), ACT.Sigmoid, bias=cols[:, C_W0 + c:C_W0 + c + 1])\
                    .then_inc(logw_done, 1)
                act.wait_ge(a_mm, c + 1)
                nc.scalar.activation(beta[:, c, :], flat(2), ACT.Sigmoid, bias=cols[:, C_A0 + c:C_A0 + c + 1])\
                    .then_inc(rate_done, 1)
                act.wait_ge(rate_done, c + 1)
                act.wait_ge(keep_done, 1)
                if c >= 2:
                    act.wait_ge(blend_done, c - 1)
                nc.scalar.activation(rate[c % 2][:], beta[:, c, :], ACT.Identity, scale=cols[:, C_KA + c:C_KA + c + 1],
                                     bias=keep_a[:, c:c + 1]).then_inc(key_rate, 1)
            nc.scalar.activation(hT[:, T_G, :], hT[:, T_G, :], ACT.Sigmoid)
            nc.scalar.activation(spare[:], keep_a[:, 0:1], ACT.Exp)

        @block.vector
        def _(dve):
            V = nc.vector
            step = k.dve_steps.on(dve)
            V.memset(k.one[:], 1.0)
            step.mark(V.memset(reset[:], 1.0))
            step.wait()
            V.memset(reset[:].rearrange("p (n c) -> p n c", c=CH)[:, :, 0:1], 0.0)
            V.tensor_scalar(keep_a[:], cols[:, C_KA:C_KA + RT], -1.0, 1.0, ALU.mult, ALU.add).then_inc(keep_done, 1)
            out, src = widened(norm, wide[0], 0)
            V.tensor_copy(out, src).then_inc(wide_done, 1)
            last_head_leaves(nc, k, step)

            def decay_sum(c):
                dve.wait_ge(logw_done, c + 1)
                V.tensor_tensor_scan(cum[:, c, :], reset[:], logw[c % 2][:], 0.0, ALU.mult, ALU.add).then_inc(cum_done, 1)

            def keys(c):
                dve.wait_ge(rate_done, c + 1)
                dve.wait_ge(key_rate, c + 1)
                dve.wait_ge(spread, c + 1)
                V.scalar_tensor_tensor(kk[:, c, :], hT[:, T_K + c, :], cols[:, C_KK + c:C_KK + c + 1],
                                       flat(SPREAD[c % 2]), ALU.mult, ALU.mult).then_inc(kk_done, 1)
                dve.wait_ge(kk_done, c + 1)
                V.scalar_tensor_tensor(beta[:, c, :], beta[:, c, :], -1.0, kk[:, c, :], ALU.mult, ALU.mult)

            decay_sum(0)
            for c in range(RT):
                if c < RT - 1:
                    decay_sum(c + 1)
                keys(c)
            V.tensor_tensor(hT[:, T_K + RT - 1, :], hT[:, T_K + RT - 1, :], rate[(RT - 1) % 2][:], ALU.mult)

        @block.gpsimd
        def _(pool):
            def blend(c):
                pool.wait_ge(key_rate, c + 1)
                pool.wait_ge(kk_done, c + 1)
                nc.gpsimd.tensor_tensor(hT[:, T_K + c, :], hT[:, T_K + c, :], rate[c % 2][:], ALU.mult)\
                    .then_inc(blend_done, 1)

            for c in range(1, RT):
                pool.wait_ge(wide_done, c)
                out, src = widened(norm, wide[c], c)
                nc.gpsimd.tensor_copy(out, src).then_inc(wide_done, 1)
            for c in range(RT - 1):
                blend(c)


def rwkv_chunks(nc, mem, k):
    ident, ps = k.ident, k.ps
    hT, cum, kk_all, beta, mask, merge = k.hT, k.cum, k.kk, k.beta, k.chunk_mask, k.merge
    at = [94.0]

    def new(name, shape, dtype=F32, copies=1):
        out = []
        size = -(-int(np.prod(shape[1:])) * 4 // 32) * 32 / KB
        for n in range(copies):
            out.append(mem.at(f"{name}{n}", at[0], shape, dtype))
            at[0] += size
        return out if copies > 1 else out[0]

    pair = [P, RT, P]
    decay = new("decay", [P, RT, CH + 1], copies=2)
    undecay = new("undecay", [P, RT, CH], copies=2)
    bk = new("bk_chunk", [P, RT, 2, CH], copies=2)
    ar = new("ar_chunk", [P, RT, 2, CH], copies=2)
    v_st = new("v_static", [P, RT, CH], copies=2)
    scores = new("scores", [P, 2, RT, P], copies=2)
    inv_t = new("inverse_t", pair, copies=2)
    bk_tok = new("bk_tok", pair, copies=2)
    uv = new("u_v", [P, 2, RT, CH], copies=2)
    sv = new("s_v", [P, 2, RT, CH], copies=2)
    am = new("a_m", [P, 2, RT, CH], copies=2)
    rho = new("rho", [P, 2, RT, CH], copies=2)
    end = new("end_decay", [64, 2, RT], copies=2)
    low_t = new("lower_t", pair, copies=2)
    inv = new("inverse", pair, copies=2)
    prod = new("product", pair)
    rhs = mem.at("rhs", 38 + 4 * T_WA, [P, RT, CH])
    state_sum = new("state_sum", [64, 2, RT, CH])
    assert at[0] <= 153, at
    LEVELS = 6
    lo, hi = slice(0, 64), slice(64, P)
    half = lambda p: slice(64 * p, 64 * p + 64)
    grp = lambda g: slice(2 * g, 2 * g + 2)
    B_SA, B_RHS = 0, 1
    B_T1, B_X, B_XT = (2, 3), (4, 5), (6, 7)
    B_BKT, B_V = 0, 1
    L_SCORES, L_LOW = 4, 5
    view = lambda bank, n=P, rows=slice(0, P), cols=2: ps[rows, bank, 0:cols * n].rearrange("p (c n) -> p c n", n=n)

    with ExitStack() as ctx:
        exps, bk_ready, x_reset, ar_ready, scores_mm, tr_done, sc_ready, low_ready, am_ready, tok_ready, init = sems(
            nc, ctx, "d_exps", "d_bk_ready", "d_x_reset", "d_ar_ready", "d_scores_mm", "d_tr_done", "d_sc_ready",
            "d_low_ready", "d_am_ready", "d_tok_ready", "d_init")
        t1_mm = sems(nc, ctx, "d_t1_mm0", "d_t1_mm1")
        t1_out = sems(nc, ctx, "d_t1_out0", "d_t1_out1")
        x_mm = sems(nc, ctx, "d_x_mm0", "d_x_mm1")
        xt_mm = sems(nc, ctx, "d_xt_mm0", "d_xt_mm1")
        x_up = sems(nc, ctx, "d_x_up0", "d_x_up1")
        xt_up = sems(nc, ctx, "d_xt_up0", "d_xt_up1")
        rhs_mm, rhs_ready, sa_mm, sa_ready, s_mm, state_ready, y_mm, y_out, passed, v_ready = sems(
            nc, ctx, "d_rhs_mm", "d_rhs_ready", "d_sa_mm", "d_sa_ready", "d_s_mm", "d_state_ready", "d_y_mm",
            "d_y_out", "d_passed", "d_v_ready")
        LOOPS = NC_ // 2 - 1
        SLOTS_FREE, Y_FREE = 2, 1
        block = ctx.enter_context(nc.Block())

        def stages(body, eng, enter=None, leave=None):
            body(0, 0, False, True)
            with eng.Fori(0, LOOPS) as i:
                if enter:
                    enter(i)
                body(2 * i + 1, 1, True, True)
                body(2 * i + 2, 0, True, True)
                if leave:
                    leave(LOOPS)
            body(NC_ - 1, 1, True, False)

        @block.tensor
        def _(pe):
            mm = nc.tensor.matmul

            def rhs_step(n, q):
                pe.wait_ge(am_ready, n + 1)
                pe.wait_ge(state_ready, n + 1)
                for c in range(RT):
                    for p in range(2):
                        last = mm(ps[half(p), B_RHS, c * CH:(c + 1) * CH], am[q][:, p, c, :], sv[q][:, p, c, :],
                                  start=True, stop=True)
                last.then_inc(rhs_mm, 1)

            def sa_step(n, q):
                pe.wait_ge(rhs_ready, n + 1)
                for g in range(2):
                    pe.wait_ge(xt_up[g], LEVELS * (n + 1))
                for c in range(RT):
                    last = mm(ps[:, B_SA, c * CH:(c + 1) * CH], inv_t[q][:, c, :], rhs[:, c, :], start=True, stop=True)
                last.then_inc(sa_mm, 1)

            def state_step(n, q):
                pe.wait_ge(sa_ready, n + 1)
                for p in range(2):
                    for c in range(RT):
                        last = mm(ps[lo, B_SA, (p * RT + c) * CH:(p * RT + c + 1) * CH], bk_tok[q][:, c, half(p)],
                                  uv[q][:, p, c, :], start=True, stop=True)
                last.then_inc(s_mm, 1)

            def y_step(n, q):
                for c in range(RT):
                    for p in range(2):
                        out = ps[half(p), B_RHS, c * CH:(c + 1) * CH]
                        mm(out, sv[q][:, p, c, :], rho[q][:, p, c, :], start=True, stop=False)
                        last = mm(out, uv[q][:, p, c, :], scores[q][:, p, c, CH:P], start=False, stop=True)
                last.then_inc(y_mm, 1)

            def scores_step(m, q):
                pe.wait_ge(bk_ready, m + 1)
                pe.wait_ge(ar_ready, m + 1)
                if not (type(m) is int and m == 0):
                    pe.wait_ge(y_out, m - 1 + Y_FREE)
                    pe.wait_ge(state_ready, m)
                for c in range(RT):
                    for p in range(2):
                        last = mm(ps[:, p, c * P:(c + 1) * P], bk[q][half(p), c, :, :].rearrange("p a t -> p (a t)"),
                                  ar[q][half(p), c, :, :].rearrange("p a t -> p (a t)"), start=True, stop=True)
                last.then_inc(scores_mm, 1)

            def transposes(m, q):
                pe.wait_ge(sc_ready, m + 1)
                for c in range(RT):
                    nc.tensor.transpose(ps[:, B_BKT, c * P:(c + 1) * P],
                                        bk[q][:, c, :, :].rearrange("p a t -> p (a t)"), ident[:])
                for c in range(RT):
                    last = nc.tensor.transpose(ps[lo, B_V, c * P:(c + 1) * P], v_st[q][:, c, :], ident[:])
                last.then_inc(tr_done, 1)

            def stage(m, q, chain, ahead):
                n, qn = m - 1, 1 - q
                pe.wait_ge(low_ready, m + 1)
                for g in range(2):
                    for c in range(2):
                        last = nc.tensor.transpose(ps[:, B_T1[g], c * P:(c + 1) * P], low_t[q][:, 2 * g + c, :], ident[:])
                    last.then_inc(t1_mm[g], 1)
                if chain:
                    pe.wait_ge(v_ready, m + 1)
                    rhs_step(n, qn)
                for l in range(1, LEVELS):
                    for g in range(2):
                        pe.wait_ge(x_up[g], (LEVELS - 1) * m + l)
                        for c in range(2):
                            last = mm(ps[:, B_T1[g], c * P:(c + 1) * P], low_t[q][:, 2 * g + c, :], inv[q][:, 2 * g + c, :],
                                      start=True, stop=True)
                        last.then_inc(t1_mm[g], 1)
                    if chain and l == 1:
                        pe.wait_ge(tok_ready, m + 1)
                        sa_step(n, qn)
                    if chain and l == 2:
                        state_step(n, qn)
                    if chain and l == 3:
                        y_step(n, qn)
                    if ahead and l == L_SCORES:
                        scores_step(m + 1, 1 - q)
                    for g in range(2):
                        pe.wait_ge(t1_out[g], (LEVELS - 1) * m + l)
                        pe.wait_ge(xt_up[g], LEVELS * m + l)
                        if l < LEVELS - 1:
                            for c in range(2):
                                last = mm(ps[:, B_X[g], c * P:(c + 1) * P], inv_t[q][:, 2 * g + c, :], prod[:, 2 * g + c, :],
                                          start=True, stop=True)
                            last.then_inc(x_mm[g], 1)
                        for c in range(2):
                            last = mm(ps[:, B_XT[g], c * P:(c + 1) * P], prod[:, 2 * g + c, :], inv_t[q][:, 2 * g + c, :],
                                      start=True, stop=True)
                        last.then_inc(xt_mm[g], 1)
                if ahead:
                    transposes(m + 1, 1 - q)

            pe.sem_inc(y_mm, SLOTS_FREE)
            scores_step(0, 0)
            transposes(0, 0)
            stages(stage, pe)
            n, q = NC_ - 1, 1
            pe.wait_ge(y_out, n + Y_FREE)
            rhs_step(n, q)
            sa_step(n, q)
            state_step(n, q)
            y_step(n, q)

        @block.scalar
        def _(act):
            A = nc.scalar.activation

            def exp_step(m, q):
                if not (type(m) is int and m < 2):
                    act.wait_ge(ar_ready, m - 1)
                    act.wait_ge(bk_ready, m - 1)
                A(decay[q][:, :, 1:CH + 1], cum[:, :, bass.ds(m * CH, CH)], ACT.Exp, scale=-EXP_M05)
                A(undecay[q][:], cum[:, :, bass.ds(m * CH, CH)], ACT.Exp, scale=EXP_M05).then_inc(exps, 1)

            def u_step(n, q):
                act.wait_ge(sa_mm, n + 1)
                for p in range(2):
                    last = A(uv[q][lo, p, :, :], view(B_SA, CH, half(p), RT), ACT.Copy)
                last.then_inc(sa_ready, 1)

            def y_leave(n, q):
                act.wait_ge(y_mm, n + 1 + SLOTS_FREE)
                A(cum[:, :, bass.ds(n * CH, CH)], view(B_RHS, CH, cols=RT), ACT.Copy).then_inc(y_out, 1)

            def rows_step(m, q):
                act.wait_ge(y_mm, m - 1 + SLOTS_FREE)
                act.wait_ge(ar_ready, m + 1)
                for p in range(2):
                    A(am[q][lo, p, :, :], ar[q][half(p), :, 0, :], ACT.Copy)
                    A(rho[q][lo, p, :, :], ar[q][half(p), :, 1, :], ACT.Copy)
                    A(end[q][:, p, :], decay[q][half(p), :, CH], ACT.Copy)

            def low_step(m, q):
                act.wait_ge(sc_ready, m + 1)
                for p in range(2):
                    last = A(low_t[q][half(p), :, half(p)], scores[q][lo, p, :, 0:CH], ACT.Copy)
                last.then_inc(low_ready, 1)

            def tokens_step(m, q):
                act.wait_ge(tr_done, m + 1)
                v_tok = ps[lo, B_V, :].rearrange("p (c a d) -> p a c d", a=2, d=HD)
                A(sv[q][hi, :, :, :], v_tok, ACT.Copy).then_inc(v_ready, 1)
                A(bk_tok[q][:], view(B_BKT, cols=RT), ACT.Copy).then_inc(tok_ready, 1)
                act.wait_ge(v_ready, m + 1)
                A(uv[q][hi, :, :, :], sv[q][hi, :, :, :], ACT.Copy)
                A(am[q][hi, :, :, :].rearrange("p a c t -> p (a c) t"),
                  scores[q][hi, :, :, 0:CH].rearrange("p a c t -> p (a c) t"), ACT.Copy).then_inc(am_ready, 1)

            def stage(m, q, chain, ahead):
                n, qn = m - 1, 1 - q
                for l in range(1, LEVELS):
                    for g in range(2):
                        act.wait_ge(t1_mm[g], LEVELS * m + l + 1)
                        A(prod[:, grp(g), :], view(B_T1[g]), ACT.Copy).then_inc(t1_out[g], 1)
                    if chain and l == 1:
                        u_step(n, qn)
                    if ahead and l == 1:
                        exp_step(m + 1, 1 - q)
                    if chain and l == 3:
                        y_leave(n, qn)
                    if ahead and l == L_SCORES:
                        rows_step(m + 1, 1 - q)
                    if ahead and l == L_LOW:
                        low_step(m + 1, 1 - q)
                        tokens_step(m + 1, 1 - q)

            exp_step(0, 0)
            act.wait_ge(init, 1)
            rows_step(0, 0)
            low_step(0, 0)
            tokens_step(0, 0)
            stages(stage, act)
            u_step(NC_ - 1, 1)
            y_leave(NC_ - 1, 1)

        @block.vector
        def _(dve):
            V = nc.vector
            step = k.dve_steps.on(dve)

            def ar_step(m, q):
                if not (type(m) is int and m < 2):
                    dve.wait_ge(scores_mm, m - 1)
                    dve.wait_ge(am_ready, m - 1)
                dve.wait_ge(exps, m + 1)
                now = bass.ds(m * CH, CH)
                V.tensor_tensor(ar[q][:, :, 0, :], kk_all[:, :, now], decay[q][:, :, 0:CH], ALU.mult)
                V.tensor_tensor(ar[q][:, :, 1, :], hT[:, T_R:T_R + RT, now], decay[q][:, :, 1:CH + 1], ALU.mult)\
                    .then_inc(ar_ready, 1)

            def rhs_out(n, q):
                dve.wait_ge(rhs_mm, n + 1)
                V.tensor_copy(rhs[:], view(B_RHS, CH, cols=RT)).then_inc(rhs_ready, 1)

            def state_out(n, q):
                dve.wait_ge(s_mm, n + 1)
                flat = lambda x: x.rearrange("p a c d -> p (a c) d")
                step.mark(V.tensor_tensor(flat(state_sum[:]), flat(sv[q][lo, :, :, :]), view(B_SA, CH, lo, 2 * RT), ALU.add))
                step.wait()
                V.tensor_tensor(flat(sv[1 - q][lo, :, :, :]), flat(state_sum[:]),
                                end[q][:].rearrange("p a (c o) -> p (a c) o", o=1).to_broadcast([64, 2 * RT, CH]),
                                ALU.mult).then_inc(state_ready, 1)

            def wait_alone(sem, value):
                dve.wait_ge(sem, value).then_inc(passed, 1)

            def merged(x, l, transposed, new, g):
                m01 = merge[:, 2 * l + transposed:2 * l + transposed + 1, :].to_broadcast([P, 2, P])
                return V.copy_predicated(x[:, grp(g), :], m01, new)

            def mask_step(m, q):
                dve.wait_ge(scores_mm, m + 1)
                dve.wait_ge(y_mm, m - 1 + SLOTS_FREE)
                for p in range(2):
                    last = V.tensor_tensor(scores[q][:, p, :, :], view(p, cols=RT),
                                           mask[:].rearrange("p (o n) -> p o n", o=1).to_broadcast([P, RT, P]), ALU.mult)
                last.then_inc(sc_ready, 1)

            def stage(m, q, chain, ahead):
                n, qn = m - 1, 1 - q
                wait_alone(x_reset, m + 1)
                wait_alone(low_ready, m + 1)
                for g in range(2):
                    merged(inv_t[q], 0, 1, low_t[q][:, grp(g), :], g).then_inc(xt_up[g], 1)
                for g in range(2):
                    wait_alone(t1_mm[g], LEVELS * m + 1)
                    merged(inv[q], 0, 0, view(B_T1[g]), g).then_inc(x_up[g], 1)
                if chain:
                    rhs_out(n, qn)
                for l in range(1, LEVELS):
                    for g in range(2):
                        if l < LEVELS - 1:
                            wait_alone(x_mm[g], (LEVELS - 2) * m + l)
                            merged(inv[q], l, 0, view(B_X[g]), g).then_inc(x_up[g], 1)
                        wait_alone(xt_mm[g], (LEVELS - 1) * m + l)
                        merged(inv_t[q], l, 1, view(B_XT[g]), g).then_inc(xt_up[g], 1)
                    if chain and l == 2:
                        state_out(n, qn)
                    if ahead and l == 2:
                        ar_step(m + 1, 1 - q)
                    if ahead and l == L_SCORES:
                        mask_step(m + 1, 1 - q)

            for q in range(2):
                step.mark(V.memset(decay[q][:, :, 0:1], 1.0))
            step.wait()
            ar_step(0, 0)
            for q in range(2):
                V.memset(rho[q][hi, :, :, :], 0.0)
            V.memset(sv[0][lo, :, :, :], 0.0).then_inc(state_ready, 1)
            V.memset(low_t[0][:], 0.0)
            V.memset(low_t[1][:], 0.0).then_inc(init, 1)
            mask_step(0, 0)
            stages(stage, dve, lambda i: step.enter(i, 2), step.leave)
            rhs_out(NC_ - 1, 1)
            state_out(NC_ - 1, 1)

        @block.gpsimd
        def _(pool):
            G = nc.gpsimd

            def bk_step(m, q):
                if not (type(m) is int and m < 2):
                    pool.wait_ge(tr_done, m - 1)
                pool.wait_ge(exps, m + 1)
                now = bass.ds(m * CH, CH)
                G.tensor_tensor(bk[q][:, :, 0, :], beta[:, :, now], undecay[q][:], ALU.mult)
                G.tensor_tensor(bk[q][:, :, 1, :], hT[:, T_K:T_K + RT, now], undecay[q][:], ALU.mult)
                G.tensor_copy(v_st[q][:], hT[:, T_V:T_V + RT, now]).then_inc(bk_ready, 1)

            def stage(m, q, chain, ahead):
                if chain:
                    pool.wait_ge(y_mm, m - 1 + SLOTS_FREE)
                eye = ident[:].rearrange("p (o n) -> p o n", o=1).to_broadcast([P, RT, P])
                one = k.one[:, 0:1].rearrange("p (a b) -> p a b", a=1).to_broadcast([P, RT, P])
                G.tensor_tensor(inv_t[q][:], eye, one, ALU.mult)
                G.tensor_tensor(inv[q][:], eye, one, ALU.mult).then_inc(x_reset, 1)
                if ahead:
                    bk_step(m + 1, 1 - q)

            pool.sem_inc(y_out, Y_FREE)
            bk_step(0, 0)
            stages(stage, pool)


def rwkv_outputs(nc, mem, k, t):
    hT, cols, ps, y, ones_block, ident = k.hT, k.cols, k.ps, k.cum, k.ones_block, k.ident
    square = [mem.at(f"dev_square{j}", 126 + 4 * j, [P, S]) for j in range(2)]
    dot = [mem.at(f"bonus{j}", 134 + 4 * j, [P, S]) for j in range(RT)]
    full = [mem.at(f"yr_full{j}", 150 + 4 * j, [P, S]) for j in range(2)]
    scale = mem.at("gn_scale", 158, [P, RT, TT, 2])
    gn_eps = mem.at("gn_eps", 4.5, [P, 1])
    flat = lambda b: ps[:, b:b + 2, :].rearrange("p b n -> p (b n)")
    MEAN, DOT, VAR = 0, 2, 4
    SPREAD, GATE = (0, 2), (4, 6)
    var = ps[:, VAR, 0:RT * TT * 2].rearrange("p (c t h) -> p c t h", c=RT, t=TT)
    with ExitStack() as ctx:
        init, mean_mm, dot_in, dot_mm, gate_mm, dev, bonus, sq_done, var_mm = sems(
            nc, ctx, "e_init", "e_mean_mm", "e_dot_in", "e_dot_mm", "e_gate_mm", "e_dev", "e_bonus", "e_sq", "e_var_mm")
        root_done, scaled, spread, done, hi_done, lo_done, wide_done, w_out_in = sems(
            nc, ctx, "e_root", "e_scaled", "e_spread", "e_done", "e_hi", "e_lo", "e_wide", "e_w_out_in")
        block = ctx.enter_context(nc.Block())

        @block.sync
        def _(sp):
            for kt, raw in enumerate(k.wout_raw):
                sp.dma_start(raw[:], t["w_out"][kt]).then_inc(w_out_in, 16)
            sp.wait_ge(w_out_in, 16 * len(k.wout_raw))

        @block.tensor
        def _(pe):
            def product(bank, w, r):
                for b in range(2):
                    last = nc.tensor.matmul(ps[:, bank + b, :], w, r[:, b * HALF:(b + 1) * HALF], start=True, stop=True)
                return last

            def variance(c):
                pe.wait_ge(sq_done, c + 1)
                head_stats(nc, var, square[c % 2], ones_block, c).then_inc(var_mm, 1)

            for c in range(RT):
                if c:
                    pe.wait_ge(dev, c)
                product(MEAN, ones_block[:], y[:, c, :]).then_inc(mean_mm, 1)
                pe.wait_ge(dot_in, c + 1)
                if c:
                    pe.wait_ge(bonus, c)
                product(DOT, ones_block[:], dot[c]).then_inc(dot_mm, 1)
                if c:
                    variance(c - 1)
            variance(RT - 1)
            for c in range(RT):
                if c == 0:
                    pe.wait_ge(root_done, 1)
                if c >= 2:
                    pe.wait_ge(done, c - 1)
                product(GATE[c % 2], k.gate[:, c * P:(c + 1) * P], hT[:, T_G, :]).then_inc(gate_mm, 1)
                if c == 0:
                    pe.wait_ge(dev, RT)
                    pe.wait_ge(bonus, RT)
                pe.wait_ge(wide_done, c + 1)
                b = SPREAD[c % 2]
                spread_stats(nc, [ps[:, b, :], ps[:, b + 1, :]], square[c % 2], ident).then_inc(spread, 1)

        @block.scalar
        def _(act):
            act.wait_ge(init, 1)
            for c in range(RT):
                act.wait_ge(dev, c + 1)
                if c >= 2:
                    act.wait_ge(var_mm, c - 1)
                nc.scalar.activation(square[c % 2][:], y[:, c, :], ACT.Square).then_inc(sq_done, 1)
            act.wait_ge(var_mm, RT)
            nc.scalar.activation(scale[:], var, ACT.Sqrt, scale=1.0 / HD, bias=gn_eps[:]).then_inc(root_done, 1)
            act.wait_ge(scaled, 1)
            for c in range(RT + 1):
                if c < RT:
                    if c >= 2:
                        act.wait_ge(spread, c - 1)
                    out, src = widened(scale, square[c % 2], c)
                    nc.scalar.activation(out, src, ACT.Copy).then_inc(wide_done, 1)
                if c:
                    act.wait_ge(done, c)
                    nc.scalar.activation(k.yr_hi[:, c - 1, :], full[(c - 1) % 2][:], ACT.Copy).then_inc(hi_done, 1)

        @block.vector
        def _(dve):
            V = nc.vector
            step = k.dve_steps.on(dve)
            V.memset(gn_eps[:], GN_EPS).then_inc(init, 1)

            def dot_step(c):
                V.scalar_tensor_tensor(dot[c][:], hT[:, T_R + c, :], cols[:, C_RK + c:C_RK + c + 1],
                                       hT[:, T_K + c, :], ALU.mult, ALU.mult).then_inc(dot_in, 1)

            dot_step(0)
            for c in range(RT):
                dve.wait_ge(mean_mm, c + 1)
                V.scalar_tensor_tensor(y[:, c, :], flat(MEAN), -1.0 / HD, y[:, c, :], ALU.mult, ALU.add).then_inc(dev, 1)
                if c < RT - 1:
                    dot_step(c + 1)
                dve.wait_ge(dot_mm, c + 1)
                V.tensor_tensor(dot[c][:], flat(DOT), hT[:, T_V + c, :], ALU.mult).then_inc(bonus, 1)
            dve.wait_ge(root_done, 1)
            V.reciprocal(scale[:], scale[:]).then_inc(scaled, 1)
            for c in range(RT):
                dve.wait_ge(spread, c + 1)
                step.mark(V.scalar_tensor_tensor(y[:, c, :], y[:, c, :], cols[:, C_LG + c:C_LG + c + 1],
                                                 flat(SPREAD[c % 2]), ALU.mult, ALU.mult))
                step.wait()
                step.mark(V.scalar_tensor_tensor(y[:, c, :], y[:, c, :], cols[:, C_LB + c:C_LB + c + 1], dot[c][:],
                                                 ALU.add, ALU.add))
                step.wait()
                dve.wait_ge(gate_mm, c + 1)
                if c >= 2:
                    dve.wait_ge(lo_done, c - 1)
                V.tensor_tensor(full[c % 2][:], flat(GATE[c % 2]), y[:, c, :], ALU.mult).then_inc(done, 1)
            dve.wait_ge(hi_done, RT)
            step.mark(V.tensor_tensor(k.yr_lo[:, RT - 1, :], full[(RT - 1) % 2][:], k.yr_hi[:, RT - 1, :].bitcast(F32),
                                      ALU.subtract))

        @block.gpsimd
        def _(pool):
            for c in range(RT - 1):
                pool.wait_ge(hi_done, c + 1)
                nc.gpsimd.tensor_tensor(k.yr_lo[:, c, :], full[c % 2][:], k.yr_hi[:, c, :].bitcast(F32), ALU.subtract)\
                    .then_inc(lo_done, 1)


def layer_norm_stats(nc, dve, step, rows, stats, mean_var):
    a = step.mark(nc.vector.bn_stats(stats[:, 0, :], rows[:, 0:HALF]))
    step.mark(nc.vector.bn_stats(stats[:, 1, :], rows[:, HALF:D]))
    step.wait()
    return nc.vector.bn_aggr(mean_var, stats[:].rearrange("p a n -> p (a n)"))


def mix_out(nc, mem, k, t):
    ps, x1 = k.ps, k.x1
    w_hi = mem.at("wout_hi", 126, [P, KT, D], F32R)
    w_lo = mem.at("wout_lo", 158, [P, KT, D], F32R)
    w_raw, AHEAD = k.wout_raw, len(k.wout_raw)
    x_hi, x_lo, w1_raw, w1_hi, w1_lo = k.x1T_hi, k.x1T_lo, k.w1_raw, k.w1_hi, k.w1_lo
    gain = mem.at("ln1_gain", 70, [P, D])
    bias = mem.at("ln1_bias", 74, [P, D])
    stats = mem.at("ln1_stats", 2.5, [P, TT, 2, 6])
    mean_var = mem.at("ln1_mean_var", 2.875, [P, TT, 2])
    sd = mem.at("ln1_sd", 3, [P, TT])
    eps = mem.at("ln1_eps", 3.125, [P, 1])
    y = lambda kt: (k.yr_hi, k.yr_lo) if kt < RT else (k.ym_hi, k.ym_lo)
    with ExitStack() as ctx:
        x_in, rows_in, init, w_whi, w_split, mix_mm, mixed, var_done, sd_done, scaled, normed, last_normed = sems(
            nc, ctx, "f_x_in", "f_rows_in", "f_init", "f_w_hi", "f_w_split", "f_mix_mm", "f_mixed", "f_var",
            "f_sd", "f_scaled", "f_normed", "f_last_normed")
        w_in = sems(nc, ctx, *(f"f_w_in{j}" for j in range(AHEAD)))
        w1_in, w1_whi, w1_split, xT_ready, xhi_done, xlo_done = sems(
            nc, ctx, "f_w1_in", "f_w1_hi", "f_w1_split", "f_xT_ready", "f_xhi", "f_xlo")
        block = ctx.enter_context(nc.Block())

        @block.sync
        def _(sp):
            for kt in range(AHEAD, KT):
                sp.wait_ge(w_split, kt - AHEAD + 1)
                sp.dma_start(w_raw[kt % AHEAD][:], t["w_out"][kt]).then_inc(w_in[kt % AHEAD], 16)
            sp.dma_start(gain[:], t["ln"][0:1, :].to_broadcast([P, D])).then_inc(rows_in, 16)
            sp.dma_start(bias[:], t["ln"][1:2, :].to_broadcast([P, D])).then_inc(rows_in, 16)
            sp.dma_start(x1[:], t["x"].rearrange("o (t p) d -> p (o t) d", p=P)).then_inc(x_in, 16)
            for j in range(2):
                sp.dma_start(w1_raw[j][:], t["w_ffn1"][j]).then_inc(w1_in, 16)

        @block.tensor
        def _(pe):
            def products(tt, bank, kt):
                y_hi, y_lo = y(kt)
                tok = slice(tt * P, (tt + 1) * P)
                for n, (a, w) in enumerate(((y_hi, w_hi), (y_hi, w_lo), (y_lo, w_hi))):
                    for b in range(2):
                        last = nc.tensor.matmul(ps[:, bank + b, :], a[:, kt % RT, tok], w[:, kt, b * HALF:(b + 1) * HALF],
                                                start=kt == 0 and n == 0, stop=kt == KT - 1 and n == 2)
                return last

            for kt in range(KT):
                pe.wait_ge(w_split, kt + 1)
                for tt in range(4):
                    last = products(tt, 2 * tt, kt)
                    if kt == KT - 1:
                        last.then_inc(mix_mm, 1)
            def transposes(h):
                pe.wait_ge(mixed, 6 if h == 0 else TT)
                pe.wait_ge(normed, (4, TT - 1)[h])
                if h:
                    pe.wait_ge(last_normed, 1)
                for kt in range(KT):
                    n = h * KT + kt
                    if n >= 4:
                        pe.wait_ge(xlo_done, n - 3)
                    for tt in range(4):
                        last = nc.tensor.transpose(ps[:, n % 4, tt * P:(tt + 1) * P],
                                                   x1[:, 4 * h + tt, kt * P:(kt + 1) * P], k.ident[:])
                    last.then_inc(xT_ready, 1)

            for tt in range(4, TT):
                pe.wait_ge(mixed, tt - 3)
                for kt in range(KT):
                    last = products(tt, 2 * (tt - 4), kt)
                last.then_inc(mix_mm, 1)
                if tt == TT - 2:
                    transposes(0)
            transposes(1)
        @block.scalar
        def _(act):
            def high(h):
                for kt in range(KT):
                    act.wait_ge(xT_ready, h * KT + kt + 1)
                    nc.scalar.activation(x_hi[:, kt, h * HALF:(h + 1) * HALF], ps[:, (h * KT + kt) % 4, :], ACT.Copy)\
                        .then_inc(xhi_done, 1)

            act.wait_ge(init, 1)
            for tt in range(TT):
                act.wait_ge(var_done, tt + 1)
                nc.scalar.activation(sd[:, tt:tt + 1], mean_var[:, tt, 1:2], ACT.Sqrt, bias=eps[:]).then_inc(sd_done, 1)
                if tt in (TT - 2, TT - 1):
                    high(tt - (TT - 2))

        @block.vector
        def _(dve):
            V = nc.vector
            step = k.dve_steps.on(dve)
            V.memset(eps[:], LN_EPS).then_inc(init, 1)
            for kt in range(KT):
                if kt >= AHEAD:
                    dve.wait_ge(w_in[kt % AHEAD], 16 * (kt // AHEAD))
                split2(nc, dve, w_raw[kt % AHEAD][:], w_hi[:, kt, :], w_lo[:, kt, :], w_whi, kt + 1, w_split)
            dve.wait_ge(w1_in, 32)
            for j in range(2):
                split2(nc, dve, w1_raw[j][:], w1_hi[j][:], w1_lo[j][:], w1_whi, j + 1, w1_split)
            dve.wait_ge(x_in, 16)

            def low(h):
                cut = slice(h * HALF, (h + 1) * HALF)
                for kt in range(KT):
                    dve.wait_ge(xhi_done, h * KT + kt + 1)
                    V.tensor_tensor(x_lo[:, kt, cut], ps[:, (h * KT + kt) % 4, :], x_hi[:, kt, cut].bitcast(F32),
                                    ALU.subtract).then_inc(xlo_done, 1)

            def normalise(tt):
                dve.wait_ge(sd_done, tt + 1)
                step.mark(V.reciprocal(sd[:, tt:tt + 1], sd[:, tt:tt + 1]))
                step.wait()
                V.tensor_scalar(x1[:, tt, :], x1[:, tt, :], mean_var[:, tt, 0:1], sd[:, tt:tt + 1],
                                ALU.subtract, ALU.mult).then_inc(scaled, 1)

            for tt in range(TT):
                dve.wait_ge(mix_mm, tt + 1)
                bank = 2 * (tt % 4)
                V.scalar_tensor_tensor(x1[:, tt, :], x1[:, tt, :], ALPHA,
                                       ps[:, bank:bank + 2, :].rearrange("p b n -> p (b n)"), ALU.mult, ALU.add)\
                    .then_inc(mixed, 1)
                dve.wait_ge(mixed, tt + 1)
                layer_norm_stats(nc, dve, step, x1[:, tt, :], stats[:, tt, :, :], mean_var[:, tt, :]).then_inc(var_done, 1)
                if 0 < tt <= 4:
                    normalise(tt - 1)
                if 4 <= tt < TT - 1:
                    normalise(tt)
                if tt == TT - 2:
                    low(0)
            last, tt = x1[:, TT - 1, :], slice(TT - 1, TT)
            dve.wait_ge(sd_done, TT)
            step.mark(V.reciprocal(sd[:, tt], sd[:, tt]))
            dve.wait_ge(rows_in, 32)
            step.mark(V.scalar_tensor_tensor(last, last, mean_var[:, TT - 1, 0:1], gain[:], ALU.subtract, ALU.mult))
            step.wait()
            V.scalar_tensor_tensor(last, last, sd[:, tt], bias[:], ALU.mult, ALU.add).then_inc(last_normed, 1)
            low(1)

        @block.gpsimd
        def _(pool):
            G = nc.gpsimd
            step = k.pool_steps.on(pool)
            pool.wait_ge(rows_in, 32)
            for tt in range(TT - 1):
                pool.wait_ge(scaled, tt + 1)
                step.mark(G.tensor_tensor(x1[:, tt, :], x1[:, tt, :], gain[:], ALU.mult))
                step.wait()
                G.tensor_tensor(x1[:, tt, :], x1[:, tt, :], bias[:], ALU.add).then_inc(normed, 1)


def ffn(nc, mem, k, t, out):
    ps, acc, ident = k.ps, k.x1, k.ident
    GRP = 2
    GROUPS = DFF // P // GRP
    BY_DVE = (3, 6, 7)
    OUTS = 2 * TT
    x_hi, x_lo, w1_raw, w1_hi, w1_lo = k.x1T_hi, k.x1T_lo, k.w1_raw, k.w1_hi, k.w1_lo
    hid_hi = [mem.at(f"hid_hi{q}", 134 + 8 * q, [P, GRP, S], F32R) for q in range(2)]
    hid_lo = [mem.at(f"hid_lo{q}", 150 + 8 * q, [P, GRP, S], F32R) for q in range(2)]
    w2_hi = mem.at("w2_hi", 166, [P, GRP, D], F32R)
    w2_lo = mem.at("w2_lo", 174, [P, GRP, D], F32R)
    w2_last = [mem.at("w2_last_hi", 190, [P, GRP, D], F32R), mem.at("w2_last_lo", 198, [P, GRP, D], F32R)]
    w2_raw = mem.at("w2_raw", 182, [P, GRP, D])
    gain = mem.at("ln2_gain", 86, [P, D])
    bias = mem.at("ln2_bias", 90, [P, D])
    relu = [mem.at(f"relu{j}", 70 + 4 * j, [P, S]) for j in range(GRP)]
    squared = [mem.at(f"squared{j}", 126 + 4 * j, [P, S]) for j in range(GRP)]
    stats = mem.at("ln2_stats", 1, [P, TT, 2, 6])
    mean_var = mem.at("ln2_mean_var", 1.5, [P, TT, 2])
    sd = mem.at("ln2_sd", 2, [P, TT])
    eps = mem.at("ln2_eps", 2.25, [P, 1])
    flat = lambda b: ps[:, b:b + 2, :].rearrange("p b n -> p (b n)")
    with ExitStack() as ctx:
        rows_in, init, relu_done, square_done, hid_ready, out_mm, added = sems(
            nc, ctx, "g_rows_in", "g_init", "g_relu", "g_square",
            "g_hid_ready", "g_out_mm", "g_added")
        var_done, sd_done, scaled, inverted, stored, w2_in, w2_whi, w2_split = sems(
            nc, ctx, "g_var", "g_sd", "g_scaled", "g_inverted", "g_stored", "g_w2_in",
            "g_w2_hi", "g_w2_split")
        normed = sems(nc, ctx, "g_normed_pool", "g_normed_dve")
        relu_free, = sems(nc, ctx, "g_relu_free")
        w1_in = sems(nc, ctx, "g_w1_in0", "g_w1_in1")
        w1_whi = sems(nc, ctx, "g_w1_hi0", "g_w1_hi1")
        w1_split = sems(nc, ctx, "g_w1_split0", "g_w1_split1")
        slab_mm = sems(nc, ctx, "g_slab_mm0", "g_slab_mm1")
        SLAB_FREE, OUT_FREE = GRP, 4
        block = ctx.enter_context(nc.Block())
        loops = GROUPS // 2 - 1

        def count(tt, by_dve):
            return sum((u in BY_DVE) == by_dve for u in range(tt + 1))

        @block.sync
        def _(sp):
            load2 = lambda g: sp.dma_start(w2_raw[:], t["w_ffn2"][g]).then_inc(w2_in, 16)
            load2(0)
            sp.dma_start(gain[:], t["ln"][2:3, :].to_broadcast([P, D])).then_inc(rows_in, 16)
            sp.dma_start(bias[:], t["ln"][3:4, :].to_broadcast([P, D])).then_inc(rows_in, 16)
            for j in range(GRP):
                sp.sem_inc(w1_in[j], 16)
            with sp.Fori(1, GROUPS) as g:
                for j in range(GRP):
                    sp.wait_ge(w1_split[j], g)
                    sp.dma_start(w1_raw[j][:], t["w_ffn1"][GRP * g + j]).then_inc(w1_in[j], 16)
                sp.wait_ge(w2_split, g)
                load2(g)
            for tt in range(TT):
                sp.wait_ge(normed[tt in BY_DVE], count(tt, tt in BY_DVE))
                sp.dma_start(out[0, tt * P:(tt + 1) * P, :], acc[:, tt, :]).then_inc(stored, 16)
            sp.wait_ge(stored, 16 * TT)

        @block.tensor
        def _(pe):
            def first(g):
                for j in range(GRP):
                    pe.wait_ge(w1_split[j], g + 1)
                    pe.wait_ge(relu_done, GRP * (g - 1) + j + 1 + SLAB_FREE)
                    project3(nc, [ps[:, 2 * j + b, :] for b in range(2)], w1_hi[j], w1_lo[j],
                             lambda kt, b: x_hi[:, kt, b * HALF:(b + 1) * HALF],
                             lambda kt, b: x_lo[:, kt, b * HALF:(b + 1) * HALF], KT).then_inc(slab_mm[j], 1)

            def second(g, q, w2_hi=w2_hi, w2_lo=w2_lo):
                pe.wait_ge(w2_split, g + 1)
                pe.wait_ge(hid_ready, GRP * (g + 1))
                for n in range(OUTS):
                    tt, b = divmod(n, 2)
                    tok, col = slice(tt * P, (tt + 1) * P), slice(b * HALF, (b + 1) * HALF)
                    pe.wait_ge(added, OUTS * g + n - 3 + OUT_FREE)
                    for j in range(GRP):
                        for m, (a, w) in enumerate(((hid_hi, w2_hi), (hid_hi, w2_lo), (hid_lo, w2_hi))):
                            last = nc.tensor.matmul(ps[:, 4 + n % 4, :], a[q][:, j, tok], w[:, j, col],
                                                    start=j == 0 and m == 0, stop=j == GRP - 1 and m == 2)
                    last.then_inc(out_mm, 1)

            first(0)
            with pe.Fori(0, loops) as i:
                for q in range(2):
                    first(2 * i + q + 1)
                    second(2 * i + q, q)
            first(GROUPS - 1)
            second(GROUPS - 2, 0)
            second(GROUPS - 1, 1, *w2_last)

        @block.scalar
        def _(act):
            A = nc.scalar.activation
            act.sem_inc(relu_done, SLAB_FREE)
            def first(g, q):
                for j in range(GRP):
                    act.wait_ge(slab_mm[j], g + 1)
                    act.wait_ge(relu_free, GRP * (g - 1) + j + 1 + GRP)
                    A(relu[j][:], flat(2 * j), ACT.Relu).then_inc(relu_done, 1)
                    act.wait_ge(relu_done, GRP * g + j + 1 + SLAB_FREE)
                    A(hid_hi[q][:, j, :], relu[j][:], ACT.Square).then_inc(square_done, 1)

            first(0, 0)
            with act.Fori(0, loops) as i:
                for q in range(2):
                    first(2 * i + q + 1, 1 - q)
            first(GROUPS - 1, 1)

            def scale(tt):
                act.wait_ge(inverted, count(tt, False))
                A(acc[:, tt, :], acc[:, tt, :], ACT.Identity, scale=sd[:, tt:tt + 1], bias=mean_var[:, tt, 1:2])\
                    .then_inc(scaled, 1)

            act.wait_ge(init, 1)
            for tt in range(TT):
                act.wait_ge(var_done, tt + 1)
                A(sd[:, tt:tt + 1], mean_var[:, tt, 1:2], ACT.Sqrt, bias=eps[:]).then_inc(sd_done, 1)
                if tt and tt - 1 not in BY_DVE:
                    scale(tt - 1)

        @block.vector
        def _(dve):
            V = nc.vector
            step = k.dve_steps.on(dve)
            V.memset(eps[:], LN_EPS).then_inc(init, 1)

            def split1(g, j):
                dve.wait_ge(w1_in[j], 16 * (g + 1))
                split2(nc, dve, w1_raw[j][:], w1_hi[j][:], w1_lo[j][:], w1_whi[j], g + 1, w1_split[j])

            def first(g, q):
                for j in range(GRP):
                    dve.wait_ge(relu_done, GRP * g + j + 1 + SLAB_FREE)
                    V.tensor_tensor(squared[j][:], relu[j][:], relu[j][:], ALU.mult).then_inc(relu_free, 1)
                    dve.wait_ge(relu_free, GRP * g + j + 1 + GRP)
                    dve.wait_ge(square_done, GRP * g + j + 1)
                    V.tensor_tensor(hid_lo[q][:, j, :], squared[j][:], hid_hi[q][:, j, :].bitcast(F32), ALU.subtract)\
                        .then_inc(hid_ready, 1)
                    yield j

            def split_second(g, w2_hi=w2_hi, w2_lo=w2_lo):
                dve.wait_ge(w2_in, 16 * (g + 1))
                split2(nc, dve, w2_raw[:], w2_hi[:], w2_lo[:], w2_whi, g + 1, w2_split)

            def add(g, n):
                tt, b = divmod(n, 2)
                piece = acc[:, tt, b * HALF:(b + 1) * HALF]
                dve.wait_ge(out_mm, OUTS * g + n + 1)
                return V.tensor_tensor(piece, ps[:, 4 + n % 4, :], piece, ALU.add).then_inc(added, 1)

            def stage(g, q, last=False):
                for j in first(g + 1, 1 - q):
                    if not last and j == 0:
                        split1(g + 2, j)
                if last:
                    for j in range(GRP):
                        dve.wait_ge(slab_mm[j], GROUPS)
                    split_second(g + 1, *w2_last)
                for n in range(OUTS):
                    add(g, n)
                    if not last and n == OUTS // 2:
                        split1(g + 2, 1)
                if not last:
                    split_second(g + 1)

            dve.sem_inc(relu_free, GRP)
            for j in range(GRP):
                dve.sem_inc(w1_whi[j], 1)
                dve.sem_inc(w1_split[j], 1)
            step.mark(V.tensor_scalar(acc[:], acc[:], ALPHA, None, ALU.mult))
            step.wait()
            dve.sem_inc(added, OUT_FREE)
            split_second(0)
            for j in first(0, 0):
                split1(1, j)
            with dve.Fori(0, loops) as i:
                for q in range(2):
                    stage(2 * i + q, q)
            stage(GROUPS - 2, 0, True)

            def invert(tt):
                dve.wait_ge(sd_done, tt + 1)
                step.mark(V.reciprocal(sd[:, tt:tt + 1], sd[:, tt:tt + 1]))
                step.wait()
                V.scalar_tensor_tensor(mean_var[:, tt, 1:2], mean_var[:, tt, 0:1], -1.0, sd[:, tt:tt + 1],
                                       ALU.mult, ALU.mult).then_inc(inverted, 1)

            def finish(tt):
                dve.wait_ge(sd_done, tt + 1)
                step.mark(V.reciprocal(sd[:, tt:tt + 1], sd[:, tt:tt + 1]))
                dve.wait_ge(rows_in, 32)
                step.mark(V.scalar_tensor_tensor(acc[:, tt, :], acc[:, tt, :], mean_var[:, tt, 0:1], gain[:],
                                                 ALU.subtract, ALU.mult))
                step.wait()
                V.scalar_tensor_tensor(acc[:, tt, :], acc[:, tt, :], sd[:, tt:tt + 1], bias[:], ALU.mult, ALU.add)\
                    .then_inc(normed[1], 1)

            for tt in range(TT):
                for b in range(2):
                    add(GROUPS - 1, 2 * tt + b)
                dve.wait_ge(added, OUTS * (GROUPS - 1) + 2 * tt + 2 + OUT_FREE)
                layer_norm_stats(nc, dve, step, acc[:, tt, :], stats[:, tt, :, :], mean_var[:, tt, :]).then_inc(var_done, 1)
                if tt:
                    (finish if tt - 1 in BY_DVE else invert)(tt - 1)
            finish(TT - 1)

        @block.gpsimd
        def _(pool):
            G = nc.gpsimd
            step = k.pool_steps.on(pool)
            pool.wait_ge(rows_in, 32)
            for tt in (tt for tt in range(TT) if tt not in BY_DVE):
                pool.wait_ge(scaled, count(tt, False))
                step.mark(G.tensor_tensor(acc[:, tt, :], acc[:, tt, :], gain[:], ALU.mult))
                step.wait()
                G.tensor_tensor(acc[:, tt, :], acc[:, tt, :], bias[:], ALU.add).then_inc(normed[0], 1)


def build(nc, t, out, debug=None):
    mem = Memory(nc)

    class K:
        pass

    k = K()
    k.ident = mem.at("ident", 0, [P, P])
    k.cols = mem.at("cols", 0.5, [P, NCOLS])
    k.keep = mem.at("keep", 0.75, [P, SLABS])
    k.hT = mem.at("hT", 38, [P, SLABS, S])
    k.ym_hi = mem.at("ym_hi", 6, [P, RT, S], F32R)
    k.ym_lo = mem.at("ym_lo", 22, [P, RT, S], F32R)
    k.beta = mem.at("beta", 159, [P, RT, S])
    k.cum = mem.at("cum", 175, [P, RT, S])
    k.kk = mem.at("kk", 191, [P, RT, S])
    k.yr_hi = mem.at("yr_hi", 94, [P, RT, S], F32R)
    k.yr_lo = mem.at("yr_lo", 110, [P, RT, S], F32R)
    k.ones_block = mem.at("ones_block", 5, [P, P])
    k.key_norm = mem.at("key_norm", 5.5, [P, RT, TT, 2])
    k.chunk_mask = mem.at("chunk_mask", 1.5, [P, P])
    k.gate = mem.at("gate", 2, [P, RW])
    k.one = mem.at("one", 4, [P, 8])
    k.merge = mem.at("merge", 153, [P, 12, P], I32)
    k.ones = mem.at("ones_full", 1, [P, P])
    k.trig_in = mem.at("trig_in", 6, [P, S])
    k.key_rot = mem.at("key_rot", 10, [P, S])
    k.att_recip = mem.at("att_recip", 191, [P, S])
    k.att_y = mem.at("att_y", 195, [P, S])
    k.att = mem.at("att", 199, [P, S])
    k.wout_raw = [mem.at(f"wout_raw{j}", 191 + 4 * j, [P, D]) for j in range(4)]
    k.x1T_hi = mem.at("x1T_hi", 6, [P, KT, S], F32R)
    k.x1T_lo = mem.at("x1T_lo", 94, [P, KT, S], F32R)
    k.w1_raw = [mem.at(f"w1_raw{j}", 78 + 4 * j, [P, KT, P]) for j in range(2)]
    k.w1_hi = [mem.at(f"w1_hi{j}", 190 + 4 * j, [P, KT, P], F32R) for j in range(2)]
    k.w1_lo = [mem.at(f"w1_lo{j}", 198 + 4 * j, [P, KT, P], F32R) for j in range(2)]
    k.x1 = mem.at("x1", 38, [P, TT, D])
    k.d_ident, k.d_cols, k.d_ones_block = t["ident"], t["cols"], t["ones_block"]
    with ExitStack() as ctx:
        k.dve_steps, k.pool_steps = (Steps(s) for s in sems(nc, ctx, "dve_steps", "pool_steps"))
        k.ps = ctx.enter_context(nc.psum_tensor("banks", [P, 8, HALF], F32))
        project_in(nc, mem, k, t["x"], t["w_in"], t["positions"])
        mla(nc, mem, k, t)
        clear_released(nc)
        rwkv_inputs(nc, mem, k, t)
        rwkv_chunks(nc, mem, k)
        rwkv_outputs(nc, mem, k, t)
        mix_out(nc, mem, k, t)
        ffn(nc, mem, k, t, out)


def lay_out(i):
    columns = lambda a: a.reshape(-1, P).T
    swap = np.r_[ROPE // 2:ROPE, 0:ROPE // 2]

    w_in = i["w_in"][0]
    main, pe = w_in[:, :T_PE * P], w_in[:, T_PE * P:]
    last = np.concatenate([np.zeros((D, HD), np.float32), pe, pe[:, swap]], axis=1)
    w_in = np.concatenate([main, last], axis=1)
    w_in = w_in.reshape(KT, P, SLABS, P).transpose(2, 1, 0, 3)

    w_uq = i["w_uq"][0].reshape(QLT, P, NH, HD + ROPE)
    w_uq = np.concatenate([w_uq, w_uq[..., HD + swap]], axis=-1).transpose(2, 1, 0, 3)
    w_ukv = i["w_ukv"][0].reshape(KVLT, P, NH, 2 * HD).transpose(2, 1, 0, 3)

    freq = (np.float32(10000.0) ** (-np.arange(0, ROPE, 2, dtype=np.float32) / ROPE)).astype(np.float32)
    rotary = np.zeros((P, 2), np.float32)
    rotary[HD:, 0] = np.tile(freq, 4)
    rotary[HD:HD + ROPE, 1] = 1.0
    rotary[HD + ROPE:, 1] = np.repeat([-1.0, 1.0], ROPE // 2)
    cols = np.concatenate([
        columns(i["shift_mu"][0]), np.zeros((P, SLABS - T_CQ), np.float32)]
        + [columns(i[n][0].reshape(-1)) for n in ("decay_w0", "iclr_a0", "k_k", "k_a", "r_k", "lnx_g", "lnx_b",
                                                  "q_norm_g", "kv_norm_g")] + [rotary], axis=1)

    row, col = np.arange(P)[:, None], np.arange(P)[None, :]
    rc, cc = row % CH, col % CH
    same = (row // CH) == (col // CH)
    chunk_mask = np.where(col < CH, rc < cc, rc <= cc).astype(np.float32)
    merge = [(same & (rc // b % 2 == 1) & (cc // b == rc // b - 1)) for b in (1, 2, 4, 8, 16, 32)]
    merge = np.stack([m for mm in merge for m in (mm, mm.T)], axis=1).astype(np.int32)
    return {
        "x": i["x"], "positions": i["positions"], "w_in": w_in, "cols": cols,
        "ident": np.eye(P, dtype=np.float32), "ones_block": same.astype(np.float32),
        "causal": np.where(row > col, NEG, 0.0).astype(np.float32),
        "chunk_mask": chunk_mask, "merge": merge,
        "w_uq": w_uq, "w_ukv": w_ukv,
        "w_lora": np.stack([np.pad(i["decay_w2"][0], ((0, HD), (0, 0))), np.pad(i["iclr_a2"][0], ((HD, 0), (0, 0)))],
                           axis=1), "gate_g2": i["gate_g2"][0],
        "w_out": i["w_out"][0].reshape(KT, P, D),
        "w_ffn1": i["w_ffn1"][0].reshape(KT, P, DFF // P, P).transpose(2, 1, 0, 3),
        "w_ffn2": i["w_ffn2"][0].reshape(DFF // (2 * P), 2, P, D).transpose(0, 2, 1, 3),
        "ln": np.stack([i[n][0] for n in ("ln1_g", "ln1_b", "ln2_g", "ln2_b")]),
    }


def kernel(**inputs):
    import concourse.bacc as bacc
    from concourse.bass_utils import run_bass_kernel_spmd as run

    nc = bacc.Bacc("TRN2", target_bir_lowering=False, num_devices=1)
    arrays, args = {}, {}
    for name, a in lay_out({n: np.asarray(a) for n, a in inputs.items()}).items():
        arrays[f"in_{name}"] = a = np.ascontiguousarray(a)
        args[name] = nc.dram_tensor(f"in_{name}", a.shape, mybir.dt.from_np(a.dtype), kind="ExternalInput").ap()
    out = nc.dram_tensor("layer_out", OUT_SHAPE, F32, kind="ExternalOutput").ap()
    build(nc, args, out)
    return run(nc, [arrays], core_ids=[0]).results[0]["layer_out"]
```
